# Optimizing a Trainium2 kernel written in Bass

```python
import jax, jax.numpy as jnp
from jax import lax
import numpy as np

D_MODEL = 1024
BATCH = 1
SEQ = 1024
DEPTH = 2

N_A_LAYERS = DEPTH // 2
N_B_LAYERS = DEPTH - N_A_LAYERS
CHUNK = 128
GMLP_WIDTH = 2 * D_MODEL
GMLP_GROUPS = 8
N_HEADS = 16
HEAD_DIM = D_MODEL // N_HEADS
D_FF = 4 * D_MODEL
Q_BLOCK = 128
MOD_INIT = 0.5
EPS = 1e-6

kernel_name = "yoco_gmlp_stickbreaking_hybrid"

def _rmsnorm(x, g):
    xf = x.astype(jnp.float32)
    y = xf * lax.rsqrt(jnp.mean(xf * xf, axis=-1, keepdims=True) + EPS)
    return (y * g.astype(jnp.float32)).astype(x.dtype)

def _modulate(h, shift, scale):
    return h * (1 + scale[:, None, :]) + shift[:, None, :]

def _gmlp_mixer(h, w_in, v_norm_g, w_s, b_s, w_out):
    B, S, _ = h.shape
    uv = jax.nn.gelu(h @ w_in, approximate=False)
    u, v = jnp.split(uv, 2, axis=-1)
    v = _rmsnorm(v, v_norm_g)
    n_chunks = S // CHUNK
    v = v.reshape(B, n_chunks, CHUNK, GMLP_GROUPS, GMLP_WIDTH // GMLP_GROUPS)
    w_causal = jnp.tril(w_s)
    z = jnp.einsum("gts,bnsgc->bntgc", w_causal, v) + b_s.T[None, None, :, :, None]
    z = z.reshape(B, S, GMLP_WIDTH)
    return (u * z) @ w_out

def _stick_breaking(q, k, v):
    S = q.shape[2]
    scale = HEAD_DIM ** -0.5
    outs = []
    for blk in range(S // Q_BLOCK):
        t0 = blk * Q_BLOCK
        n_keys = t0 + Q_BLOCK
        qb = q[:, :, t0:n_keys]
        kb = k[:, :, :n_keys]
        vb = v[:, :, :n_keys]
        z = jnp.einsum("bhtd,bhsd->bhts", qb, kb,
                       preferred_element_type=jnp.float32) * scale
        t_pos = t0 + jnp.arange(Q_BLOCK)[:, None]
        s_pos = jnp.arange(n_keys)[None, :]
        causal = s_pos < t_pos
        log_beta = jax.nn.log_sigmoid(z)
        log_keep = jnp.where(causal, jax.nn.log_sigmoid(-z), 0.0)
        between = lax.cumsum(log_keep, axis=3, reverse=True) - log_keep
        weights = jnp.where(causal, jnp.exp(log_beta + between), 0.0)
        outs.append(jnp.einsum("bhts,bhsd->bhtd", weights.astype(vb.dtype), vb))
    return jnp.concatenate(outs, axis=2)

def setup_inputs(seed: int = 0) -> dict:
    key = jax.random.key(seed)
    ks = jax.random.split(key, 20)
    D = D_MODEL
    W = GMLP_WIDTH

    def nrm(k, shape, s):
        return jax.random.normal(k, shape, jnp.float32) * s

    return {
        "x": nrm(ks[0], (BATCH, SEQ, D), 1.0),
        "c": nrm(ks[1], (BATCH, D), 1.0),
        "mod_w": nrm(ks[2], (DEPTH, D, 6 * D), MOD_INIT * D ** -0.5),
        "mod_b": nrm(ks[3], (DEPTH, 6 * D), 0.02),
        "norm_g": 1.0 + nrm(ks[4], (DEPTH, 2, D), 0.02),
        "mlp_w_up": nrm(ks[5], (DEPTH, D, D_FF), D ** -0.5),
        "mlp_w_down": nrm(ks[6], (DEPTH, D_FF, D), D_FF ** -0.5),
        "a_w_in": nrm(ks[7], (N_A_LAYERS, D, 2 * W), D ** -0.5),
        "a_v_norm_g": 1.0 + nrm(ks[8], (N_A_LAYERS, W), 0.02),
        "a_w_spatial": nrm(ks[9], (N_A_LAYERS, GMLP_GROUPS, CHUNK, CHUNK), CHUNK ** -0.5),
        "a_b_spatial": 1.0 + nrm(ks[10], (N_A_LAYERS, GMLP_GROUPS, CHUNK), 0.02),
        "a_w_out": nrm(ks[11], (N_A_LAYERS, W, D), W ** -0.5),
        "kv_mod_w": nrm(ks[12], (D, 2 * D), MOD_INIT * D ** -0.5),
        "kv_mod_b": nrm(ks[13], (2 * D,), 0.02),
        "kv_norm_g": 1.0 + nrm(ks[14], (D,), 0.02),
        "kv_w": nrm(ks[15], (D, 2 * D), D ** -0.5),
        "k_norm_g": 1.0 + nrm(ks[16], (HEAD_DIM,), 0.02),
        "b_w_q": nrm(ks[17], (N_B_LAYERS, D, D), D ** -0.5),
        "q_norm_g": 1.0 + nrm(ks[18], (N_B_LAYERS, HEAD_DIM), 0.02),
        "b_w_out": nrm(ks[19], (N_B_LAYERS, D, D), D ** -0.5),
    }

def reference(x, c, mod_w, mod_b, norm_g, mlp_w_up, mlp_w_down, a_w_in, a_v_norm_g,
              a_w_spatial, a_b_spatial, a_w_out, kv_mod_w, kv_mod_b, kv_norm_g, kv_w,
              k_norm_g, b_w_q, q_norm_g, b_w_out):
    B, S, D = x.shape
    k_shared = None
    v_shared = None
    for layer in range(DEPTH):
        mod = c @ mod_w[layer] + mod_b[layer]
        sh1, sc1, g1, sh2, sc2, g2 = jnp.split(mod, 6, axis=-1)
        h = _modulate(_rmsnorm(x, norm_g[layer, 0]), sh1, sc1)
        if layer < N_A_LAYERS:
            i = layer
            y = _gmlp_mixer(h, a_w_in[i], a_v_norm_g[i], a_w_spatial[i],
                            a_b_spatial[i], a_w_out[i])
        else:
            j = layer - N_A_LAYERS
            q = (h @ b_w_q[j]).reshape(B, S, N_HEADS, HEAD_DIM)
            q = _rmsnorm(q, q_norm_g[j]).transpose(0, 2, 1, 3)
            o = _stick_breaking(q, k_shared, v_shared)
            y = o.transpose(0, 2, 1, 3).reshape(B, S, D) @ b_w_out[j]
        x = x + g1[:, None, :] * y
        h = _modulate(_rmsnorm(x, norm_g[layer, 1]), sh2, sc2)
        y = jnp.square(jax.nn.relu(h @ mlp_w_up[layer])) @ mlp_w_down[layer]
        x = x + g2[:, None, :] * y
        if layer == N_A_LAYERS - 1:
            kv_shift, kv_scale = jnp.split(c @ kv_mod_w + kv_mod_b, 2, axis=-1)
            hk = _modulate(_rmsnorm(x, kv_norm_g), kv_shift, kv_scale)
            k_all, v_all = jnp.split(hk @ kv_w, 2, axis=-1)
            k_shared = _rmsnorm(k_all.reshape(B, S, N_HEADS, HEAD_DIM),
                                k_norm_g).transpose(0, 2, 1, 3)
            v_shared = v_all.reshape(B, S, N_HEADS, HEAD_DIM).transpose(0, 2, 1, 3)
    return x


_drawn_inputs = setup_inputs


def setup_inputs(seed=0):
    import zlib

    import numpy as np

    out = dict(_drawn_inputs(seed))
    spreads = {}
    factors = {'norm_g': 2.775,
     'a_v_norm_g': 8.0,
     'a_b_spatial': 7.583,
     'kv_mod_b': 6.496,
     'kv_norm_g': 8.0,
     'k_norm_g': 8.0,
     'q_norm_g': 8.0}
    for name, (base, spread) in spreads.items():
        noise = np.random.default_rng([zlib.crc32(name.encode()), seed]).standard_normal(out[name].shape)
        drawn = base * np.exp(spread * noise) if base else spread * noise
        out[name] = __import__('jax').numpy.asarray(drawn.astype(out[name].dtype))
    for name, factor in factors.items():
        out[name] = (out[name] * factor).astype(out[name].dtype)
    return out
```

```python
import numpy as np
from contextlib import ExitStack

import concourse.bass as bass
from concourse import mybir

F32 = mybir.dt.float32
F32R = mybir.dt.float32r
ACT = mybir.ActivationFunctionType
ALU = mybir.AluOpType
AX = mybir.AxisListType

P = 128
D = 1024
S = 1024
KT = D // P
HALF = S // 2
W = 2 * D
GROUPS = 8
CHUNK = 128
NCHUNK = S // CHUNK
CT = W // P
FF = 4 * D
HEADS = 16
HD = D // HEADS
EPS = 1e-6
RING = 4
AHEAD = 3

T_V = 0
T_C = T_V + W // P
T_M0 = T_C + 2 * (W // P)
T_KV_V = T_M0 + 2 * (FF // P)
T_K = T_KV_V + D // P
T_Q = T_K + D // P
T_O = T_Q + D // P
T_M1 = T_O + D // P
TILES = T_M1 + 2 * (FF // P)

(SH1A, SC1A, G1A, SH2A, SC2A, G2A, SHKV, SCKV, SH1B, SC1B, G1B, SH2B, SC2B, G2B) = range(0, 14 * KT, KT)
MODS = 14 * KT
MOD_FIRST = 2 * KT
NORMS = ((SH1A, SC1A), (SH2A, SC2A), (SHKV, SCKV), (SH1B, SC1B), (SH2B, SC2B))

U_V = 0
U_SP = U_V + W // P // 2 * NCHUNK
U_C = U_SP + 2 * NCHUNK
U_M0 = U_C + 4 * 12
U_KV_V = U_M0 + 8 * 12
U_K = U_KV_V + 4 * NCHUNK
U_Q = U_K + KT
U_O = U_Q + KT
U_M1 = U_O + KT


def unit_at(t):
    if t < T_C:
        return U_V + (t + 1) // 2 * NCHUNK
    if t < T_M0:
        q, j = divmod(t - T_C, 8)
        return U_C + 12 * q + (j if j < 4 else 2 * j - 4)
    if t >= T_M1 or t < T_KV_V:
        u0, j = (U_M1, t - T_M1) if t >= T_M1 else (U_M0, t - T_M0)
        if j < 4:
            return u0 + j
        if j >= 60:
            return u0 + 88 + 2 * (j - 60)
        b, j = divmod(j - 4, 8)
        return u0 + 4 + 12 * b + (j if j < 4 else 2 * j - 4)
    if t < T_K:
        return U_KV_V + (t - T_KV_V + 1) // 2 * NCHUNK
    return U_K + t - T_K


def freed(u):
    return u - (U_SP - 1)


STRIP = [sum((KT - j) * P for j in range(b)) for b in range(KT + 1)]
GROUP = [(g, j) for g in range(2) for j in range(KT - 1, 4 * g - 1, -1)]


class Count:

    def __init__(self, c, s=0, i=None):
        self.c, self.s, self.i = c, (s if i is not None else 0), i

    def __add__(self, n):
        return Count(self.c + n, self.s, self.i)

    def __sub__(self, n):
        return self + (-n)

    def __mul__(self, n):
        return Count(self.c * n, self.s * n, self.i)

    def __floordiv__(self, n):
        assert self.s % n == 0
        return Count(self.c // n, self.s // n, self.i)

    def __mod__(self, n):
        assert self.s % n == 0
        return self.c % n

    @property
    def v(self):
        if self.i is None or self.s == 0:
            return self.c
        return self.i * self.s + self.c


def build(nc, xT, cT, wt, modw, modb, ng, vg, qkg, spw, spb, out):
    with ExitStack() as ctx:
        sem_names = """
            small_in xa_in xb_in m0_in0 m0_in1 m0_in2 m0_in3 raw_in0 raw_in1 mod_in spw_in spb_in
            z_in0 z_in1 x_back x_spilled z_out0 z_out1 vs_out0 vs_out1 kq_out qk_in0 qk_in1 v_in0 v_in1 y_out
            consts w_hi w_lo  m0_mul_pool m0_mul_dve mod_mul mod_red mod_mm mod_vec
            av_done sq_done s_added stat_full rs_sqrt rs_done t_mul hf_done h_hi h_lo
             v_gelu v_ss v_rms v_rstd ws_mask ws_hi ws_lo sp_hi sp_lo 
            acc_full acc_free uz_zb uz_gelu  uz_hi uz_lo
            relu_done hid_hi  
            vs_hi  kq_sq  kq_full kq_sqrt kq_rec kq_norm kq_hi kq_lo
            ident_ok mask_turn z_full keep_ok beta_ok masked scanned a_ok at_full at_hi at_lo  o_bot o_sum o_hi o_lo
        """.split()
        sem = {n: ctx.enter_context(nc.semaphore(n)) for n in sem_names}

        base = -(-nc.sbuf_base // 32) * 32

        def at(name, shape, dt, off):
            return nc.alloc_sbuf_tensor_at(name, shape, dt, offset=base + off)

        KB = 1024
        RX, RB, RH, RR, RW, RC = 0, 32 * KB, 96 * KB, 160 * KB, 192 * KB, 200 * KB
        X = at("X", [P, KT, S], F32, RX)
        H_HI = at("H_HI", [P, KT, S], F32R, RH)
        H_LO = at("H_LO", [P, KT, S], F32R, RH + 32 * KB)
        W_HI = at("W_HI", [P, 8, RING * P], F32R, RR)
        W_LO = at("W_LO", [P, 8, RING * P], F32R, RR + 16 * KB)
        RAW = at("RAW", [P, 2, 1024], F32, RW)
        MODRAW = at("MODRAW", [P, 8, P], F32, RC)
        co = [RC + 4 * KB]

        def small(name, cols):
            t = at(name, [P, cols], F32, co[0])
            co[0] += -(-cols * 4 // 32) * 32
            return t

        MODACC = small("MODACC", 2 * P)
        ONES = small("ONES", P)
        MODV = small("MODV", MODS)
        MODB = small("MODB", MODS)
        NG = small("NG", 5 * KT)
        GS = small("GS", 5 * KT)
        VG = small("VG", CT)
        QKG = small("QKG", 2)
        CC = small("CC", KT)
        EPSC = small("EPSC", 1)
        SS = small("SS", KT)
        RSTDV = small("RSTDV", KT)
        assert co[0] <= 212800, co[0]

        ZIN = at("ZIN", [P, 2, S], F32, RB)
        BBC = at("BBC", [P, GROUPS, CHUNK], F32, RB + 8 * KB)
        RS = at("RS", [P, S], F32, RB + 12 * KB)
        TT = at("TT", [P, 2, HALF], F32, RB + 16 * KB)
        HF = at("HF", [P, 2, HALF], F32, RB + 20 * KB)
        SUMSQ = at("SUMSQ", [P, S], F32, RB)
        SQ = at("SQ", [P, 2, S], F32, RB + 24 * KB)
        V = at("V", [P, NCHUNK, W], F32, RB)
        UZ_HI = at("UZ_HI", [P, 4, S], F32R, RB + 32 * KB)
        UZ_LO = at("UZ_LO", [P, 4, S], F32R, RB + 48 * KB)
        HID_HI = [at(f"HID_HI{e}", [P, 4, S], F32R, RB + 32 * KB * e) for e in range(2)]
        HID_LO = [at(f"HID_LO{e}", [P, 4, S], F32R, RB + 32 * KB * e + 16 * KB) for e in range(2)]
        MOD0 = at("MOD0", [P, MOD_FIRST, 8, P], F32, RH)
        WS_HI = at("WS_HI", [P, GROUPS, CHUNK], F32R, RX)
        WS_LO = at("WS_LO", [P, GROUPS, CHUNK], F32R, RX + 4 * KB)
        VC_HI = at("VC_HI", [P, 2, W // 2], F32R, RX + 8 * KB)
        VC_LO = at("VC_LO", [P, 2, W // 2], F32R, RX + 16 * KB)
        ZST = at("ZST", [P, 2, 8, CHUNK], F32, RX + 24 * KB)
        TRASH = at("TRASH", [P, W], F32, RX + 24 * KB)
        WS_RAW = at("WS_RAW", [P, GROUPS, CHUNK], F32, RX + 8 * KB)
        KSQ = at("KSQ", [P, S], F32, RB + 32 * KB)
        KRAW = at("KRAW", [P, 2, S], F32, RB + 36 * KB)
        KN = at("KN", [P, S], F32, RB + 44 * KB)
        KOUT = at("KOUT", [P, 2, S], F32R, RB + 48 * KB)
        VST = at("VST", [P, 2, 4, 2 * HD], F32R, RB + 56 * KB)
        BLK = at("BLK", [P, P], F32, RB + 60 * KB)
        QK = at("QK", [P, 4, S], F32R, RX)
        A = at("A", [P, 2, STRIP[KT]], F32, RH)
        KEEP = at("KEEP", [P, 2, S + 8], F32, RH + 36 * KB)
        VH = at("VH", [P, 2, NCHUNK, 2 * HD], F32R, RH + 36 * KB + 8256)
        AT_HI = at("AT_HI", [P, 2, HALF], F32R, RH + 36 * KB + 8256 + 8192)
        AT_LO = at("AT_LO", [P, 2, HALF], F32R, RH + 36 * KB + 8256 + 12288)
        OSUM = at("OSUM", [P, HALF], F32, RH + 36 * KB + 8256 + 16384)
        SUMSQ3 = at("SUMSQ3", [P, S], F32, RH)
        SQ3 = at("SQ3", [P, 2, S], F32, RH + 4 * KB)
        IDENT = at("IDENT", [P, P], F32, RX + 16 * KB)
        OT_HI = at("OT_HI", [P, KT, S], F32R, RB)
        OT_LO = at("OT_LO", [P, KT, S], F32R, RB + 32 * KB)

        PS = ctx.enter_context(nc.psum_tensor("PS", [P, 8, HALF], F32))
        STAT = PS[:, 4:6, :]
        MODPS = PS[:, 6, 0:MODS]

        def acc(slot):
            return PS[:, 2 * slot:2 * slot + 2, :]

        def flat(ap):
            return ap.rearrange("p a b -> p (a b)")

        ZD = nc.dram_tensor("z_scratch", [CT, P, S], F32).ap()
        XD = nc.dram_tensor("x_scratch", [P, KT, S], F32).ap()
        VD = nc.dram_tensor("v_scratch", [HEADS, NCHUNK, P, 2 * HD], F32).ap()
        QKD = nc.dram_tensor("qk_scratch", [KT, P, 4, S], F32).ap()

        def raw_view(n):
            return RAW[:, n % 2, :].rearrange("p (k c) -> p k c", k=8)

        def ring_view(t, n):
            s = n % RING
            return t[:, :, s * P:(s + 1) * P]

        def read_before(n):
            a = unit_at(n.c - RING + 1)
            return Count(a, unit_at(n.c + n.s - RING + 1) - a, n.i) if n.i is not None else Count(a)

        def load_raw(sp, n):
            if n.i is not None or n.c >= 2:
                sp.wait_ge(sem["w_lo"], (n - 1).v)
            sp.dma_start(RAW[:, n % 2, :], wt[n.v]).then_inc(sem[f"raw_in{n % 2}"], 16)

        def load_mod(sp, j):
            if j.i is not None or j.c >= 1:
                sp.wait_ge(sem["mod_red"], (j + MOD_FIRST).v)
            sp.dma_start(MODRAW[:], modw[(j + MOD_FIRST).v]).then_inc(sem["mod_in"], 16)

        def cut_hi(act, n):
            act.wait_ge(sem[f"raw_in{n % 2}"], ((n // 2) * 16 + 16).v)
            if n.i is not None or n.c >= RING:
                act.wait_ge(sem["acc_full"], read_before(n).v)
            act.activation(ring_view(W_HI, n), raw_view(n), ACT.Copy).then_inc(sem["w_hi"], 1)

        def cut_lo(dve, n):
            dve.wait_ge(sem["w_hi"], (n + 1).v)
            dve.tensor_tensor(ring_view(W_LO, n), raw_view(n), ring_view(W_HI, n).bitcast(F32),
                              ALU.subtract).then_inc(sem["w_lo"], 1)

        def mod_reduce(dve, j):
            dve.wait_ge(sem["mod_mul"], (j + 1).v)
            dve.wait_ge(sem["mod_mm"], (j + MOD_FIRST - 1).v)
            dve.tensor_reduce(MODACC[:, (j % 2) * P:(j % 2 + 1) * P], MODRAW[:].rearrange("p k c -> p c k"),
                              AX.X, ALU.add).then_inc(sem["mod_red"], 1)

        def mod_mm(pe, j):
            m = j + MOD_FIRST
            pe.wait_ge(sem["mod_red"], (m + 1).v)
            pe.matmul(PS[:, 6, bass.ds(m.v, 1)], MODACC[:, (j % 2) * P:(j % 2 + 1) * P], ONES[:, 0:1],
                      start=True, stop=True).then_inc(sem["mod_mm"], 1)

        block = ctx.enter_context(nc.Block())
        piece_of_norm = lambda r: 16 * r

        @block.sync
        def _(sp):
            for dst, src in ((CC, cT), (MODB, modb), (NG, ng), (VG, vg), (QKG, qkg)):
                sp.dma_start(dst[:], src).then_inc(sem["small_in"], 16)
            for a in range(4):
                sp.dma_start(MOD0[:, 4 * a:4 * a + 4, :, :],
                             modw[4 * a:4 * a + 4].rearrange("m p k c -> p m k c")).then_inc(sem[f"m0_in{a}"], 16)
            sp.dma_start(X[:, 0:4, :], xT[:, 0:4, :]).then_inc(sem["xa_in"], 16)
            sp.dma_start(X[:, 4:8, :], xT[:, 4:8, :]).then_inc(sem["xb_in"], 16)
            for n in range(5):
                load_raw(sp, Count(n))
            load_mod(sp, Count(0))
            sp.wait_ge(sem["h_lo"], 16)
            sp.dma_start(WS_RAW[:], spw).then_inc(sem["spw_in"], 16)

            def v_tiles(i, js):
                for j in js:
                    n = Count(T_V + j, 4, i)
                    load_raw(sp, n + 5)
                    load_mod(sp, n - T_V + 1)
            with sp.Fori(0, 4) as i:
                v_tiles(i, range(4))

            for u in range(2 * NCHUNK):
                place, half = u // 2, u % 2
                chunk = (place + 4) % NCHUNK
                sp.wait_ge(sem["acc_free"], freed(U_SP + u))
                sp.dma_start(ZD[8 * half:8 * half + 8, :, chunk * CHUNK:(chunk + 1) * CHUNK]
                             .rearrange("c p t -> p c t"), ZST[:, u % 2, :, :]).then_inc(sem[f"z_out{u % 2}"], 16)
            for b in range(2):
                sp.wait_ge(sem[f"z_out{b}"], 16 * NCHUNK)
            sp.wait_ge(sem["acc_full"], U_SP + 2 * NCHUNK)
            sp.dma_start(BBC[:].rearrange("p g t -> p (g t)"), spb).then_inc(sem["spb_in"], 16)
            sp.dma_start(X[:], xT).then_inc(sem["x_back"], 16)

            def load_z(ct):
                if ct.i is not None or ct.c >= 2:
                    sp.wait_ge(sem["uz_lo"], (ct - 1).v)
                sp.dma_start(ZIN[:, ct % 2, :], ZD[ct.v]).then_inc(sem[f"z_in{ct % 2}"], 16)

            load_z(Count(0))

            def c_tiles(i, q, last):
                for j in range(8):
                    n = Count(T_C + 8 * q + j, 8, i)
                    load_raw(sp, n + 5)
                    ct = Count(4 * q + j, 4, i)
                    if j < 4 and not (last and j == 3):
                        load_z(ct + 1)
                    load_mod(sp, n - T_V + 1)
            with sp.Fori(0, 3) as i:
                c_tiles(i, 0, False)
            c_tiles(None, 3, True)

            def m_tiles(first, stop, ld_mod, i=None, step=0, t_end=TILES):
                for t in range(first, stop):
                    n = Count(t, step, i)
                    if i is not None or t + 5 < t_end:
                        load_raw(sp, n + 5)
                    if ld_mod is not None:
                        j = n - ld_mod + 1
                        load_mod(sp, j)

            m_tiles(T_M0, T_M0 + 4, None)
            with sp.Fori(0, 2) as i:
                m_tiles(T_M0 + 4, T_M0 + 20, T_V + 4, i, 16)
            m_tiles(T_M0 + 36, T_M0 + 51, T_V + 4)
            m_tiles(T_M0 + 51, T_M0 + 64, None)

            sp.wait_ge(sem["acc_free"], freed(U_M0 + 95))
            sp.dma_start(XD[:], X[:]).then_inc(sem["x_spilled"], 16)

            for u in range(4 * NCHUNK):
                pair, chunk = divmod(u, NCHUNK)
                if chunk in (1, 7):
                    load_raw(sp, Count(T_KV_V + 2 * pair + (chunk == 7) + 5))
                sp.wait_ge(sem["acc_free"], freed(U_KV_V + u))
                sp.dma_start(VD[4 * pair:4 * pair + 4, chunk].rearrange("h p d -> p h d"),
                             VST[:, chunk % 2, :, :].bitcast(F32)).then_inc(sem[f"vs_out{chunk % 2}"], 16)

            for kind, t0, c0 in ((1, T_K, 0), (0, T_Q, KT)):
                for j in range(KT):
                    load_raw(sp, Count(t0 + j + 5))
                    sp.wait_ge(sem["kq_lo"], c0 + j + 1)
                    sp.dma_start(QKD[j, :, 2 * kind:2 * kind + 2, :], KOUT[:].bitcast(F32)).then_inc(sem["kq_out"], 16)

            sp.wait_ge(sem["kq_out"], 16 * 2 * KT)
            for b in range(2):
                sp.wait_ge(sem[f"vs_out{b}"], 16 * 2 * NCHUNK)
            sp.wait_ge(sem["x_spilled"], 16)
            sp.wait_ge(sem["t_mul"], piece_of_norm(4))

            def load_qk(h, par):
                sp.dma_start(QK[64 * par:64 * par + 64, :, :].bitcast(F32), QKD[(h // 2).v, 64 * par:64 * par + 64]
                             ).then_inc(sem[f"qk_in{par}"], 16)

            def load_v(h, par):
                sp.dma_start(VH[:, par, :, :].bitcast(F32), VD[h.v].rearrange("c p d -> p c d")).then_inc(sem[f"v_in{par}"], 16)

            for par in range(2):
                load_qk(Count(par), par)
            sp.wait_ge(sem["acc_full"], U_O)
            for par in range(2):
                load_v(Count(par), par)
            with sp.Fori(0, 7) as i:
                for par in range(2):
                    h = Count(par, 2, i)
                    sp.wait_ge(sem["z_full"], ((h + 1) * KT).v)
                    sp.dma_start(QK[64 * par:64 * par + 64, :, :].bitcast(F32), QKD[Count(1, 1, i).v, 64 * par:64 * par + 64]
                                 ).then_inc(sem[f"qk_in{par}"], 16)
                    sp.wait_ge(sem["av_done"], ((h + 1) * len(GROUP)).v)
                    load_v(h + 2, par)
            sp.wait_ge(sem["z_full"], HEADS * KT)
            sp.wait_ge(sem["at_full"], HEADS * len(GROUP))
            sp.dma_start(X[:], XD[:]).then_inc(sem["x_back"], 16)

            for t in range(T_O, T_O + 8):
                load_raw(sp, Count(t + 5))
            m_tiles(T_M1, T_M1 + 4, None)
            with sp.Fori(0, 3) as i:
                m_tiles(T_M1 + 4, T_M1 + 20, None, i, 16)
            m_tiles(T_M1 + 52, T_M1 + 64, None)
            for k in range(KT):
                sp.wait_ge(sem["acc_free"], freed(U_M1 + 88 + k))
                sp.dma_start(out[:, k, :], X[:, k, :]).then_inc(sem["y_out"], 16)
            sp.wait_ge(sem["y_out"], 16 * KT)

        @block.gpsimd
        def _(pool):
            pool.memset(ONES[:], 1.0).then_inc(sem["consts"], 1)
            pool.memset(EPSC[:], EPS).then_inc(sem["consts"], 1)
            cb = CC[:].unsqueeze(2).to_broadcast([P, 8, P])
            pool.wait_ge(sem["small_in"], 80)
            for m in range(1, MOD_FIRST, 2):
                pool.wait_ge(sem[f"m0_in{m // 4}"], 16)
                pool.tensor_tensor(MOD0[:, m], MOD0[:, m], cb, ALU.mult).then_inc(sem["m0_mul_pool"], 1)
            pool.wait_ge(sem["spw_in"], 16)
            pool.affine_select(out=WS_RAW[:], in_=WS_RAW[:], compare_op=ALU.is_ge, fill=0.0, base=0,
                               pattern=[[0, GROUPS], [-1, CHUNK]], channel_multiplier=1).then_inc(sem["ws_mask"], 1)
            with pool.Fori(0, MODS - MOD_FIRST) as i:
                j = Count(0, 1, i)
                pool.wait_ge(sem["mod_in"], ((j + 1) * 16).v)
                pool.tensor_tensor(MODRAW[:], MODRAW[:], cb, ALU.mult).then_inc(sem["mod_mul"], 1)
            pool.wait_ge(sem["acc_free"], freed(U_M0 + 95))
            pool.memset(BLK[:], 0.0).then_inc(sem["consts"], 1)
            pool.wait_ge(sem["consts"], 3)
            pool.memset(BLK[0:HD, 0:HD], 1.0).then_inc(sem["consts"], 1)
            pool.memset(BLK[HD:P, HD:P], 1.0).then_inc(sem["consts"], 1)
            pool.wait_ge(sem["x_spilled"], 16)
            pool.wait_ge(sem["t_mul"], piece_of_norm(4))
            pool.memset(IDENT[:], 0.0).then_inc(sem["ident_ok"], 1)
            pool.wait_ge(sem["acc_full"], U_O)
            pool.memset(KEEP[:, :, 0:1], 1.0).then_inc(sem["ident_ok"], 1)
            pool.wait_ge(sem["ident_ok"], 2)
            pool.affine_select(out=IDENT[:], in_=IDENT[:], compare_op=ALU.not_equal, fill=1.0, base=0,
                               pattern=[[-1, P]], channel_multiplier=1).then_inc(sem["ident_ok"], 1)

            def mask(h, par):
                for b in range(KT):
                    n = h * KT + b
                    pool.wait_ge(sem["keep_ok"], (n + 1).v)
                    pool.sem_inc(sem["mask_turn"], 1)
                    a = A[:, par, STRIP[b]:STRIP[b] + P]
                    pool.affine_select(out=a, in_=a, compare_op=ALU.is_gt, fill=0.0, base=0,
                                       pattern=[[1, P]], channel_multiplier=-1).then_inc(sem["masked"], 1)
                    k = KEEP[:, b % 2, 1:1 + P]
                    pool.affine_select(out=k, in_=k, compare_op=ALU.is_gt, fill=1.0, base=0,
                                       pattern=[[1, P]], channel_multiplier=-1).then_inc(sem["masked"], 1)
            with pool.Fori(0, HEADS // 2) as i:
                for par in range(2):
                    mask(Count(par, 2, i), par)

        @block.scalar
        def _(act):
            act.sem_inc(sem["v_gelu"], 2)
            act.wait_ge(sem["consts"], 2)

            def square_x(s, k, u, sq=SQ):
                act.wait_ge(sem["acc_free"], freed(u))
                if k >= 2:
                    act.wait_ge(sem["s_added"], 8 * s + k - 1)
                act.activation(sq[:, k % 2, :], X[:, k, :], ACT.Square).then_inc(sem["sq_done"], 1)

            def rms_root(s):
                for n in range(2):
                    act.wait_ge(sem["stat_full"], 2 * s + n + 1)
                    act.activation(STAT[:, n, :], STAT[:, n, :], ACT.Sqrt, bias=EPSC[:, 0:1], scale=1.0 / D
                                   ).then_inc(sem["rs_sqrt"], 1)

            def modulate(r):
                sh, _ = NORMS[r]
                for i in range(16):
                    n, k, b = i // 8, i % 8, 16 * r + i
                    g, s0 = GS[:, KT * r + k:KT * r + k + 1], MODV[:, sh + k:sh + k + 1]
                    act.wait_ge(sem["t_mul"], b + 1)
                    if i >= 2:
                        act.wait_ge(sem["h_lo"], b - 1)
                    act.activation(HF[:, i % 2, :], TT[:, i % 2, :], ACT.Identity, bias=s0, scale=g
                                   ).then_inc(sem["hf_done"], 1)
                    act.activation(H_HI[:, k, n * HALF:(n + 1) * HALF], TT[:, i % 2, :], ACT.Identity,
                                   bias=s0, scale=g).then_inc(sem["h_hi"], 1)

            for k in range(KT):
                act.wait_ge(sem["xa_in" if k < 4 else "xb_in"], 16)
                if k >= 2:
                    act.wait_ge(sem["s_added"], k - 1)
                act.activation(SQ[:, k % 2, :], X[:, k, :], ACT.Square).then_inc(sem["sq_done"], 1)
            for n in range(AHEAD):
                cut_hi(act, Count(n))
            rms_root(0)
            act.wait_ge(sem["mod_vec"], 2)
            modulate(0)

            def v_pair(i, j, last):
                n = Count(T_V + 2 * j, 4, i)
                cut_hi(act, n + AHEAD)
                for chunk in range(NCHUNK):
                    u = Count(8 * j + chunk, 16, i)
                    act.wait_ge(sem["acc_full"], (u + U_V + 1).v)
                    if chunk == 4:
                        act.wait_ge(sem["h_lo"], 16)
                    act.activation(V[:, (chunk + 4) % 8, bass.ds((n * P).v, 2 * P)], acc(u % 2)[:, 0, 0:2 * P],
                                   ACT.Gelu).then_inc(sem["v_gelu"], 1)
                cut_hi(act, n + AHEAD + 1)
            with act.Fori(0, 4) as i:
                for j in range(2):
                    v_pair(i, j, False)

            act.wait_ge(sem["ws_mask"], 1)
            act.activation(WS_HI[:], WS_RAW[:], ACT.Copy).then_inc(sem["ws_hi"], 1)

            act.wait_ge(sem["v_ss"], NCHUNK)
            act.activation(RSTDV[:], SS[:], ACT.Sqrt, bias=EPSC[:, 0:1], scale=1.0 / W).then_inc(sem["v_rms"], 1)

            act.wait_ge(sem["v_rstd"], 1)
            act.wait_ge(sem["ws_lo"], 1)
            for u in range(2 * NCHUNK):
                place, half = u // 2, u % 2
                if u >= 2:
                    act.wait_ge(sem["acc_full"], U_SP + u - 1)
                act.activation(VC_HI[:, u % 2, :], V[:, place, half * 1024:(half + 1) * 1024], ACT.Copy,
                               scale=RSTDV[:, (place + 4) % 8:(place + 4) % 8 + 1]).then_inc(sem["sp_hi"], 1)

            def c_tiles(i, q):
                for j in range(8):
                    n = Count(T_C + 8 * q + j, 8, i)
                    cut_hi(act, n + AHEAD)
                    if i is None and j > 4:
                        for k in (2 * j - 10, 2 * j - 9):
                            square_x(1, k, U_C + 40 + k)
                    if j < 4:
                        ct, u = Count(4 * q + j, 4, i), Count(U_C + 12 * q + j, 12, i)
                        act.wait_ge(sem["acc_full"], (u + 1).v)
                        act.activation(acc(u % 2), acc(u % 2), ACT.Gelu).then_inc(sem["uz_gelu"], 1)
                        act.wait_ge(sem["acc_free"], freed(u).v)
                        act.activation(UZ_HI[:, j, :], ZIN[:, ct % 2, :], ACT.Copy).then_inc(sem["uz_hi"], 1)
            with act.Fori(0, 3) as i:
                c_tiles(i, 0)
            c_tiles(None, 3)
            for k in (KT - 2, KT - 1):
                square_x(1, k, U_C + 40 + k)
            rms_root(1)
            act.wait_ge(sem["mod_vec"], 6)
            modulate(1)

            def up(n, hx, u, e, cut):
                for j in range(4):
                    if cut:
                        cut_hi(act, n + j + AHEAD)
                    act.wait_ge(sem["relu_done"], (hx + j + 1).v)
                    p = acc((u + j) % 2)
                    act.activation(HID_HI[e][:, j, :], flat(p), ACT.Square).then_inc(sem["hid_hi"], 1)
                    act.activation(p, p, ACT.Square).then_inc(sem["hid_hi"], 1)

            def down(n, stat=None, u=0):
                for j in range(4):
                    if n.i is not None or n.c + j + AHEAD < TILES:
                        cut_hi(act, n + j + AHEAD)
                    if stat is not None and j:
                        square_x(stat, 2 * j - 2, u + 2 * j - 2)
                        square_x(stat, 2 * j - 1, u + 2 * j - 1)

            def mlp(t0, h0, u0, stat):
                up(Count(t0), Count(h0), Count(u0), 0, True)
                with act.Fori(0, 3) as i:
                    for a in range(2):
                        up(Count(t0 + 4 + 8 * a, 16, i), Count(h0 + 4 + 4 * a, 8, i),
                           Count(u0 + 4 + 12 * a, 24, i), (a + 1) % 2, True)
                        down(Count(t0 + 8 + 8 * a, 16, i))
                up(Count(t0 + 52), Count(h0 + 28), Count(u0 + 76), 1, True)
                down(Count(t0 + 56))
                down(Count(t0 + 60), stat, u0 + 88)

            mlp(T_M0, 0, U_M0, 2)
            for k in (KT - 2, KT - 1):
                square_x(2, k, U_M0 + 88 + k)
            rms_root(2)
            act.wait_ge(sem["mod_vec"], 6)
            modulate(2)

            for u in range(4 * NCHUNK):
                pair, chunk = divmod(u, NCHUNK)
                if chunk == 0:
                    cut_hi(act, Count(T_KV_V + 2 * pair + AHEAD))
                act.wait_ge(sem["acc_full"], U_KV_V + u + 1)
                if u >= 2:
                    act.wait_ge(sem[f"vs_out{u % 2}"], 16 * (u // 2))
                src = acc(u % 2)[:, 0, 0:2 * P].rearrange("p (h d) -> p h d", h=4)
                act.activation(VST[:, u % 2, :, 0:HD], src, ACT.Copy).then_inc(sem["vs_hi"], 1)
                if chunk == NCHUNK - 1:
                    cut_hi(act, Count(T_KV_V + 2 * pair + AHEAD + 1))

            def kq_square(c, u):
                act.wait_ge(sem["acc_full"], u + 1)
                if c:
                    act.wait_ge(sem["kq_full"], 2 * c)
                act.activation(KSQ[:], flat(acc(u % 2)), ACT.Square).then_inc(sem["kq_sq"], 1)

            def kq_rest(c):
                act.wait_ge(sem["kq_full"], 2 * c + 2)
                act.activation(STAT, STAT, ACT.Sqrt, bias=EPSC[:, 0:1], scale=1.0 / HD).then_inc(sem["kq_sqrt"], 1)
                act.wait_ge(sem["kq_norm"], c + 1)
                if c:
                    act.wait_ge(sem["kq_out"], 16 * c)
                act.activation(KOUT[:, 0, :], KN[:], ACT.Copy).then_inc(sem["kq_hi"], 1)

            def kq(c0, t0, u0):
                for j in range(KT):
                    if j:
                        kq_square(c0 + j - 1, u0 + j - 1)
                    cut_hi(act, Count(t0 + j + AHEAD))
                    if j:
                        kq_rest(c0 + j - 1)
                kq_square(c0 + KT - 1, u0 + KT - 1)
                kq_rest(c0 + KT - 1)

            kq(0, T_K, U_K)
            act.wait_ge(sem["mod_vec"], 9)
            act.wait_ge(sem["acc_full"], U_K + KT)
            modulate(3)
            kq(KT, T_Q, U_Q)

            def sig(h, par, b, first):
                n = h * KT + b
                w = (KT - b) * P
                z = flat(PS[:, 2 * (b % 2):2 * (b % 2) + 2, :])[:, 0:w]
                act.wait_ge(sem["z_full"], (n + 1).v)
                if not first:
                    act.wait_ge(sem["at_full"], ((h - 1) * len(GROUP)).v)
                act.activation(A[:, par, STRIP[b]:STRIP[b] + w], z, ACT.Sigmoid, scale=HD ** -0.5
                               ).then_inc(sem["beta_ok"], 1)
                if not (first and par == 0 and b < 2):
                    act.wait_ge(sem["a_ok"], (n - 1).v)
                act.activation(KEEP[:, b % 2, 1:1 + w], z, ACT.Sigmoid, scale=-HD ** -0.5
                               ).then_inc(sem["keep_ok"], 1)

            def at_cut(h, s, first):
                g, j = GROUP[s]
                n = h * len(GROUP) + s
                w = min(j - 4 * g + 1, 4) * P
                act.wait_ge(sem["at_full"], (n + 1).v)
                if not (first and s < 2):
                    act.wait_ge(sem["av_done"], (n - 1).v)
                act.activation(AT_HI[:, s % 2, 0:w], PS[:, 4 + s % 2, 0:w], ACT.Copy).then_inc(sem["at_hi"], 1)

            def o_copy(h, par, g, first):
                n = h * 2 + g
                act.wait_ge(sem["av_done"], (h * len(GROUP) + (8, 12)[g]).v)
                if not (first and g == 0):
                    act.wait_ge(sem["o_lo"], n.v)
                act.activation(OSUM[0:HD, :], PS[HD:P, 6 + g, :], ACT.Copy).then_inc(sem["o_bot"], 1)

            def o_cut(h, par, g, pair):
                n = h * 2 + g
                r = slice(HD * par, HD * par + HD)
                act.wait_ge(sem["o_sum"], (n + 1).v)
                act.activation(OT_HI[r, bass.ds(pair.v, 1), g * HALF:(g + 1) * HALF],
                               OSUM[r, :].unsqueeze(1), ACT.Copy).then_inc(sem["o_hi"], 1)

            def both(h1, p1, h2, p2, pair2, first1, first2):
                for s in range(len(GROUP)):
                    if h2 is not None:
                        at_cut(h2, s, first2)
                        if s == 9:
                            o_copy(h2, p2, 0, first2)
                    if h1 is not None and s < KT:
                        sig(h1, p1, s, first1)
                    if h2 is not None and s == 10:
                        o_cut(h2, p2, 0, pair2)
                if h2 is not None:
                    o_copy(h2, p2, 1, first2)
                    o_cut(h2, p2, 1, pair2)

            act.wait_ge(sem["acc_full"], U_O)
            both(Count(0), 0, None, 0, None, True, False)
            both(Count(1), 1, Count(0), 0, Count(0), True, True)
            with act.Fori(0, 7) as i:
                both(Count(2, 2, i), 0, Count(1, 2, i), 1, Count(0, 1, i), False, False)
                both(Count(3, 2, i), 1, Count(2, 2, i), 0, Count(1, 1, i), False, False)
            both(None, 0, Count(HEADS - 1), 1, Count(KT - 1), False, False)

            for j in range(KT):
                cut_hi(act, Count(T_O + j + AHEAD))
                if j:
                    square_x(3, j - 1, U_O + j - 1, SQ3)
            square_x(3, KT - 1, U_O + KT - 1, SQ3)
            rms_root(3)
            modulate(4)
            mlp(T_M1, 32, U_M1, None)

        @block.vector
        def _(dve):
            cb = CC[:].unsqueeze(2).to_broadcast([P, 8, P])
            dve.wait_ge(sem["small_in"], 80)
            for m in range(MOD_FIRST):
                if m % 2 == 0:
                    dve.wait_ge(sem[f"m0_in{m // 4}"], 16)
                    dve.tensor_tensor(MOD0[:, m], MOD0[:, m], cb, ALU.mult).then_inc(sem["m0_mul_dve"], 1)
                    dve.wait_ge(sem["m0_mul_dve"], m // 2 + 1)
                else:
                    dve.wait_ge(sem["m0_mul_pool"], m // 2 + 1)
                if m >= 2:
                    dve.wait_ge(sem["mod_mm"], m - 1)
                dve.tensor_reduce(MODACC[:, (m % 2) * P:(m % 2 + 1) * P], MOD0[:, m].rearrange("p k c -> p c k"),
                                  AX.X, ALU.add).then_inc(sem["mod_red"], 1)

            vec = [0]

            def mod_vectors(a, b, norms, made):
                dve.wait_ge(sem["mod_mm"], made)
                dve.tensor_tensor(MODV[:, a:b], MODPS[:, a:b], MODB[:, a:b], ALU.add).then_inc(sem["mod_vec"], 1)
                vec[0] += 1
                dve.wait_ge(sem["mod_vec"], vec[0])
                for r in norms:
                    sc = NORMS[r][1]
                    dve.scalar_tensor_tensor(GS[:, KT * r:KT * r + KT], MODV[:, sc:sc + KT], 1.0,
                                             NG[:, KT * r:KT * r + KT], ALU.add, ALU.mult
                                             ).then_inc(sem["mod_vec"], 1)
                    vec[0] += 1

            def sum_squares(s, k):
                dve.wait_ge(sem["sq_done"], 8 * s + k + 1)
                total, sq = (SUMSQ3, SQ3) if s == 3 else (SUMSQ, SQ)
                if k == 0:
                    dve.tensor_copy(total[:], sq[:, 0, :]).then_inc(sem["s_added"], 1)
                else:
                    dve.wait_ge(sem["s_added"], 8 * s + k)
                    dve.tensor_tensor(total[:], total[:], sq[:, k % 2, :], ALU.add).then_inc(sem["s_added"], 1)

            def reciprocals(s):
                for n in range(2):
                    dve.wait_ge(sem["rs_sqrt"], 2 * s + n + 1)
                    dve.reciprocal(RS[:, n * HALF:(n + 1) * HALF], STAT[:, n, :]).then_inc(sem["rs_done"], 1)

            def normalise(r, s):
                def mul(i):
                    n, k = i // 8, i % 8
                    b = 16 * r + i
                    if i % 8 == 0:
                        dve.wait_ge(sem["rs_done"], 2 * s + n + 1)
                    if i >= 2:
                        dve.wait_ge(sem["h_hi"], b - 1)
                    sl = slice(n * HALF, (n + 1) * HALF)
                    dve.tensor_tensor(TT[:, i % 2, :], X[:, k, sl], RS[:, sl], ALU.mult).then_inc(sem["t_mul"], 1)

                mul(0)
                for i in range(16):
                    n, k = i // 8, i % 8
                    if i + 1 < 16:
                        mul(i + 1)
                    dve.wait_ge(sem["h_hi"], 16 * r + i + 1)
                    sl = slice(n * HALF, (n + 1) * HALF)
                    dve.tensor_tensor(H_LO[:, k, sl], HF[:, i % 2, :], H_HI[:, k, sl].bitcast(F32),
                                      ALU.subtract).then_inc(sem["h_lo"], 1)

            mod_vectors(0, MOD_FIRST, (0,), MOD_FIRST)
            for k in range(KT):
                sum_squares(0, k)
            for n in range(AHEAD):
                cut_lo(dve, Count(n))
            reciprocals(0)
            normalise(0, 0)

            def v_pair(i, j, stats):
                n = Count(T_V + 2 * j, 4, i)
                cut_lo(dve, n + AHEAD)
                mod_reduce(dve, n - T_V)
                if not stats:
                    mod_reduce(dve, n - T_V + 1)
                else:
                    for chunk in range(NCHUNK):
                        u = 56 + chunk
                        dve.wait_ge(sem["v_gelu"], u + 3)
                        if chunk:
                            dve.wait_ge(sem["v_ss"], chunk)
                        dve.tensor_tensor_reduce(TRASH[:], V[:, (chunk + 4) % 8, :], V[:, (chunk + 4) % 8, :], 1.0, 0.0,
                                                 ALU.mult, ALU.add, SS[:, chunk:chunk + 1]).then_inc(sem["v_ss"], 1)
                        if chunk == 3:
                            mod_reduce(dve, n - T_V + 1)
                cut_lo(dve, n + AHEAD + 1)
            with dve.Fori(0, 3) as i:
                for j in range(2):
                    v_pair(i, j, False)
            v_pair(None, 6, False)
            v_pair(None, 7, True)
            dve.wait_ge(sem["ws_hi"], 1)
            dve.tensor_tensor(WS_LO[:], WS_RAW[:], WS_HI[:].bitcast(F32), ALU.subtract).then_inc(sem["ws_lo"], 1)
            mod_vectors(MOD_FIRST, MOD_FIRST + 8, (), MOD_FIRST + T_C)
            dve.wait_ge(sem["v_rms"], 1)
            dve.reciprocal(RSTDV[:], RSTDV[:]).then_inc(sem["v_rstd"], 1)
            dve.wait_ge(sem["v_rstd"], 1)

            def sp_cut(u):
                place, half = u // 2, u % 2
                dve.wait_ge(sem["sp_hi"], u + 1)
                dve.scalar_tensor_tensor(VC_LO[:, u % 2, :], V[:, place, half * 1024:(half + 1) * 1024],
                                         RSTDV[:, (place + 4) % 8:(place + 4) % 8 + 1],
                                         VC_HI[:, u % 2, :].bitcast(F32), ALU.mult, ALU.subtract
                                         ).then_inc(sem["sp_lo"], 1)

            sp_cut(0)
            for u in range(2 * NCHUNK):
                if u + 1 < 2 * NCHUNK:
                    sp_cut(u + 1)
                dve.wait_ge(sem["acc_full"], U_SP + u + 1)
                if u >= 2:
                    dve.wait_ge(sem[f"z_out{u % 2}"], 16 * (u // 2))
                dve.tensor_copy(ZST[:, u % 2, :, :].rearrange("p c t -> p (c t)"), flat(acc(u % 2))
                                ).then_inc(sem["acc_free"], 1)

            def add_x(u, k, gate):
                dve.wait_ge(sem["acc_full"], (u + 1).v)
                dve.wait_ge(sem["acc_free"], freed(u - 1).v)
                dve.scalar_tensor_tensor(X[:, k, :], flat(acc(u % 2)), MODV[:, gate + k:gate + k + 1], X[:, k, :],
                                         ALU.mult, ALU.add).then_inc(sem["acc_free"], 1)

            def c_tiles(i, q, last):
                for j in range(8):
                    n = Count(T_C + 8 * q + j, 8, i)
                    if j < 4:
                        ct, u = Count(4 * q + j, 4, i), Count(U_C + 12 * q + j, 12, i)
                        zin = ZIN[:, ct % 2, :]
                        dve.wait_ge(sem[f"z_in{ct % 2}"], ((ct // 2) * 16 + 16).v)
                        if i is None:
                            vgc = VG[:, 4 * q + j:4 * q + j + 1]
                            bb = BBC[:, (4 * q + j) // 2:(4 * q + j) // 2 + 1, :]
                        else:
                            vgc = VG[:, bass.ds(ct.v, 1)]
                            bb = BBC[:, bass.ds(Count(j // 2, 2, i).v, 1), :]
                        zc = zin.rearrange("p (c t) -> p c t", c=NCHUNK)
                        dve.scalar_tensor_tensor(zc, zc, vgc, bb.to_broadcast([P, NCHUNK, CHUNK]),
                                                 ALU.mult, ALU.add).then_inc(sem["uz_zb"], 1)
                        cut_lo(dve, n + AHEAD)
                        dve.wait_ge(sem["uz_gelu"], (ct + 1).v)
                        dve.wait_ge(sem["uz_zb"], (ct + 1).v)
                        dve.tensor_tensor(zin, flat(acc(u % 2)), zin, ALU.mult).then_inc(sem["acc_free"], 1)
                        mod_reduce(dve, n - T_V)
                        dve.wait_ge(sem["uz_hi"], (ct + 1).v)
                        dve.tensor_tensor(UZ_LO[:, j, :], zin, UZ_HI[:, j, :].bitcast(F32),
                                          ALU.subtract).then_inc(sem["uz_lo"], 1)
                    else:
                        cut_lo(dve, n + AHEAD)
                        for m in range(2):
                            k = 2 * (j - 4) + m
                            add_x(Count(U_C + 12 * q + 4 + k, 12, i), k, G1A)
                            if m == 0:
                                mod_reduce(dve, n - T_V)
                            if last:
                                sum_squares_late(1, k)

            pending = []

            def sum_squares_late(s, k):
                pending.append((s, k))
                if len(pending) > 1:
                    sum_squares(*pending.pop(0))

            dve.wait_ge(sem["spb_in"], 16)
            dve.wait_ge(sem["x_back"], 16)
            with dve.Fori(0, 3) as i:
                c_tiles(i, 0, False)
            c_tiles(None, 3, True)
            sum_squares(*pending.pop(0))
            mod_vectors(MOD_FIRST + 8, MOD_FIRST + 48, (1, 2), MOD_FIRST + T_M0)
            reciprocals(1)
            normalise(1, 1)

            def up(n, hx, u, e, jm):
                for j in range(4):
                    p = acc((u + j) % 2)
                    dve.wait_ge(sem["acc_full"], (u + j + 1).v)
                    dve.tensor_scalar(p, p, 0.0, None, ALU.max).then_inc(sem["relu_done"], 1)
                    cut_lo(dve, n + j + AHEAD)
                    if jm is not None:
                        mod_reduce(dve, jm + j)
                    dve.wait_ge(sem["hid_hi"], ((hx + j) * 2 + 2).v)
                    dve.tensor_tensor(HID_LO[e][:, j, :], flat(p), HID_HI[e][:, j, :].bitcast(F32), ALU.subtract
                                      ).then_inc(sem["acc_free"], 1)

            def down(n, u, gate, jm, stat):
                for j in range(4):
                    if n.i is not None or n.c + j + AHEAD < TILES:
                        cut_lo(dve, n + j + AHEAD)
                    if jm is not None:
                        mod_reduce(dve, jm + j)
                    for m in range(2):
                        k = 2 * j + m
                        add_x(u + k, k, gate)
                        if stat is not None:
                            sum_squares_late(stat, k)

            def mlp(t0, h0, u0, gate, mods, stat):
                up(Count(t0), Count(h0), Count(u0), 0, None)
                with dve.Fori(0, 3) as i:
                    for a in range(2):
                        jm = Count(mods + 8 * a, 16, i) if mods is not None else None
                        up(Count(t0 + 4 + 8 * a, 16, i), Count(h0 + 4 + 4 * a, 8, i),
                           Count(u0 + 4 + 12 * a, 24, i), (a + 1) % 2, jm)
                        down(Count(t0 + 8 + 8 * a, 16, i), Count(u0 + 8 + 12 * a, 24, i),
                             gate, jm + 4 if jm is not None else None, None)
                up(Count(t0 + 52), Count(h0 + 28), Count(u0 + 76), 1, None)
                down(Count(t0 + 56), Count(u0 + 80), gate, None, None)
                down(Count(t0 + 60), Count(u0 + 88), gate, None, stat)
                if stat is not None:
                    sum_squares(*pending.pop(0))

            mlp(T_M0, 0, U_M0, G2A, 48, 2)
            mod_vectors(MOD_FIRST + 48, MODS, (3, 4), MODS)
            reciprocals(2)
            normalise(2, 2)

            for u in range(4 * NCHUNK):
                pair, chunk = divmod(u, NCHUNK)
                if chunk == 0:
                    cut_lo(dve, Count(T_KV_V + 2 * pair + AHEAD))
                src = acc(u % 2)[:, 0, 0:2 * P].rearrange("p (h d) -> p h d", h=4)
                dve.wait_ge(sem["vs_hi"], u + 1)
                dve.tensor_tensor(VST[:, u % 2, :, HD:2 * HD], src, VST[:, u % 2, :, 0:HD].bitcast(F32),
                                  ALU.subtract).then_inc(sem["acc_free"], 1)
                if chunk == NCHUNK - 1:
                    cut_lo(dve, Count(T_KV_V + 2 * pair + AHEAD + 1))

            def kq_copy(c, u):
                dve.wait_ge(sem["acc_full"], u + 1)
                dve.wait_ge(sem["kq_sq"], c + 1)
                dve.tensor_copy(KRAW[:, c % 2, :], flat(acc(u % 2))).then_inc(sem["acc_free"], 1)

            def kq_rest(c, u):
                dve.wait_ge(sem["kq_sqrt"], c + 1)
                if c:
                    dve.wait_ge(sem["kq_lo"], c)
                dve.reciprocal(KN[:], flat(STAT)).then_inc(sem["kq_rec"], 1)
                dve.wait_ge(sem["kq_rec"], c + 1)
                dve.wait_ge(sem["acc_free"], freed(u))
                g = QKG[:, 0:1] if c < KT else QKG[:, 1:2]
                dve.scalar_tensor_tensor(KN[:], KRAW[:, c % 2, :], g, KN[:], ALU.mult, ALU.mult
                                         ).then_inc(sem["kq_norm"], 1)
                dve.wait_ge(sem["kq_hi"], c + 1)
                dve.tensor_tensor(KOUT[:, 1, :], KN[:], KOUT[:, 0, :].bitcast(F32), ALU.subtract
                                  ).then_inc(sem["kq_lo"], 1)

            def kq(c0, t0, u0):
                for j in range(KT):
                    if j:
                        kq_copy(c0 + j - 1, u0 + j - 1)
                    cut_lo(dve, Count(t0 + j + AHEAD))
                    if j:
                        kq_rest(c0 + j - 1, u0 + j - 1)
                kq_copy(c0 + KT - 1, u0 + KT - 1)
                kq_rest(c0 + KT - 1, u0 + KT - 1)

            kq(0, T_K, U_K)
            normalise(3, 2)
            kq(KT, T_Q, U_Q)

            def stick(h, par, b):
                n = h * KT + b
                w = (KT - b) * P
                dve.wait_ge(sem["masked"], (n * 2 + 2).v)
                k = KEEP[:, b % 2, 1:1 + w]
                dve.tensor_tensor_scan(k, k, k, 1.0, ALU.mult, ALU.min).then_inc(sem["scanned"], 1)
                dve.wait_ge(sem["scanned"], (n + 1).v)
                a = A[:, par, STRIP[b]:STRIP[b] + w]
                dve.tensor_tensor(a, a, KEEP[:, b % 2, 0:w], ALU.mult).then_inc(sem["a_ok"], 1)

            def at_cut(h, s):
                g, j = GROUP[s]
                n = h * len(GROUP) + s
                w = min(j - 4 * g + 1, 4) * P
                dve.wait_ge(sem["at_hi"], (n + 1).v)
                dve.tensor_tensor(AT_LO[:, s % 2, 0:w], PS[:, 4 + s % 2, 0:w], AT_HI[:, s % 2, 0:w].bitcast(F32),
                                  ALU.subtract).then_inc(sem["at_lo"], 1)

            def o_add(h, par, g):
                n = h * 2 + g
                r = slice(HD * par, HD * par + HD)
                dve.wait_ge(sem["o_bot"], (n + 1).v)
                dve.tensor_tensor(OSUM[r, :], PS[0:HD, 6 + g, :], OSUM[0:HD, :], ALU.add).then_inc(sem["o_sum"], 1)

            def o_cut(h, par, g, pair):
                n = h * 2 + g
                r = slice(HD * par, HD * par + HD)
                dve.wait_ge(sem["o_hi"], (n + 1).v)
                o = (r, bass.ds(pair.v, 1), slice(g * HALF, (g + 1) * HALF))
                dve.tensor_tensor(OT_LO[o], OSUM[r, :].unsqueeze(1), OT_HI[o].bitcast(F32), ALU.subtract
                                  ).then_inc(sem["o_lo"], 1)

            def both(h1, p1, h2, p2, pair2):
                for s in range(len(GROUP)):
                    if h2 is not None:
                        at_cut(h2, s)
                        if s == 9:
                            o_add(h2, p2, 0)
                    if h1 is not None and s < KT:
                        stick(h1, p1, s)
                    if h2 is not None and s == 10:
                        o_cut(h2, p2, 0, pair2)
                if h2 is not None:
                    o_add(h2, p2, 1)
                    o_cut(h2, p2, 1, pair2)

            both(Count(0), 0, None, 0, None)
            both(Count(1), 1, Count(0), 0, Count(0))
            with dve.Fori(0, 7) as i:
                both(Count(2, 2, i), 0, Count(1, 2, i), 1, Count(0, 1, i))
                both(Count(3, 2, i), 1, Count(2, 2, i), 0, Count(1, 1, i))
            both(None, 0, Count(HEADS - 1), 1, Count(KT - 1))

            dve.wait_ge(sem["x_back"], 32)
            for j in range(8):
                cut_lo(dve, Count(T_O + j + AHEAD))
                add_x(Count(U_O + j), j, G1B)
                sum_squares_late(3, j)
            sum_squares(*pending.pop(0))
            reciprocals(3)
            normalise(4, 3)
            mlp(T_M1, 32, U_M1, G2B, None, None)

        @block.tensor
        def _(pe):
            def three(dst, w_hi, w_lo, m_hi, m_lo, first, last):
                pe.matmul(dst, w_hi, m_hi, start=first, stop=False)
                pe.matmul(dst, w_hi, m_lo, start=False, stop=False)
                return pe.matmul(dst, w_lo, m_hi, start=False, stop=last)

            def ones_sum(s):
                pe.wait_ge(sem["s_added"], 8 * s + 8)
                total = SUMSQ3 if s == 3 else SUMSQ
                for n in range(2):
                    pe.matmul(STAT[:, n, :], ONES[:], total[:, n * HALF:(n + 1) * HALF], start=True, stop=True
                              ).then_inc(sem["stat_full"], 1)

            def wide_unit(n, u, m_hi, m_lo, piece=None, between=None):
                s, slot = n % RING, u % 2
                pe.wait_ge(sem["w_lo"], (n + 1).v)
                pe.wait_ge(sem["acc_free"], freed(u - 2).v)
                for half in range(2):
                    sl = slice(half * HALF, (half + 1) * HALF)
                    for k in range(8):
                        if piece is not None:
                            pe.wait_ge(sem["h_lo"], piece + 8 * half + k + 1)
                        mm = three(PS[:, 2 * slot + half, :], W_HI[:, k, s * P:(s + 1) * P],
                                   W_LO[:, k, s * P:(s + 1) * P], m_hi[:, k, sl], m_lo[:, k, sl], k == 0, k == 7)
                    if half == 0 and between is not None:
                        between()
                mm.then_inc(sem["acc_full"], 1)

            def narrow_units(n, u, m_hi, m_lo, ready=None):
                s = n % RING
                pe.wait_ge(sem["w_lo"], (n + 1).v)
                for m in range(2):
                    slot = (u + m) % 2
                    pe.wait_ge(sem["acc_free"], freed(u + m - 2).v)
                    for half in range(2):
                        sl = slice(half * HALF, (half + 1) * HALF)
                        for k in range(4):
                            if ready is not None and m == 0 and half == 0:
                                ready(k)
                            mm = three(PS[:, 2 * slot + half, :], W_HI[:, 2 * k + m, s * P:(s + 1) * P],
                                       W_LO[:, 2 * k + m, s * P:(s + 1) * P], m_hi[:, k, sl], m_lo[:, k, sl],
                                       k == 0, k == 3)
                    mm.then_inc(sem["acc_full"], 1)

            def token_unit(n, chunk, slot, piece=None):
                s, sl, dst = n % RING, slice(chunk * CHUNK, (chunk + 1) * CHUNK), PS[:, 2 * slot, 0:2 * P]
                for k in range(8):
                    if piece is not None:
                        pe.wait_ge(sem["h_lo"], piece + 8 * (chunk // 4) + k + 1)
                    hi, lo = W_HI[:, k, s * P:(s + 2) * P], W_LO[:, k, s * P:(s + 2) * P]
                    pe.matmul(dst, H_HI[:, k, sl], hi, start=(k == 0), stop=False)
                    pe.matmul(dst, H_LO[:, k, sl], hi, start=False, stop=False)
                    mm = pe.matmul(dst, H_HI[:, k, sl], lo, start=False, stop=(k == 7))
                mm.then_inc(sem["acc_full"], 1)

            pe.wait_ge(sem["consts"], 1)
            for m in range(MOD_FIRST):
                mod_mm(pe, Count(m - MOD_FIRST))
            ones_sum(0)

            with pe.Fori(0, 4) as i:
                for j in range(2):
                    n = Count(T_V + 2 * j, 4, i)
                    pe.wait_ge(sem["w_lo"], (n + 2).v)
                    for chunk in range(NCHUNK):
                        u = Count(8 * j + chunk, 16, i)
                        pe.wait_ge(sem["v_gelu"], (u + 1).v)
                        token_unit(n, chunk, u % 2, 0 if j == 0 and chunk in (0, 4) else None)
                    mod_mm(pe, n - T_V)
                    mod_mm(pe, n - T_V + 1)

            for u in range(2 * NCHUNK):
                half = u % 2
                pe.wait_ge(sem["sp_lo"], u + 1)
                if u < 2:
                    pe.wait_ge(sem["v_gelu"], U_SP + 2)
                    pe.wait_ge(sem["ws_lo"], 1)
                else:
                    pe.wait_ge(sem["acc_free"], freed(U_SP + u - 2))
                for c in range(8):
                    g, sl = (8 * half + c) // 2, slice(c * P, (c + 1) * P)
                    dst = PS[:, 2 * (u % 2) + c // 4, (c % 4) * P:(c % 4 + 1) * P]
                    mm = three(dst, VC_HI[:, u % 2, sl], VC_LO[:, u % 2, sl], WS_HI[:, g, :], WS_LO[:, g, :],
                               True, True)
                mm.then_inc(sem["acc_full"], 1)

            def uz_ready(q4):
                return lambda k: pe.wait_ge(sem["uz_lo"], (q4 + k + 1).v)

            def c_tiles(i, q):
                for j in range(8):
                    n = Count(T_C + 8 * q + j, 8, i)
                    if j < 4:
                        wide_unit(n, Count(U_C + 12 * q + j, 12, i), H_HI, H_LO)
                    else:
                        narrow_units(n, Count(U_C + 12 * q + 2 * j - 4, 12, i), UZ_HI, UZ_LO,
                                     uz_ready(Count(4 * q, 4, i)) if j == 4 else None)
                    mod_mm(pe, n - T_V)
            with pe.Fori(0, 3) as i:
                c_tiles(i, 0)
            c_tiles(None, 3)
            ones_sum(1)

            def up(n, u, jm, piece=None):
                for j in range(4):
                    wide_unit(n + j, u + j, H_HI, H_LO, piece if j == 0 else None)
                    if jm is not None:
                        mod_mm(pe, jm + j)

            def down(n, u, e, hid_unit, jm):
                for j in range(4):
                    if j == 0:
                        ready = lambda k: pe.wait_ge(sem["acc_free"], freed(hid_unit + k).v)
                    narrow_units(n + j, u + 2 * j, HID_HI[e], HID_LO[e], ready if j == 0 else None)
                    if jm is not None:
                        mod_mm(pe, jm + j)

            def mlp(t0, u0, mods, piece):
                up(Count(t0), Count(u0), None, piece)
                with pe.Fori(0, 3) as i:
                    for a in range(2):
                        jm = Count(mods + 8 * a, 16, i) if mods is not None else None
                        up(Count(t0 + 4 + 8 * a, 16, i), Count(u0 + 4 + 12 * a, 24, i), jm)
                        before = Count(u0, 24, i) if a == 0 else Count(u0 + 4, 24, i)
                        down(Count(t0 + 8 + 8 * a, 16, i), Count(u0 + 8 + 12 * a, 24, i), a,
                             before, jm + 4 if jm is not None else None)
                up(Count(t0 + 52), Count(u0 + 76), None)
                down(Count(t0 + 56), Count(u0 + 80), 0, Count(u0 + 64), None)
                down(Count(t0 + 60), Count(u0 + 88), 1, Count(u0 + 76), None)

            mlp(T_M0, U_M0, 48, 16)
            ones_sum(2)

            with pe.Fori(0, 2) as i:
                for j in range(2):
                    n = Count(T_KV_V + 2 * j, 4, i)
                    pe.wait_ge(sem["w_lo"], (n + 2).v)
                    for chunk in range(NCHUNK):
                        u = Count(U_KV_V + 8 * j + chunk, 16, i)
                        pe.wait_ge(sem["acc_free"], freed(u - 2).v)
                        token_unit(n, chunk, u % 2, 32 if j == 0 and chunk in (0, 4) else None)

            def head_sums(c):
                pe.wait_ge(sem["kq_sq"], c + 1)
                pe.wait_ge(sem["consts"], 5)
                if c:
                    pe.wait_ge(sem["kq_rec"], c)
                for n in range(2):
                    pe.matmul(STAT[:, n, :], BLK[:], KSQ[:, n * HALF:(n + 1) * HALF], start=True, stop=True
                              ).then_inc(sem["kq_full"], 1)

            def kq(c0, t0, u0, piece):
                for j in range(KT):
                    wide_unit(Count(t0 + j), Count(u0 + j), H_HI, H_LO, piece if j == 0 else None,
                              (lambda: head_sums(c0 + j - 1)) if j else None)
                head_sums(c0 + KT - 1)

            kq(0, T_K, U_K, None)
            kq(KT, T_Q, U_Q, 48)

            def scores(h, par, b, first):
                n = h * KT + b
                r = slice(HD * par, HD * par + HD)
                if b == 0:
                    pe.wait_ge(sem[f"qk_in{par}"], ((h // 2) * 16 + 16).v)
                if not (first and par == 0 and b < 2):
                    pe.wait_ge(sem["keep_ok"], (n - 1).v)
                q = QK[r, 0:2, b * P:(b + 1) * P]
                for part in range(1 if b >= 4 else 2):
                    c0, c1 = b * P + part * HALF, min(b * P + (part + 1) * HALF, S)
                    dst = PS[:, 2 * (b % 2) + part, 0:c1 - c0]
                    k = QK[r, 2:4, c0:c1]
                    mm = three(dst, q[:, 0, :], q[:, 1, :], k[:, 0, :], k[:, 1, :], True, True)
                mm.then_inc(sem["z_full"], 1)

            def turn(h, par, s, first):
                g, j = GROUP[s]
                n = h * len(GROUP) + s
                if s == 0:
                    pe.wait_ge(sem["a_ok"], ((h + 1) * KT).v)
                if not (first and s < 2):
                    pe.wait_ge(sem["at_lo"], (n - 1).v)
                blocks = min(j - 4 * g + 1, 4)
                for b in range(blocks):
                    t = 4 * g + b
                    c = STRIP[t] + (j - t) * P
                    mm = pe.transpose(PS[:, 4 + s % 2, b * P:(b + 1) * P], A[:, par, c:c + P], IDENT[:])
                mm.then_inc(sem["at_full"], 1)

            def weigh(h, par, s, first):
                g, j = GROUP[s]
                n = h * len(GROUP) + s
                w = min(j - 4 * g + 1, 4) * P
                if s == 0:
                    pe.wait_ge(sem[f"v_in{par}"], ((h // 2) * 16 + 16).v)
                if j == KT - 1 and not first:
                    pe.wait_ge(sem["o_sum"], (h * 2 + g - 1).v)
                pe.wait_ge(sem["at_lo"], (n + 1).v)
                dst = PS[:, 6 + g, 0:w]
                pe.matmul(dst, VH[:, par, j, :], AT_HI[:, s % 2, 0:w], start=(j == KT - 1), stop=False)
                pe.matmul(dst, VH[:, par, j, :], AT_LO[:, s % 2, 0:w], start=False, stop=(j == 4 * g)
                          ).then_inc(sem["av_done"], 1)

            def both(h1, p1, h2, p2, first1, first2):
                if h2 is not None:
                    turn(h2, p2, 0, first2)
                for s in range(len(GROUP)):
                    if h2 is not None and s + 1 < len(GROUP):
                        turn(h2, p2, s + 1, first2)
                    if h1 is not None and s < KT:
                        scores(h1, p1, s, first1)
                    if h2 is not None:
                        weigh(h2, p2, s, first2)

            pe.wait_ge(sem["acc_free"], freed(U_O - 1))
            pe.wait_ge(sem["ident_ok"], 3)
            both(Count(0), 0, None, 0, True, False)
            both(Count(1), 1, Count(0), 0, False, True)
            with pe.Fori(0, 7) as i:
                both(Count(2, 2, i), 0, Count(1, 2, i), 1, False, False)
                both(Count(3, 2, i), 1, Count(2, 2, i), 0, False, False)
            both(None, 0, Count(HEADS - 1), 1, False, False)

            pe.wait_ge(sem["o_lo"], 2 * HEADS)
            for j in range(KT):
                wide_unit(Count(T_O + j), Count(U_O + j), OT_HI, OT_LO)
            ones_sum(3)
            mlp(T_M1, U_M1, None, 64)


def tiles_of(w, rows):
    cols = 1024 // rows
    k, n = w.shape
    a = w.reshape(k // (rows * P), rows, P, n // cols, cols)
    return a.transpose(0, 3, 2, 1, 4).reshape(-1, P, 1024)


def column(v):
    return np.ascontiguousarray(v.reshape(-1, P).T)


def mlp_tiles(up, down):
    u = tiles_of(up, 8).reshape(8, 4, P, 1024)
    d = tiles_of(down, 4).reshape(8, 4, P, 1024)
    parts = [u[0]]
    for e in range(7):
        parts += [u[e + 1], d[e]]
    return parts + [d[7]]


def kernel(x, c, mod_w, mod_b, norm_g, mlp_w_up, mlp_w_down, a_w_in, a_v_norm_g, a_w_spatial, a_b_spatial,
           a_w_out, kv_mod_w, kv_mod_b, kv_norm_g, kv_w, k_norm_g, b_w_q, q_norm_g, b_w_out):
    import concourse.bacc as bacc
    from concourse.bass_utils import run_bass_kernel_spmd

    args = [np.asarray(a) for a in (x, c, mod_w, mod_b, norm_g, mlp_w_up, mlp_w_down, a_w_in, a_v_norm_g,
                                    a_w_spatial, a_b_spatial, a_w_out, kv_mod_w, kv_mod_b, kv_norm_g, kv_w,
                                    k_norm_g, b_w_q, q_norm_g, b_w_out)]
    (x, c, mod_w, mod_b, norm_g, mlp_w_up, mlp_w_down, a_w_in, a_v_norm_g, a_w_spatial, a_b_spatial,
     a_w_out, kv_mod_w, kv_mod_b, kv_norm_g, kv_w, k_norm_g, b_w_q, q_norm_g, b_w_out) = args

    u_t = tiles_of(a_w_in[0][:, 0:W], 8).reshape(4, 4, P, 1024)
    o_t = tiles_of(a_w_out[0], 4).reshape(4, 4, P, 1024)
    stream = [tiles_of(a_w_in[0][:, W:2 * W], 8)]
    for q in range(4):
        stream += [u_t[q], o_t[q]]
    stream += mlp_tiles(mlp_w_up[0], mlp_w_down[0])
    stream += [tiles_of(kv_w[:, D:2 * D], 8), tiles_of(kv_w[:, 0:D], 8), tiles_of(b_w_q[0], 8),
               tiles_of(b_w_out[0], 8)]
    stream += mlp_tiles(mlp_w_up[1], mlp_w_down[1])

    arrays = {
        "xT": np.ascontiguousarray(x[0, ::-1].T.reshape(KT, P, S).transpose(1, 0, 2)),
        "cT": column(c[0]),
        "wt": np.concatenate(stream),
        "modw": np.concatenate([tiles_of(m, 8) for m in (mod_w[0], kv_mod_w, mod_w[1])]).reshape(MODS, P, 8, P),
        "modb": column(np.concatenate([mod_b[0], kv_mod_b, mod_b[1]])),
        "ng": column(np.concatenate([norm_g[0, 0], norm_g[0, 1], kv_norm_g, norm_g[1, 0], norm_g[1, 1]])),
        "vg": column(a_v_norm_g[0]),
        "qkg": np.ascontiguousarray(np.stack([np.concatenate([k_norm_g] * 2), np.concatenate([q_norm_g[0]] * 2)], 1)),
        "spw": np.ascontiguousarray(a_w_spatial[0][:, ::-1, ::-1].transpose(2, 0, 1)),
        "spb": np.ascontiguousarray(np.broadcast_to(a_b_spatial[0][:, ::-1].reshape(1, -1), (P, GROUPS * CHUNK))),
    }
    nc = bacc.Bacc("TRN2", target_bir_lowering=False, num_devices=1)
    aps = [nc.dram_tensor(f"in_{n}", a.shape, mybir.dt.from_np(a.dtype), kind="ExternalInput").ap()
           for n, a in arrays.items()]
    out = nc.dram_tensor("out_x", (P, KT, S), F32, kind="ExternalOutput").ap()
    build(nc, *aps, out)
    r = run_bass_kernel_spmd(nc, [{f"in_{n}": a for n, a in arrays.items()}], core_ids=[0])
    y = r.results[0]["out_x"]
    return np.ascontiguousarray(y.transpose(1, 0, 2).reshape(D, S).T[::-1])[None]
```

```python
import numpy as np
from contextlib import ExitStack

import concourse.bass as bass
from concourse import mybir

F32 = mybir.dt.float32
F32R = mybir.dt.float32r
ACT = mybir.ActivationFunctionType
ALU = mybir.AluOpType
AX = mybir.AxisListType

P = 128
D = 1024
S = 1024
KT = D // P
HALF = S // 2
W = 2 * D
GROUPS = 8
CHUNK = 128
NCHUNK = S // CHUNK
CT = W // P
FF = 4 * D
HEADS = 16
HD = D // HEADS
EPS = 1e-6
RING = 4
AHEAD = 3

T_V = 0
T_U = T_V + W // P
T_G = T_U + W // P
T_M0 = T_G + W // P
T_KV_V = T_M0 + 2 * (FF // P)
T_K = T_KV_V + D // P
T_Q = T_K + D // P
T_O = T_Q + D // P
T_M1 = T_O + D // P
TILES = T_M1 + 2 * (FF // P)

(SH1A, SC1A, G1A, SH2A, SC2A, G2A, SHKV, SCKV, SH1B, SC1B, G1B, SH2B, SC2B, G2B) = range(0, 14 * KT, KT)
MODS = 14 * KT
MOD_FIRST = 2 * KT
NORMS = ((SH1A, SC1A), (SH2A, SC2A), (SHKV, SCKV), (SH1B, SC1B), (SH2B, SC2B))

U_V = 0
U_SP = U_V + W // P // 2 * NCHUNK
U_U = U_SP + 2 * NCHUNK
U_G = U_U + W // P // 2 * NCHUNK
U_M0 = U_G + 4 + 3 * 12 + 8
U_KV_V = U_M0 + 8 * 12
U_K = U_KV_V + 4 * NCHUNK
U_Q = U_K + KT
U_O = U_Q + KT
U_M1 = U_O + KT


def gate_unit(q, j):
    return U_G + 4 + 12 * q + (3 if q < 3 else 2) * j


def turn_unit(q, j):
    return U_G + j if q == 0 else gate_unit(q - 1, j) + 2


def unit_at(t):
    if t < T_U:
        return U_V + (t + 1) // 2 * NCHUNK
    if t < T_G:
        return U_U + (t - T_U + 1) // 2 * NCHUNK
    if t < T_M0:
        return gate_unit(*divmod(t - T_G, 4))
    if t >= T_M1 or t < T_KV_V:
        u0, j = (U_M1, t - T_M1) if t >= T_M1 else (U_M0, t - T_M0)
        if j < 4:
            return u0 + j
        if j >= 60:
            return u0 + 88 + 2 * (j - 60)
        b, j = divmod(j - 4, 8)
        return u0 + 4 + 12 * b + (j if j < 4 else 2 * j - 4)
    if t < T_K:
        return U_KV_V + (t - T_KV_V + 1) // 2 * NCHUNK
    return U_K + t - T_K


def freed(u):
    return u - (U_U - 3)


STRIP = [sum((KT - j) * P for j in range(b)) for b in range(KT + 1)]
STRIPS = list(range(KT - 1, -1, -1))
SLOT_OF = {0: 0, 1: 1, 2: 2, 3: 3, 5: 4, 6: 5, 7: 6, 9: 7}
GROUP = [(g, j) for g in range(2) for j in range(KT - 1, 4 * g - 1, -1)]


class Count:

    def __init__(self, c, s=0, i=None):
        self.c, self.s, self.i = c, (s if i is not None else 0), i

    def __add__(self, n):
        return Count(self.c + n, self.s, self.i)

    def __sub__(self, n):
        return self + (-n)

    def __mul__(self, n):
        return Count(self.c * n, self.s * n, self.i)

    def __floordiv__(self, n):
        assert self.s % n == 0
        return Count(self.c // n, self.s // n, self.i)

    def __mod__(self, n):
        assert self.s % n == 0
        return self.c % n

    @property
    def v(self):
        if self.i is None or self.s == 0:
            return self.c
        return self.i * self.s + self.c


def build(nc, xT, cT, wt, modw, modb, ng, vg, qkg, spw, spb, out):
    with ExitStack() as ctx:
        sem_names = """
            small_in xa_in xb_in m0_in0 m0_in1 m0_in2 m0_in3 raw_in0 raw_in1 mod_in spw_in vg_in x_back
            x_spilled vs_out0 vs_out1 kq_out qk_in0 qk_in1 v_in0 v_in1 y_out consts w_hi w_lo
            m0_mul_pool m0_mul_dve mod_mul mod_red mod_mm mod_vec av_done sq_done s_added stat_full
            rs_sqrt rs_done t_mul hf_done h_hi h_lo v_gelu v_ss v_rms v_rstd ws_mask ws_hi ws_lo
            sp_scaled sp_hi sp_lo acc_full acc_free u_gelu uz_hi relu_done hid_hi vs_hi kq_sq kq_full
            kq_sqrt kq_rec kq_norm kq_hi kq_lo ident_ok mask_turn z_full keep_ok beta_ok masked scanned
            a_ok at_full at_hi at_lo o_bot o_sum o_hi o_lo sp_z
        """.split()
        sem = {n: ctx.enter_context(nc.semaphore(n)) for n in sem_names}

        base = -(-nc.sbuf_base // 32) * 32

        def at(name, shape, dt, off):
            return nc.alloc_sbuf_tensor_at(name, shape, dt, offset=base + off)

        KB = 1024
        RX, RB, RH, RR, RW, RC = 0, 32 * KB, 96 * KB, 160 * KB, 192 * KB, 200 * KB
        X = at("X", [P, KT, S], F32, RX)
        H_HI = at("H_HI", [P, KT, S], F32R, RH)
        H_LO = at("H_LO", [P, KT, S], F32R, RH + 32 * KB)
        W_HI = at("W_HI", [P, 8, RING * P], F32R, RR)
        W_LO = at("W_LO", [P, 8, RING * P], F32R, RR + 16 * KB)
        RAW = at("RAW", [P, 2, 1024], F32, RW)
        MODRAW = at("MODRAW", [P, 8, P], F32, RC)
        co = [RC + 4 * KB]

        def small(name, cols):
            t = at(name, [P, cols], F32, co[0])
            co[0] += -(-cols * 4 // 32) * 32
            return t

        MODACC = small("MODACC", 2 * P)
        ONES = small("ONES", P)
        MODV = small("MODV", MODS)
        MODB = small("MODB", MODS)
        NG = small("NG", 5 * KT)
        GS = small("GS", 5 * KT)
        QKG = small("QKG", 2)
        CC = small("CC", KT)
        BS = small("BS", GROUPS)
        IDENT = small("IDENT", P)
        EPSC = small("EPSC", 1)
        SS = small("SS", KT)
        RSTDV = small("RSTDV", KT)
        assert co[0] <= 212800, co[0]

        RS = at("RS", [P, S], F32, RB + 12 * KB)
        TT = at("TT", [P, 2, HALF], F32, RB + 16 * KB)
        HF = at("HF", [P, 2, HALF], F32, RB + 20 * KB)
        SUMSQ = at("SUMSQ", [P, S], F32, RB)
        SQ = at("SQ", [P, 2, S], F32, RB + 24 * KB)
        V = at("V", [P, NCHUNK, W], F32, RB)
        UZ_HI = [at(f"UZ_HI{e}", [P, 4, S], F32R, RH + 32 * KB * e) for e in range(2)]
        UZ_LO = [at(f"UZ_LO{e}", [P, 4, S], F32R, RH + 32 * KB * e + 16 * KB) for e in range(2)]
        HID_HI = [at(f"HID_HI{e}", [P, 4, S], F32R, RB + 32 * KB * e) for e in range(2)]
        HID_LO = [at(f"HID_LO{e}", [P, 4, S], F32R, RB + 32 * KB * e + 16 * KB) for e in range(2)]
        MOD0 = at("MOD0", [P, MOD_FIRST, 8, P], F32, RH)
        WS_HI = at("WS_HI", [P, GROUPS, CHUNK], F32R, RX)
        WS_LO = at("WS_LO", [P, GROUPS, CHUNK], F32R, RX + 4 * KB)
        VC_HI = at("VC_HI", [P, 2, W // 2], F32R, RX + 8 * KB)
        VC_LO = at("VC_LO", [P, 2, W // 2], F32R, RX + 16 * KB)
        GBC = at("GBC", [P, W], F32, RX + 24 * KB)
        TRASH = at("TRASH", [P, W], F32, RX + 8 * KB)
        WS_RAW = at("WS_RAW", [P, GROUPS, CHUNK], F32, RX + 16 * KB)
        KSQ = at("KSQ", [P, S], F32, RB + 32 * KB)
        KRAW = at("KRAW", [P, 2, S], F32, RB + 36 * KB)
        KN = at("KN", [P, S], F32, RB + 44 * KB)
        KOUT = at("KOUT", [P, 2, S], F32R, RB + 48 * KB)
        VST = at("VST", [P, 2, 4, 2 * HD], F32R, RB + 56 * KB)
        BLK = at("BLK", [P, P], F32, RB + 60 * KB)
        QK = at("QK", [P, 4, S], F32R, RX)
        A = at("A", [P, 2, STRIP[KT]], F32, RH)
        KEEP = at("KEEP", [P, 2, S + 8], F32, RH + 36 * KB)
        VH = at("VH", [P, 2, NCHUNK, 2 * HD], F32R, RH + 36 * KB + 8256)
        AT_HI = at("AT_HI", [P, 2, HALF], F32R, RH + 36 * KB + 8256 + 8192)
        AT_LO = at("AT_LO", [P, 2, HALF], F32R, RH + 36 * KB + 8256 + 12288)
        OSUM = at("OSUM", [P, HALF], F32, RH + 36 * KB + 8256 + 16384)
        SUMSQ3 = at("SUMSQ3", [P, S], F32, RH)
        SQ3 = at("SQ3", [P, 2, S], F32, RH + 4 * KB)
        OT_HI = at("OT_HI", [P, KT, S], F32R, RB)
        OT_LO = at("OT_LO", [P, KT, S], F32R, RB + 32 * KB)

        PS = ctx.enter_context(nc.psum_tensor("PS", [P, 8, HALF], F32))
        STAT = PS[:, 4:6, :]
        MODPS = PS[:, 6, 0:MODS]

        def acc(slot):
            return PS[:, 2 * slot:2 * slot + 2, :]

        def flat(ap):
            return ap.rearrange("p a b -> p (a b)")

        XD = nc.dram_tensor("x_scratch", [P, KT, S], F32).ap()
        VD = nc.dram_tensor("v_scratch", [HEADS, NCHUNK, P, 2 * HD], F32).ap()
        QKD = nc.dram_tensor("qk_scratch", [KT, P, 4, S], F32).ap()

        def raw_view(n):
            return RAW[:, n % 2, :].rearrange("p (k c) -> p k c", k=8)

        def ring_view(t, n):
            s = n % RING
            return t[:, :, s * P:(s + 1) * P]

        def read_before(n):
            a = unit_at(n.c - RING + 1)
            return Count(a, unit_at(n.c + n.s - RING + 1) - a, n.i) if n.i is not None else Count(a)

        def load_raw(sp, n):
            if n.i is not None or n.c >= 2:
                sp.wait_ge(sem["w_lo"], (n - 1).v)
            sp.dma_start(RAW[:, n % 2, :], wt[n.v]).then_inc(sem[f"raw_in{n % 2}"], 16)

        def load_mod(sp, j):
            if j.i is not None or j.c >= 1:
                sp.wait_ge(sem["mod_red"], (j + MOD_FIRST).v)
            sp.dma_start(MODRAW[:], modw[(j + MOD_FIRST).v]).then_inc(sem["mod_in"], 16)

        def cut_hi(act, n):
            act.wait_ge(sem[f"raw_in{n % 2}"], ((n // 2) * 16 + 16).v)
            if n.i is not None or n.c >= RING:
                act.wait_ge(sem["acc_full"], read_before(n).v)
            act.activation(ring_view(W_HI, n), raw_view(n), ACT.Copy).then_inc(sem["w_hi"], 1)

        def cut_lo(dve, n):
            dve.wait_ge(sem["w_hi"], (n + 1).v)
            dve.tensor_tensor(ring_view(W_LO, n), raw_view(n), ring_view(W_HI, n).bitcast(F32),
                              ALU.subtract).then_inc(sem["w_lo"], 1)

        def mod_reduce(dve, j):
            dve.wait_ge(sem["mod_mul"], (j + 1).v)
            dve.wait_ge(sem["mod_mm"], (j + MOD_FIRST - 1).v)
            dve.tensor_reduce(MODACC[:, (j % 2) * P:(j % 2 + 1) * P], MODRAW[:].rearrange("p k c -> p c k"),
                              AX.X, ALU.add).then_inc(sem["mod_red"], 1)

        def mod_mm(pe, j):
            m = j + MOD_FIRST
            pe.wait_ge(sem["mod_red"], (m + 1).v)
            pe.matmul(PS[:, 6, bass.ds(m.v, 1)], MODACC[:, (j % 2) * P:(j % 2 + 1) * P], ONES[:, 0:1],
                      start=True, stop=True).then_inc(sem["mod_mm"], 1)

        block = ctx.enter_context(nc.Block())
        piece_of_norm = lambda r: 16 * r

        @block.sync
        def _(sp):
            for dst, src in ((CC, cT), (MODB, modb), (NG, ng), (BS, spb), (QKG, qkg)):
                sp.dma_start(dst[:], src).then_inc(sem["small_in"], 16)
            for a in range(4):
                sp.dma_start(MOD0[:, 4 * a:4 * a + 4, :, :],
                             modw[4 * a:4 * a + 4].rearrange("m p k c -> p m k c")).then_inc(sem[f"m0_in{a}"], 16)
            sp.dma_start(X[:, 0:4, :], xT[:, 0:4, :]).then_inc(sem["xa_in"], 16)
            sp.dma_start(X[:, 4:8, :], xT[:, 4:8, :]).then_inc(sem["xb_in"], 16)
            for n in range(5):
                load_raw(sp, Count(n))
            load_mod(sp, Count(0))
            sp.wait_ge(sem["h_lo"], 16)
            sp.dma_start(WS_RAW[:], spw).then_inc(sem["spw_in"], 16)
            sp.dma_start(GBC[:], vg).then_inc(sem["vg_in"], 16)

            def v_tiles(i, js):
                for j in js:
                    n = Count(T_V + j, 4, i)
                    load_raw(sp, n + 5)
                    load_mod(sp, n - T_V + 1)
            with sp.Fori(0, 4) as i:
                v_tiles(i, range(4))

            sp.wait_ge(sem["sp_z"], 2 * NCHUNK)
            sp.dma_start(X[:], xT).then_inc(sem["x_back"], 16)

            with sp.Fori(0, 4) as i:
                v_tiles(i, range(T_U, T_U + 4))

            def m_tiles(first, stop, ld_mod, i=None, step=0, t_end=TILES):
                for t in range(first, stop):
                    n = Count(t, step, i)
                    if i is not None or t + 5 < t_end:
                        load_raw(sp, n + 5)
                    if ld_mod is not None:
                        j = n - ld_mod + 1
                        load_mod(sp, j)

            m_tiles(T_G, T_M0, T_V)
            m_tiles(T_M0, T_M0 + 4, None)
            with sp.Fori(0, 2) as i:
                m_tiles(T_M0 + 4, T_M0 + 20, T_V + 4, i, 16)
            m_tiles(T_M0 + 36, T_M0 + 51, T_V + 4)
            m_tiles(T_M0 + 51, T_M0 + 64, None)

            sp.wait_ge(sem["acc_free"], freed(U_M0 + 95))
            sp.dma_start(XD[:], X[:]).then_inc(sem["x_spilled"], 16)

            for u in range(4 * NCHUNK):
                pair, chunk = divmod(u, NCHUNK)
                if chunk in (1, 7):
                    load_raw(sp, Count(T_KV_V + 2 * pair + (chunk == 7) + 5))
                sp.wait_ge(sem["acc_free"], freed(U_KV_V + u))
                sp.dma_start(VD[4 * pair:4 * pair + 4, chunk].rearrange("h p d -> p h d"),
                             VST[:, chunk % 2, :, :].bitcast(F32)).then_inc(sem[f"vs_out{chunk % 2}"], 16)

            for kind, t0, c0 in ((1, T_K, 0), (0, T_Q, KT)):
                for j in range(KT):
                    load_raw(sp, Count(t0 + j + 5))
                    sp.wait_ge(sem["kq_lo"], c0 + j + 1)
                    sp.dma_start(QKD[j, :, 2 * kind:2 * kind + 2, :], KOUT[:].bitcast(F32)).then_inc(sem["kq_out"], 16)
                    if kind == 0 and j == 1:
                        sp.wait_ge(sem["kq_out"], 16 * (KT + 1))
                        sp.wait_ge(sem["x_spilled"], 16)
                        sp.wait_ge(sem["t_mul"], piece_of_norm(4))
                        for par in range(2):
                            sp.dma_start(QK[64 * par:64 * par + 64, :, :].bitcast(F32),
                                         QKD[0, 64 * par:64 * par + 64]).then_inc(sem[f"qk_in{par}"], 16)

            sp.wait_ge(sem["kq_out"], 16 * 2 * KT)
            for b in range(2):
                sp.wait_ge(sem[f"vs_out{b}"], 16 * 2 * NCHUNK)
            def load_v(h, par):
                sp.dma_start(VH[:, par, :, :].bitcast(F32), VD[h.v].rearrange("c p d -> p c d")).then_inc(sem[f"v_in{par}"], 16)

            sp.wait_ge(sem["acc_full"], U_O)
            for par in range(2):
                load_v(Count(par), par)
            with sp.Fori(0, 7) as i:
                for par in range(2):
                    h = Count(par, 2, i)
                    sp.wait_ge(sem["z_full"], ((h + 1) * KT).v)
                    sp.dma_start(QK[64 * par:64 * par + 64, :, :].bitcast(F32), QKD[Count(1, 1, i).v, 64 * par:64 * par + 64]
                                 ).then_inc(sem[f"qk_in{par}"], 16)
                    sp.wait_ge(sem["av_done"], ((h + 1) * len(GROUP)).v)
                    load_v(h + 2, par)
            sp.wait_ge(sem["z_full"], HEADS * KT)
            sp.dma_start(X[:], XD[:]).then_inc(sem["x_back"], 16)

            for t in range(T_O, T_O + 8):
                load_raw(sp, Count(t + 5))
            m_tiles(T_M1, T_M1 + 4, None)
            with sp.Fori(0, 3) as i:
                m_tiles(T_M1 + 4, T_M1 + 20, None, i, 16)
            m_tiles(T_M1 + 52, T_M1 + 64, None)
            for k in range(KT):
                sp.wait_ge(sem["acc_free"], freed(U_M1 + 88 + k))
                sp.dma_start(out[:, k, :], X[:, k, :]).then_inc(sem["y_out"], 16)
            sp.wait_ge(sem["y_out"], 16 * KT)

        @block.gpsimd
        def _(pool):
            pool.memset(ONES[:], 1.0).then_inc(sem["consts"], 1)
            pool.memset(EPSC[:], EPS).then_inc(sem["consts"], 1)
            pool.memset(IDENT[:], 0.0).then_inc(sem["ident_ok"], 1)
            pool.wait_ge(sem["ident_ok"], 1)
            pool.affine_select(out=IDENT[:], in_=IDENT[:], compare_op=ALU.not_equal, fill=1.0, base=0,
                               pattern=[[-1, P]], channel_multiplier=1).then_inc(sem["ident_ok"], 1)
            cb = CC[:].unsqueeze(2).to_broadcast([P, 8, P])
            pool.wait_ge(sem["small_in"], 80)
            for m in range(1, MOD_FIRST, 2):
                pool.wait_ge(sem[f"m0_in{m // 4}"], 16)
                pool.tensor_tensor(MOD0[:, m], MOD0[:, m], cb, ALU.mult).then_inc(sem["m0_mul_pool"], 1)
            pool.wait_ge(sem["spw_in"], 16)
            pool.affine_select(out=WS_RAW[:], in_=WS_RAW[:], compare_op=ALU.is_ge, fill=0.0, base=0,
                               pattern=[[0, GROUPS], [-1, CHUNK]], channel_multiplier=1).then_inc(sem["ws_mask"], 1)
            with pool.Fori(0, MODS - MOD_FIRST) as i:
                j = Count(0, 1, i)
                pool.wait_ge(sem["mod_in"], ((j + 1) * 16).v)
                pool.tensor_tensor(MODRAW[:], MODRAW[:], cb, ALU.mult).then_inc(sem["mod_mul"], 1)
            pool.wait_ge(sem["acc_free"], freed(U_M0 + 95))
            pool.memset(BLK[:], 0.0).then_inc(sem["consts"], 1)
            pool.wait_ge(sem["consts"], 3)
            pool.memset(BLK[0:HD, 0:HD], 1.0).then_inc(sem["consts"], 1)
            pool.memset(BLK[HD:P, HD:P], 1.0).then_inc(sem["consts"], 1)
            pool.wait_ge(sem["acc_full"], U_O)
            pool.memset(KEEP[:, :, 0:1], 1.0).then_inc(sem["ident_ok"], 1)

            def mask(h, par):
                for k, b in enumerate(STRIPS):
                    n = h * KT + k
                    pool.wait_ge(sem["keep_ok"], (n + 1).v)
                    pool.sem_inc(sem["mask_turn"], 1)
                    a = A[:, par, STRIP[b]:STRIP[b] + P]
                    pool.affine_select(out=a, in_=a, compare_op=ALU.is_gt, fill=0.0, base=0,
                                       pattern=[[1, P]], channel_multiplier=-1).then_inc(sem["masked"], 1)
                    keep = KEEP[:, k % 2, 1:1 + P]
                    pool.affine_select(out=keep, in_=keep, compare_op=ALU.is_gt, fill=1.0, base=0,
                                       pattern=[[1, P]], channel_multiplier=-1).then_inc(sem["masked"], 1)
            with pool.Fori(0, HEADS // 2) as i:
                for par in range(2):
                    mask(Count(par, 2, i), par)

        @block.scalar
        def _(act):
            act.sem_inc(sem["v_gelu"], 2)
            act.wait_ge(sem["consts"], 2)

            def square_x(s, k, u, sq=SQ):
                act.wait_ge(sem["acc_free"], freed(u))
                if k >= 2:
                    act.wait_ge(sem["s_added"], 8 * s + k - 1)
                act.activation(sq[:, k % 2, :], X[:, k, :], ACT.Square).then_inc(sem["sq_done"], 1)

            def rms_root(s):
                for n in range(2):
                    act.wait_ge(sem["stat_full"], 2 * s + n + 1)
                    act.activation(STAT[:, n, :], STAT[:, n, :], ACT.Sqrt, bias=EPSC[:, 0:1], scale=1.0 / D
                                   ).then_inc(sem["rs_sqrt"], 1)

            def modulate(r):
                sh, _ = NORMS[r]
                for i in range(16):
                    n, k, b = i // 8, i % 8, 16 * r + i
                    g, s0 = GS[:, KT * r + k:KT * r + k + 1], MODV[:, sh + k:sh + k + 1]
                    act.wait_ge(sem["t_mul"], b + 1)
                    if i >= 2:
                        act.wait_ge(sem["h_lo"], b - 1)
                    act.activation(HF[:, i % 2, :], TT[:, i % 2, :], ACT.Identity, bias=s0, scale=g
                                   ).then_inc(sem["hf_done"], 1)
                    act.activation(H_HI[:, k, n * HALF:(n + 1) * HALF], TT[:, i % 2, :], ACT.Identity,
                                   bias=s0, scale=g).then_inc(sem["h_hi"], 1)

            for k in range(KT):
                act.wait_ge(sem["xa_in" if k < 4 else "xb_in"], 16)
                if k >= 2:
                    act.wait_ge(sem["s_added"], k - 1)
                act.activation(SQ[:, k % 2, :], X[:, k, :], ACT.Square).then_inc(sem["sq_done"], 1)
            for n in range(AHEAD):
                cut_hi(act, Count(n))
            rms_root(0)
            act.wait_ge(sem["mod_vec"], 2)
            modulate(0)

            def v_pair(i, j, last):
                n = Count(T_V + 2 * j, 4, i)
                cut_hi(act, n + AHEAD)
                for chunk in range(NCHUNK):
                    u = Count(8 * j + chunk, 16, i)
                    act.wait_ge(sem["acc_full"], (u + U_V + 1).v)
                    if chunk == 4:
                        act.wait_ge(sem["h_lo"], 16)
                    act.activation(V[:, (chunk + 4) % 8, bass.ds((n * P).v, 2 * P)], acc(u % 2)[:, 0, 0:2 * P],
                                   ACT.Gelu).then_inc(sem["v_gelu"], 1)
                cut_hi(act, n + AHEAD + 1)
            with act.Fori(0, 4) as i:
                for j in range(2):
                    v_pair(i, j, False)

            act.wait_ge(sem["ws_mask"], 1)
            act.activation(WS_HI[:], WS_RAW[:], ACT.Copy).then_inc(sem["ws_hi"], 1)

            act.wait_ge(sem["v_ss"], NCHUNK)
            act.activation(RSTDV[:], SS[:], ACT.Sqrt, bias=EPSC[:, 0:1], scale=1.0 / W).then_inc(sem["v_rms"], 1)

            act.wait_ge(sem["v_rstd"], 1)
            act.wait_ge(sem["ws_lo"], 1)
            def sp_cut(u):
                place, half = u // 2, u % 2
                act.wait_ge(sem["sp_scaled"], u + 1)
                if u >= 2:
                    act.wait_ge(sem["acc_full"], U_SP + u - 1)
                act.activation(VC_HI[:, u % 2, :], V[:, place, half * 1024:(half + 1) * 1024], ACT.Copy
                               ).then_inc(sem["sp_hi"], 1)

            sp_cut(0)
            for u in range(2 * NCHUNK):
                place, half = u // 2, u % 2
                if u + 1 < 2 * NCHUNK:
                    sp_cut(u + 1)
                act.wait_ge(sem["acc_full"], U_SP + u + 1)
                act.wait_ge(sem["sp_lo"], u + 1)
                for g in range(4):
                    c0 = half * 1024 + g * 2 * P
                    z = act.activation(V[:, place, c0:c0 + 2 * P],
                                       acc(u % 2)[:, g // 2, (g % 2) * 2 * P:(g % 2 + 1) * 2 * P],
                                       ACT.Identity, bias=BS[:, 4 * half + g:4 * half + g + 1])
                z.then_inc(sem["sp_z"], 1)

            with act.Fori(0, 4) as i:
                for j in range(2):
                    n = Count(T_U + 2 * j, 4, i)
                    cut_hi(act, n + AHEAD)
                    for chunk in range(NCHUNK):
                        u = Count(U_U + 8 * j + chunk, 16, i)
                        act.wait_ge(sem["acc_full"], (u + 1).v)
                        p = acc(u % 2)[:, 0, 0:2 * P]
                        act.activation(p, p, ACT.Gelu).then_inc(sem["u_gelu"], 1)
                    cut_hi(act, n + AHEAD + 1)

            def uz_cut(q, j):
                u = turn_unit(q, j)
                act.wait_ge(sem["acc_full"], u + 1)
                act.activation(UZ_HI[q % 2][:, j, :], flat(acc(u % 2)), ACT.Copy).then_inc(sem["uz_hi"], 1)

            for j in range(4):
                uz_cut(0, j)
            for q in range(4):
                for j in range(4):
                    cut_hi(act, Count(T_G + 4 * q + j + AHEAD))
                    if q < 3:
                        uz_cut(q + 1, j)
                    elif j:
                        for k in (2 * j - 2, 2 * j - 1):
                            square_x(1, k, gate_unit(3, 0) + k)
            for k in (KT - 2, KT - 1):
                square_x(1, k, gate_unit(3, 0) + k)
            rms_root(1)
            act.wait_ge(sem["mod_vec"], 6)
            modulate(1)

            def up(n, hx, u, e, cut):
                for j in range(4):
                    if cut:
                        cut_hi(act, n + j + AHEAD)
                    act.wait_ge(sem["relu_done"], (hx + j + 1).v)
                    p = acc((u + j) % 2)
                    act.activation(HID_HI[e][:, j, :], flat(p), ACT.Square).then_inc(sem["hid_hi"], 1)
                    act.activation(p, p, ACT.Square).then_inc(sem["hid_hi"], 1)

            def down(n, stat=None, u=0):
                for j in range(4):
                    if n.i is not None or n.c + j + AHEAD < TILES:
                        cut_hi(act, n + j + AHEAD)
                    if stat is not None and j:
                        square_x(stat, 2 * j - 2, u + 2 * j - 2)
                        square_x(stat, 2 * j - 1, u + 2 * j - 1)

            def mlp(t0, h0, u0, stat):
                up(Count(t0), Count(h0), Count(u0), 0, True)
                with act.Fori(0, 3) as i:
                    for a in range(2):
                        up(Count(t0 + 4 + 8 * a, 16, i), Count(h0 + 4 + 4 * a, 8, i),
                           Count(u0 + 4 + 12 * a, 24, i), (a + 1) % 2, True)
                        down(Count(t0 + 8 + 8 * a, 16, i))
                up(Count(t0 + 52), Count(h0 + 28), Count(u0 + 76), 1, True)
                down(Count(t0 + 56))
                down(Count(t0 + 60), stat, u0 + 88)

            mlp(T_M0, 0, U_M0, 2)
            for k in (KT - 2, KT - 1):
                square_x(2, k, U_M0 + 88 + k)
            rms_root(2)
            act.wait_ge(sem["mod_vec"], 6)
            modulate(2)

            for u in range(4 * NCHUNK):
                pair, chunk = divmod(u, NCHUNK)
                if chunk == 0:
                    cut_hi(act, Count(T_KV_V + 2 * pair + AHEAD))
                act.wait_ge(sem["acc_full"], U_KV_V + u + 1)
                if u >= 2:
                    act.wait_ge(sem[f"vs_out{u % 2}"], 16 * (u // 2))
                src = acc(u % 2)[:, 0, 0:2 * P].rearrange("p (h d) -> p h d", h=4)
                act.activation(VST[:, u % 2, :, 0:HD], src, ACT.Copy).then_inc(sem["vs_hi"], 1)
                if chunk == NCHUNK - 1:
                    cut_hi(act, Count(T_KV_V + 2 * pair + AHEAD + 1))

            def kq_square(c, u):
                act.wait_ge(sem["acc_full"], u + 1)
                if c:
                    act.wait_ge(sem["kq_full"], 2 * c)
                act.activation(KSQ[:], flat(acc(u % 2)), ACT.Square).then_inc(sem["kq_sq"], 1)

            def kq_rest(c):
                act.wait_ge(sem["kq_full"], 2 * c + 2)
                act.activation(STAT, STAT, ACT.Sqrt, bias=EPSC[:, 0:1], scale=1.0 / HD).then_inc(sem["kq_sqrt"], 1)
                act.wait_ge(sem["kq_norm"], c + 1)
                if c:
                    act.wait_ge(sem["kq_out"], 16 * c)
                act.activation(KOUT[:, 0, :], KN[:], ACT.Copy).then_inc(sem["kq_hi"], 1)

            def kq(c0, t0, u0):
                for j in range(KT):
                    if j:
                        kq_square(c0 + j - 1, u0 + j - 1)
                    cut_hi(act, Count(t0 + j + AHEAD))
                    if j:
                        kq_rest(c0 + j - 1)
                kq_square(c0 + KT - 1, u0 + KT - 1)
                kq_rest(c0 + KT - 1)

            kq(0, T_K, U_K)
            act.wait_ge(sem["mod_vec"], 9)
            act.wait_ge(sem["acc_full"], U_K + KT)
            modulate(3)
            kq(KT, T_Q, U_Q)

            def sig(h, par, k, first):
                n, b = h * KT + k, STRIPS[k]
                w = (KT - b) * P
                z = flat(PS[:, 2 * (k % 2):2 * (k % 2) + 2, :])[:, 0:w]
                act.wait_ge(sem["z_full"], (n + 1).v)
                if not first:
                    act.wait_ge(sem["at_full"], ((h - 1) * len(GROUP)).v)
                act.activation(A[:, par, STRIP[b]:STRIP[b] + w], z, ACT.Sigmoid, scale=HD ** -0.5
                               ).then_inc(sem["beta_ok"], 1)
                if not (first and par == 0 and k < 2):
                    act.wait_ge(sem["a_ok"], (n - 1).v)
                act.activation(KEEP[:, k % 2, 1:1 + w], z, ACT.Sigmoid, scale=-HD ** -0.5
                               ).then_inc(sem["keep_ok"], 1)

            def at_cut(h, s, first):
                g, j = GROUP[s]
                n = h * len(GROUP) + s
                w = min(j - 4 * g + 1, 4) * P
                act.wait_ge(sem["at_full"], (n + 1).v)
                if not (first and s < 2):
                    act.wait_ge(sem["av_done"], (n - 1).v)
                act.activation(AT_HI[:, s % 2, 0:w], PS[:, 4 + s % 2, 0:w], ACT.Copy).then_inc(sem["at_hi"], 1)

            def o_copy(h, par, g, first):
                n = h * 2 + g
                act.wait_ge(sem["av_done"], (h * len(GROUP) + (8, 12)[g]).v)
                if not (first and g == 0):
                    act.wait_ge(sem["o_lo"], n.v)
                act.activation(OSUM[0:HD, :], PS[HD:P, 6 + g, :], ACT.Copy).then_inc(sem["o_bot"], 1)

            def o_cut(h, par, g, pair):
                n = h * 2 + g
                r = slice(HD * par, HD * par + HD)
                act.wait_ge(sem["o_sum"], (n + 1).v)
                act.activation(OT_HI[r, bass.ds(pair.v, 1), g * HALF:(g + 1) * HALF],
                               OSUM[r, :].unsqueeze(1), ACT.Copy).then_inc(sem["o_hi"], 1)

            def both(h1, p1, h2, p2, pair2, first1, first2):
                for s in range(len(GROUP)):
                    if h2 is not None:
                        at_cut(h2, s, first2)
                        if s == 9:
                            o_copy(h2, p2, 0, first2)
                    if h1 is not None and s in SLOT_OF:
                        sig(h1, p1, SLOT_OF[s], first1)
                    if h2 is not None and s == 10:
                        o_cut(h2, p2, 0, pair2)
                if h2 is not None:
                    o_copy(h2, p2, 1, first2)
                    o_cut(h2, p2, 1, pair2)

            act.wait_ge(sem["acc_full"], U_O)
            both(Count(0), 0, None, 0, None, True, False)
            both(Count(1), 1, Count(0), 0, Count(0), True, True)
            with act.Fori(0, 7) as i:
                both(Count(2, 2, i), 0, Count(1, 2, i), 1, Count(0, 1, i), False, False)
                both(Count(3, 2, i), 1, Count(2, 2, i), 0, Count(1, 1, i), False, False)
            both(None, 0, Count(HEADS - 1), 1, Count(KT - 1), False, False)

            for j in range(KT):
                cut_hi(act, Count(T_O + j + AHEAD))
                if j:
                    square_x(3, j - 1, U_O + j - 1, SQ3)
            square_x(3, KT - 1, U_O + KT - 1, SQ3)
            rms_root(3)
            modulate(4)
            mlp(T_M1, 32, U_M1, None)

        @block.vector
        def _(dve):
            cb = CC[:].unsqueeze(2).to_broadcast([P, 8, P])
            dve.sem_inc(sem["acc_free"], 2)
            dve.wait_ge(sem["small_in"], 80)
            for m in range(MOD_FIRST):
                if m % 2 == 0:
                    dve.wait_ge(sem[f"m0_in{m // 4}"], 16)
                    dve.tensor_tensor(MOD0[:, m], MOD0[:, m], cb, ALU.mult).then_inc(sem["m0_mul_dve"], 1)
                    dve.wait_ge(sem["m0_mul_dve"], m // 2 + 1)
                else:
                    dve.wait_ge(sem["m0_mul_pool"], m // 2 + 1)
                if m >= 2:
                    dve.wait_ge(sem["mod_mm"], m - 1)
                dve.tensor_reduce(MODACC[:, (m % 2) * P:(m % 2 + 1) * P], MOD0[:, m].rearrange("p k c -> p c k"),
                                  AX.X, ALU.add).then_inc(sem["mod_red"], 1)

            vec = [0]

            def mod_vectors(a, b, norms, made):
                dve.wait_ge(sem["mod_mm"], made)
                dve.tensor_tensor(MODV[:, a:b], MODPS[:, a:b], MODB[:, a:b], ALU.add).then_inc(sem["mod_vec"], 1)
                vec[0] += 1
                dve.wait_ge(sem["mod_vec"], vec[0])
                for r in norms:
                    sc = NORMS[r][1]
                    dve.scalar_tensor_tensor(GS[:, KT * r:KT * r + KT], MODV[:, sc:sc + KT], 1.0,
                                             NG[:, KT * r:KT * r + KT], ALU.add, ALU.mult
                                             ).then_inc(sem["mod_vec"], 1)
                    vec[0] += 1

            def sum_squares(s, k):
                dve.wait_ge(sem["sq_done"], 8 * s + k + 1)
                total, sq = (SUMSQ3, SQ3) if s == 3 else (SUMSQ, SQ)
                if k == 0:
                    dve.tensor_copy(total[:], sq[:, 0, :]).then_inc(sem["s_added"], 1)
                else:
                    dve.wait_ge(sem["s_added"], 8 * s + k)
                    dve.tensor_tensor(total[:], total[:], sq[:, k % 2, :], ALU.add).then_inc(sem["s_added"], 1)

            def reciprocals(s):
                for n in range(2):
                    dve.wait_ge(sem["rs_sqrt"], 2 * s + n + 1)
                    dve.reciprocal(RS[:, n * HALF:(n + 1) * HALF], STAT[:, n, :]).then_inc(sem["rs_done"], 1)

            def normalise(r, s):
                def mul(i):
                    n, k = i // 8, i % 8
                    b = 16 * r + i
                    if i % 8 == 0:
                        dve.wait_ge(sem["rs_done"], 2 * s + n + 1)
                    if i >= 2:
                        dve.wait_ge(sem["h_hi"], b - 1)
                    sl = slice(n * HALF, (n + 1) * HALF)
                    dve.tensor_tensor(TT[:, i % 2, :], X[:, k, sl], RS[:, sl], ALU.mult).then_inc(sem["t_mul"], 1)

                mul(0)
                for i in range(16):
                    n, k = i // 8, i % 8
                    if i + 1 < 16:
                        mul(i + 1)
                    dve.wait_ge(sem["h_hi"], 16 * r + i + 1)
                    sl = slice(n * HALF, (n + 1) * HALF)
                    dve.tensor_tensor(H_LO[:, k, sl], HF[:, i % 2, :], H_HI[:, k, sl].bitcast(F32),
                                      ALU.subtract).then_inc(sem["h_lo"], 1)

            mod_vectors(0, MOD_FIRST, (0,), MOD_FIRST)
            for k in range(KT):
                sum_squares(0, k)
            for n in range(AHEAD):
                cut_lo(dve, Count(n))
            reciprocals(0)
            normalise(0, 0)

            def v_pair(i, j, stats):
                n = Count(T_V + 2 * j, 4, i)
                cut_lo(dve, n + AHEAD)
                mod_reduce(dve, n - T_V)
                if not stats:
                    mod_reduce(dve, n - T_V + 1)
                else:
                    for chunk in range(NCHUNK):
                        u = 56 + chunk
                        dve.wait_ge(sem["v_gelu"], u + 3)
                        if chunk:
                            dve.wait_ge(sem["v_ss"], chunk)
                        dve.tensor_tensor_reduce(TRASH[:], V[:, (chunk + 4) % 8, :], V[:, (chunk + 4) % 8, :], 1.0, 0.0,
                                                 ALU.mult, ALU.add, SS[:, chunk:chunk + 1]).then_inc(sem["v_ss"], 1)
                        if chunk == 3:
                            mod_reduce(dve, n - T_V + 1)
                cut_lo(dve, n + AHEAD + 1)
            with dve.Fori(0, 3) as i:
                for j in range(2):
                    v_pair(i, j, False)
            v_pair(None, 6, False)
            v_pair(None, 7, True)
            dve.wait_ge(sem["ws_hi"], 1)
            dve.tensor_tensor(WS_LO[:], WS_RAW[:], WS_HI[:].bitcast(F32), ALU.subtract).then_inc(sem["ws_lo"], 1)
            mod_vectors(MOD_FIRST, MOD_FIRST + 8, (), MOD_FIRST + T_U)
            dve.wait_ge(sem["v_rms"], 1)
            dve.reciprocal(RSTDV[:], RSTDV[:]).then_inc(sem["v_rstd"], 1)
            dve.wait_ge(sem["v_rstd"], 1)

            def sp_scale(u):
                place, half = u // 2, u % 2
                v, r = V[:, place, half * 1024:(half + 1) * 1024], (place + 4) % 8
                dve.scalar_tensor_tensor(v, v, RSTDV[:, r:r + 1], GBC[:, half * 1024:(half + 1) * 1024],
                                         ALU.mult, ALU.mult).then_inc(sem["sp_scaled"], 1)

            dve.wait_ge(sem["vg_in"], 16)
            sp_scale(0)
            for u in range(2 * NCHUNK):
                place, half = u // 2, u % 2
                if u + 1 < 2 * NCHUNK:
                    sp_scale(u + 1)
                dve.wait_ge(sem["sp_hi"], u + 1)
                dve.tensor_tensor(VC_LO[:, u % 2, :], V[:, place, half * 1024:(half + 1) * 1024],
                                  VC_HI[:, u % 2, :].bitcast(F32), ALU.subtract).then_inc(sem["sp_lo"], 1)

            dve.wait_ge(sem["sp_z"], 2 * NCHUNK)
            with dve.Fori(0, 4) as i:
                for j in range(2):
                    n = Count(T_U + 2 * j, 4, i)
                    cut_lo(dve, n + AHEAD)
                    for chunk in range(NCHUNK):
                        u = Count(8 * j + chunk, 16, i)
                        z = V[:, (chunk + 4) % 8, bass.ds(((n - T_U) * P).v, 2 * P)]
                        dve.wait_ge(sem["u_gelu"], (u + 1).v)
                        dve.tensor_tensor(z, acc(u % 2)[:, 0, 0:2 * P], z, ALU.mult).then_inc(sem["acc_free"], 1)
                        if chunk in (2, 5):
                            mod_reduce(dve, n - T_V + (chunk == 5))
                    cut_lo(dve, n + AHEAD + 1)

            def add_x(u, k, gate):
                dve.wait_ge(sem["acc_full"], (u + 1).v)
                dve.wait_ge(sem["acc_free"], freed(u - 1).v)
                dve.scalar_tensor_tensor(X[:, k, :], flat(acc(u % 2)), MODV[:, gate + k:gate + k + 1], X[:, k, :],
                                         ALU.mult, ALU.add).then_inc(sem["acc_free"], 1)

            pending = []

            def sum_squares_late(s, k):
                pending.append((s, k))
                if len(pending) > 1:
                    sum_squares(*pending.pop(0))

            def uz_cut(q, j):
                u = turn_unit(q, j)
                dve.wait_ge(sem["uz_hi"], 4 * q + j + 1)
                dve.tensor_tensor(UZ_LO[q % 2][:, j, :], flat(acc(u % 2)), UZ_HI[q % 2][:, j, :].bitcast(F32),
                                  ALU.subtract).then_inc(sem["acc_free"], 1)

            for j in range(4):
                uz_cut(0, j)
            dve.wait_ge(sem["x_back"], 16)
            for q in range(4):
                for j in range(4):
                    n = Count(T_G + 4 * q + j)
                    cut_lo(dve, n + AHEAD)
                    mod_reduce(dve, n - T_V)
                    for m in range(2):
                        add_x(Count(gate_unit(q, j) + m), 2 * j + m, G1A)
                        if q == 3:
                            sum_squares_late(1, 2 * j + m)
                    if q < 3:
                        uz_cut(q + 1, j)
            sum_squares(*pending.pop(0))
            mod_vectors(MOD_FIRST + 8, MOD_FIRST + 48, (1, 2), MOD_FIRST + T_M0)
            reciprocals(1)
            normalise(1, 1)

            def up(n, hx, u, e, jm):
                for j in range(4):
                    p = acc((u + j) % 2)
                    cut_lo(dve, n + j + AHEAD)
                    if jm is not None:
                        mod_reduce(dve, jm + j)
                    dve.wait_ge(sem["acc_full"], (u + j + 1).v)
                    dve.tensor_scalar(p, p, 0.0, None, ALU.max).then_inc(sem["relu_done"], 1)
                    dve.wait_ge(sem["hid_hi"], ((hx + j) * 2 + 2).v)
                    dve.tensor_tensor(HID_LO[e][:, j, :], flat(p), HID_HI[e][:, j, :].bitcast(F32), ALU.subtract
                                      ).then_inc(sem["acc_free"], 1)

            def down(n, u, gate, jm, stat):
                for j in range(4):
                    if n.i is not None or n.c + j + AHEAD < TILES:
                        cut_lo(dve, n + j + AHEAD)
                    if jm is not None:
                        mod_reduce(dve, jm + j)
                    for m in range(2):
                        k = 2 * j + m
                        add_x(u + k, k, gate)
                        if stat is not None:
                            sum_squares_late(stat, k)

            def mlp(t0, h0, u0, gate, mods, stat):
                up(Count(t0), Count(h0), Count(u0), 0, None)
                with dve.Fori(0, 3) as i:
                    for a in range(2):
                        jm = Count(mods + 8 * a, 16, i) if mods is not None else None
                        up(Count(t0 + 4 + 8 * a, 16, i), Count(h0 + 4 + 4 * a, 8, i),
                           Count(u0 + 4 + 12 * a, 24, i), (a + 1) % 2, jm)
                        down(Count(t0 + 8 + 8 * a, 16, i), Count(u0 + 8 + 12 * a, 24, i),
                             gate, jm + 4 if jm is not None else None, None)
                up(Count(t0 + 52), Count(h0 + 28), Count(u0 + 76), 1, None)
                down(Count(t0 + 56), Count(u0 + 80), gate, None, None)
                down(Count(t0 + 60), Count(u0 + 88), gate, None, stat)
                if stat is not None:
                    sum_squares(*pending.pop(0))

            mlp(T_M0, 0, U_M0, G2A, 48, 2)
            mod_vectors(MOD_FIRST + 48, MODS, (3, 4), MODS)
            reciprocals(2)
            normalise(2, 2)

            for u in range(4 * NCHUNK):
                pair, chunk = divmod(u, NCHUNK)
                if chunk == 0:
                    cut_lo(dve, Count(T_KV_V + 2 * pair + AHEAD))
                src = acc(u % 2)[:, 0, 0:2 * P].rearrange("p (h d) -> p h d", h=4)
                dve.wait_ge(sem["vs_hi"], u + 1)
                dve.tensor_tensor(VST[:, u % 2, :, HD:2 * HD], src, VST[:, u % 2, :, 0:HD].bitcast(F32),
                                  ALU.subtract).then_inc(sem["acc_free"], 1)
                if chunk == NCHUNK - 1:
                    cut_lo(dve, Count(T_KV_V + 2 * pair + AHEAD + 1))

            def kq_copy(c, u):
                dve.wait_ge(sem["acc_full"], u + 1)
                dve.wait_ge(sem["kq_sq"], c + 1)
                dve.tensor_copy(KRAW[:, c % 2, :], flat(acc(u % 2))).then_inc(sem["acc_free"], 1)

            def kq_rest(c, u):
                dve.wait_ge(sem["kq_sqrt"], c + 1)
                if c:
                    dve.wait_ge(sem["kq_lo"], c)
                dve.reciprocal(KN[:], flat(STAT)).then_inc(sem["kq_rec"], 1)
                dve.wait_ge(sem["kq_rec"], c + 1)
                dve.wait_ge(sem["acc_free"], freed(u))
                g = QKG[:, 0:1] if c < KT else QKG[:, 1:2]
                dve.scalar_tensor_tensor(KN[:], KRAW[:, c % 2, :], g, KN[:], ALU.mult, ALU.mult
                                         ).then_inc(sem["kq_norm"], 1)
                dve.wait_ge(sem["kq_hi"], c + 1)
                dve.tensor_tensor(KOUT[:, 1, :], KN[:], KOUT[:, 0, :].bitcast(F32), ALU.subtract
                                  ).then_inc(sem["kq_lo"], 1)

            def kq(c0, t0, u0):
                for j in range(KT):
                    if j:
                        kq_copy(c0 + j - 1, u0 + j - 1)
                    cut_lo(dve, Count(t0 + j + AHEAD))
                    if j:
                        kq_rest(c0 + j - 1, u0 + j - 1)
                kq_copy(c0 + KT - 1, u0 + KT - 1)
                kq_rest(c0 + KT - 1, u0 + KT - 1)

            kq(0, T_K, U_K)
            normalise(3, 2)
            kq(KT, T_Q, U_Q)

            def stick(h, par, k):
                n, b = h * KT + k, STRIPS[k]
                w = (KT - b) * P
                dve.wait_ge(sem["masked"], (n * 2 + 2).v)
                keep = KEEP[:, k % 2, 1:1 + w]
                dve.tensor_tensor_scan(keep, keep, keep, 1.0, ALU.mult, ALU.min).then_inc(sem["scanned"], 1)
                dve.wait_ge(sem["scanned"], (n + 1).v)
                a = A[:, par, STRIP[b]:STRIP[b] + w]
                dve.tensor_tensor(a, a, KEEP[:, k % 2, 0:w], ALU.mult).then_inc(sem["a_ok"], 1)

            def at_cut(h, s):
                g, j = GROUP[s]
                n = h * len(GROUP) + s
                w = min(j - 4 * g + 1, 4) * P
                dve.wait_ge(sem["at_hi"], (n + 1).v)
                dve.tensor_tensor(AT_LO[:, s % 2, 0:w], PS[:, 4 + s % 2, 0:w], AT_HI[:, s % 2, 0:w].bitcast(F32),
                                  ALU.subtract).then_inc(sem["at_lo"], 1)

            def o_add(h, par, g):
                n = h * 2 + g
                r = slice(HD * par, HD * par + HD)
                dve.wait_ge(sem["o_bot"], (n + 1).v)
                dve.tensor_tensor(OSUM[r, :], PS[0:HD, 6 + g, :], OSUM[0:HD, :], ALU.add).then_inc(sem["o_sum"], 1)

            def o_cut(h, par, g, pair):
                n = h * 2 + g
                r = slice(HD * par, HD * par + HD)
                dve.wait_ge(sem["o_hi"], (n + 1).v)
                o = (r, bass.ds(pair.v, 1), slice(g * HALF, (g + 1) * HALF))
                dve.tensor_tensor(OT_LO[o], OSUM[r, :].unsqueeze(1), OT_HI[o].bitcast(F32), ALU.subtract
                                  ).then_inc(sem["o_lo"], 1)

            def both(h1, p1, h2, p2, pair2):
                for s in range(len(GROUP)):
                    if h2 is not None:
                        at_cut(h2, s)
                        if s == 9:
                            o_add(h2, p2, 0)
                    if h1 is not None and s - 1 in SLOT_OF:
                        stick(h1, p1, SLOT_OF[s - 1])
                    if h2 is not None and s == 10:
                        o_cut(h2, p2, 0, pair2)
                if h2 is not None:
                    o_add(h2, p2, 1)
                    o_cut(h2, p2, 1, pair2)

            both(Count(0), 0, None, 0, None)
            both(Count(1), 1, Count(0), 0, Count(0))
            with dve.Fori(0, 7) as i:
                both(Count(2, 2, i), 0, Count(1, 2, i), 1, Count(0, 1, i))
                both(Count(3, 2, i), 1, Count(2, 2, i), 0, Count(1, 1, i))
            both(None, 0, Count(HEADS - 1), 1, Count(KT - 1))

            dve.wait_ge(sem["x_back"], 32)
            for j in range(8):
                cut_lo(dve, Count(T_O + j + AHEAD))
                add_x(Count(U_O + j), j, G1B)
                sum_squares_late(3, j)
            sum_squares(*pending.pop(0))
            reciprocals(3)
            normalise(4, 3)
            mlp(T_M1, 32, U_M1, G2B, None, None)

        @block.tensor
        def _(pe):
            def three(dst, w_hi, w_lo, m_hi, m_lo, first, last):
                pe.matmul(dst, w_hi, m_hi, start=first, stop=False)
                pe.matmul(dst, w_hi, m_lo, start=False, stop=False)
                return pe.matmul(dst, w_lo, m_hi, start=False, stop=last)

            def ones_sum(s):
                pe.wait_ge(sem["s_added"], 8 * s + 8)
                total = SUMSQ3 if s == 3 else SUMSQ
                for n in range(2):
                    pe.matmul(STAT[:, n, :], ONES[:], total[:, n * HALF:(n + 1) * HALF], start=True, stop=True
                              ).then_inc(sem["stat_full"], 1)

            def wide_unit(n, u, m_hi, m_lo, piece=None, between=None):
                s, slot = n % RING, u % 2
                pe.wait_ge(sem["w_lo"], (n + 1).v)
                pe.wait_ge(sem["acc_free"], freed(u - 2).v)
                for half in range(2):
                    sl = slice(half * HALF, (half + 1) * HALF)
                    for k in range(8):
                        if piece is not None:
                            pe.wait_ge(sem["h_lo"], piece + 8 * half + k + 1)
                        mm = three(PS[:, 2 * slot + half, :], W_HI[:, k, s * P:(s + 1) * P],
                                   W_LO[:, k, s * P:(s + 1) * P], m_hi[:, k, sl], m_lo[:, k, sl], k == 0, k == 7)
                    if half == 0 and between is not None:
                        between()
                mm.then_inc(sem["acc_full"], 1)

            def first_units(n, u, piece):
                for half in range(2):
                    sl = slice(half * HALF, (half + 1) * HALF)
                    for t in range(2):
                        s, slot = (n + t) % RING, (u + t) % 2
                        if half == 0:
                            pe.wait_ge(sem["w_lo"], (n + t + 1).v)
                            pe.wait_ge(sem["acc_free"], freed(u + t - 2).v)
                        for k in range(8):
                            if t == 0:
                                pe.wait_ge(sem["h_lo"], piece + 8 * half + k + 1)
                            mm = three(PS[:, 2 * slot + half, :], W_HI[:, k, s * P:(s + 1) * P],
                                       W_LO[:, k, s * P:(s + 1) * P], H_HI[:, k, sl], H_LO[:, k, sl], k == 0, k == 7)
                        if half == 1:
                            mm.then_inc(sem["acc_full"], 1)

            def narrow_units(n, u, m_hi, m_lo, ready=None):
                s = n % RING
                pe.wait_ge(sem["w_lo"], (n + 1).v)
                for m in range(2):
                    slot = (u + m) % 2
                    pe.wait_ge(sem["acc_free"], freed(u + m - 2).v)
                    for half in range(2):
                        sl = slice(half * HALF, (half + 1) * HALF)
                        for k in range(4):
                            if ready is not None and m == 0 and half == 0:
                                ready(k)
                            mm = three(PS[:, 2 * slot + half, :], W_HI[:, 2 * k + m, s * P:(s + 1) * P],
                                       W_LO[:, 2 * k + m, s * P:(s + 1) * P], m_hi[:, k, sl], m_lo[:, k, sl],
                                       k == 0, k == 3)
                    mm.then_inc(sem["acc_full"], 1)

            def token_unit(n, chunk, slot, piece=None):
                s, sl, dst = n % RING, slice(chunk * CHUNK, (chunk + 1) * CHUNK), PS[:, 2 * slot, 0:2 * P]
                for k in range(8):
                    if piece is not None:
                        pe.wait_ge(sem["h_lo"], piece + 8 * (chunk // 4) + k + 1)
                    hi, lo = W_HI[:, k, s * P:(s + 2) * P], W_LO[:, k, s * P:(s + 2) * P]
                    pe.matmul(dst, H_HI[:, k, sl], hi, start=(k == 0), stop=False)
                    pe.matmul(dst, H_LO[:, k, sl], hi, start=False, stop=False)
                    mm = pe.matmul(dst, H_HI[:, k, sl], lo, start=False, stop=(k == 7))
                mm.then_inc(sem["acc_full"], 1)

            pe.wait_ge(sem["consts"], 1)
            for m in range(MOD_FIRST):
                mod_mm(pe, Count(m - MOD_FIRST))
            ones_sum(0)

            with pe.Fori(0, 4) as i:
                for j in range(2):
                    n = Count(T_V + 2 * j, 4, i)
                    pe.wait_ge(sem["w_lo"], (n + 2).v)
                    for chunk in range(NCHUNK):
                        u = Count(8 * j + chunk, 16, i)
                        pe.wait_ge(sem["v_gelu"], (u + 1).v)
                        token_unit(n, chunk, u % 2, 0 if j == 0 and chunk in (0, 4) else None)
                    mod_mm(pe, n - T_V)
                    mod_mm(pe, n - T_V + 1)

            for u in range(2 * NCHUNK):
                half = u % 2
                pe.wait_ge(sem["sp_lo"], u + 1)
                if u < 2:
                    pe.wait_ge(sem["v_gelu"], U_SP + 2)
                    pe.wait_ge(sem["ws_lo"], 1)
                else:
                    pe.wait_ge(sem["sp_z"], u - 1)
                for g in range(4):
                    sl = slice(g * 2 * P, (g + 1) * 2 * P)
                    dst = PS[:, 2 * (u % 2) + g // 2, (g % 2) * 2 * P:(g % 2 + 1) * 2 * P]
                    mm = three(dst, WS_HI[:, 4 * half + g, :], WS_LO[:, 4 * half + g, :], VC_HI[:, u % 2, sl],
                               VC_LO[:, u % 2, sl], True, True)
                mm.then_inc(sem["acc_full"], 1)

            pe.wait_ge(sem["sp_z"], 2 * NCHUNK)
            with pe.Fori(0, 4) as i:
                for j in range(2):
                    n = Count(T_U + 2 * j, 4, i)
                    pe.wait_ge(sem["w_lo"], (n + 2).v)
                    for chunk in range(NCHUNK):
                        u = Count(U_U + 8 * j + chunk, 16, i)
                        pe.wait_ge(sem["acc_free"], freed(u - 2).v)
                        token_unit(n, chunk, u % 2)
                    mod_mm(pe, n - T_V)
                    mod_mm(pe, n - T_V + 1)

            def uz_turn(q, j):
                u = turn_unit(q, j)
                pe.wait_ge(sem["acc_free"], freed(u - 2))
                for chunk in range(NCHUNK):
                    c = (4 * q + j) * P
                    mm = pe.transpose(PS[:, 2 * (u % 2) + chunk // 4, (chunk % 4) * P:(chunk % 4 + 1) * P],
                                      V[:, (chunk + 4) % 8, c:c + P], IDENT[:])
                mm.then_inc(sem["acc_full"], 1)

            pe.wait_ge(sem["acc_free"], freed(U_G - 1))
            pe.wait_ge(sem["ident_ok"], 2)
            for j in range(4):
                uz_turn(0, j)
            for q in range(4):
                for j in range(4):
                    n = Count(T_G + 4 * q + j)
                    narrow_units(n, Count(gate_unit(q, j)), UZ_HI[q % 2], UZ_LO[q % 2],
                                 (lambda k: pe.wait_ge(sem["acc_free"], freed(turn_unit(q, k)))) if j == 0 else None)
                    if q < 3:
                        uz_turn(q + 1, j)
                    mod_mm(pe, n - T_V)
            ones_sum(1)

            def up(n, u, jm, piece=None):
                if piece is not None:
                    first_units(n, u, piece)
                for j in range(2 if piece is not None else 0, 4):
                    wide_unit(n + j, u + j, H_HI, H_LO)
                    if jm is not None:
                        mod_mm(pe, jm + j)

            def down(n, u, e, hid_unit, jm):
                for j in range(4):
                    if j == 0:
                        ready = lambda k: pe.wait_ge(sem["acc_free"], freed(hid_unit + k).v)
                    narrow_units(n + j, u + 2 * j, HID_HI[e], HID_LO[e], ready if j == 0 else None)
                    if jm is not None:
                        mod_mm(pe, jm + j)

            def mlp(t0, u0, mods, piece):
                up(Count(t0), Count(u0), None, piece)
                with pe.Fori(0, 3) as i:
                    for a in range(2):
                        jm = Count(mods + 8 * a, 16, i) if mods is not None else None
                        up(Count(t0 + 4 + 8 * a, 16, i), Count(u0 + 4 + 12 * a, 24, i), jm)
                        before = Count(u0, 24, i) if a == 0 else Count(u0 + 4, 24, i)
                        down(Count(t0 + 8 + 8 * a, 16, i), Count(u0 + 8 + 12 * a, 24, i), a,
                             before, jm + 4 if jm is not None else None)
                up(Count(t0 + 52), Count(u0 + 76), None)
                down(Count(t0 + 56), Count(u0 + 80), 0, Count(u0 + 64), None)
                down(Count(t0 + 60), Count(u0 + 88), 1, Count(u0 + 76), None)

            mlp(T_M0, U_M0, 48, 16)
            ones_sum(2)

            with pe.Fori(0, 2) as i:
                for j in range(2):
                    n = Count(T_KV_V + 2 * j, 4, i)
                    pe.wait_ge(sem["w_lo"], (n + 2).v)
                    for chunk in range(NCHUNK):
                        u = Count(U_KV_V + 8 * j + chunk, 16, i)
                        pe.wait_ge(sem["acc_free"], freed(u - 2).v)
                        token_unit(n, chunk, u % 2, 32 if j == 0 and chunk in (0, 4) else None)

            def head_sums(c):
                pe.wait_ge(sem["kq_sq"], c + 1)
                pe.wait_ge(sem["consts"], 5)
                if c:
                    pe.wait_ge(sem["kq_rec"], c)
                for n in range(2):
                    pe.matmul(STAT[:, n, :], BLK[:], KSQ[:, n * HALF:(n + 1) * HALF], start=True, stop=True
                              ).then_inc(sem["kq_full"], 1)

            def kq(c0, t0, u0, piece):
                for j in range(KT):
                    wide_unit(Count(t0 + j), Count(u0 + j), H_HI, H_LO, piece if j == 0 else None,
                              (lambda: head_sums(c0 + j - 1)) if j else None)
                head_sums(c0 + KT - 1)

            kq(0, T_K, U_K, None)
            kq(KT, T_Q, U_Q, 48)

            def scores(h, par, k, first):
                n, b = h * KT + k, STRIPS[k]
                r = slice(HD * par, HD * par + HD)
                if k == 0:
                    pe.wait_ge(sem[f"qk_in{par}"], ((h // 2) * 16 + 16).v)
                if not (first and par == 0 and k < 2):
                    pe.wait_ge(sem["keep_ok"], (n - 1).v)
                q = QK[r, 0:2, b * P:(b + 1) * P]
                for part in range(1 if b >= 4 else 2):
                    c0, c1 = b * P + part * HALF, min(b * P + (part + 1) * HALF, S)
                    dst = PS[:, 2 * (k % 2) + part, 0:c1 - c0]
                    keys = QK[r, 2:4, c0:c1]
                    mm = three(dst, q[:, 0, :], q[:, 1, :], keys[:, 0, :], keys[:, 1, :], True, True)
                mm.then_inc(sem["z_full"], 1)

            def turn(h, par, s, first):
                g, j = GROUP[s]
                n = h * len(GROUP) + s
                if s == 0:
                    pe.wait_ge(sem["a_ok"], ((h + 1) * KT).v)
                if not (first and s < 2):
                    pe.wait_ge(sem["at_lo"], (n - 1).v)
                blocks = min(j - 4 * g + 1, 4)
                for b in range(blocks):
                    t = 4 * g + b
                    c = STRIP[t] + (j - t) * P
                    mm = pe.transpose(PS[:, 4 + s % 2, b * P:(b + 1) * P], A[:, par, c:c + P], IDENT[:])
                mm.then_inc(sem["at_full"], 1)

            def weigh(h, par, s, first):
                g, j = GROUP[s]
                n = h * len(GROUP) + s
                w = min(j - 4 * g + 1, 4) * P
                if s == 0:
                    pe.wait_ge(sem[f"v_in{par}"], ((h // 2) * 16 + 16).v)
                if j == KT - 1 and not first:
                    pe.wait_ge(sem["o_sum"], (h * 2 + g - 1).v)
                pe.wait_ge(sem["at_lo"], (n + 1).v)
                dst = PS[:, 6 + g, 0:w]
                pe.matmul(dst, VH[:, par, j, :], AT_HI[:, s % 2, 0:w], start=(j == KT - 1), stop=False)
                pe.matmul(dst, VH[:, par, j, :], AT_LO[:, s % 2, 0:w], start=False, stop=(j == 4 * g)
                          ).then_inc(sem["av_done"], 1)

            def both(h1, p1, h2, p2, first1, first2):
                if h2 is not None:
                    turn(h2, p2, 0, first2)
                for s in range(len(GROUP)):
                    if h2 is not None and s + 1 < len(GROUP):
                        turn(h2, p2, s + 1, first2)
                    if h1 is not None and s in SLOT_OF:
                        scores(h1, p1, SLOT_OF[s], first1)
                    if h2 is not None:
                        weigh(h2, p2, s, first2)

            pe.wait_ge(sem["acc_free"], freed(U_O - 1))
            pe.wait_ge(sem["ident_ok"], 3)
            both(Count(0), 0, None, 0, True, False)
            both(Count(1), 1, Count(0), 0, False, True)
            with pe.Fori(0, 7) as i:
                both(Count(2, 2, i), 0, Count(1, 2, i), 1, False, False)
                both(Count(3, 2, i), 1, Count(2, 2, i), 0, False, False)
            both(None, 0, Count(HEADS - 1), 1, False, False)

            pe.wait_ge(sem["o_lo"], 2 * HEADS)
            for j in range(KT):
                wide_unit(Count(T_O + j), Count(U_O + j), OT_HI, OT_LO)
            ones_sum(3)
            mlp(T_M1, U_M1, None, 64)


def tiles_of(w, rows):
    cols = 1024 // rows
    k, n = w.shape
    a = w.reshape(k // (rows * P), rows, P, n // cols, cols)
    return a.transpose(0, 3, 2, 1, 4).reshape(-1, P, 1024)


def column(v):
    return np.ascontiguousarray(v.reshape(-1, P).T)


def mlp_tiles(up, down):
    u = tiles_of(up, 8).reshape(8, 4, P, 1024)
    d = tiles_of(down, 4).reshape(8, 4, P, 1024)
    parts = [u[0]]
    for e in range(7):
        parts += [u[e + 1], d[e]]
    return parts + [d[7]]


def kernel(x, c, mod_w, mod_b, norm_g, mlp_w_up, mlp_w_down, a_w_in, a_v_norm_g, a_w_spatial, a_b_spatial,
           a_w_out, kv_mod_w, kv_mod_b, kv_norm_g, kv_w, k_norm_g, b_w_q, q_norm_g, b_w_out):
    import concourse.bacc as bacc
    from concourse.bass_utils import run_bass_kernel_spmd

    args = [np.asarray(a) for a in (x, c, mod_w, mod_b, norm_g, mlp_w_up, mlp_w_down, a_w_in, a_v_norm_g,
                                    a_w_spatial, a_b_spatial, a_w_out, kv_mod_w, kv_mod_b, kv_norm_g, kv_w,
                                    k_norm_g, b_w_q, q_norm_g, b_w_out)]
    (x, c, mod_w, mod_b, norm_g, mlp_w_up, mlp_w_down, a_w_in, a_v_norm_g, a_w_spatial, a_b_spatial,
     a_w_out, kv_mod_w, kv_mod_b, kv_norm_g, kv_w, k_norm_g, b_w_q, q_norm_g, b_w_out) = args

    stream = [tiles_of(a_w_in[0][:, W:2 * W], 8), tiles_of(a_w_in[0][:, 0:W], 8), tiles_of(a_w_out[0], 4)]
    stream += mlp_tiles(mlp_w_up[0], mlp_w_down[0])
    stream += [tiles_of(kv_w[:, D:2 * D], 8), tiles_of(kv_w[:, 0:D], 8), tiles_of(b_w_q[0], 8),
               tiles_of(b_w_out[0], 8)]
    stream += mlp_tiles(mlp_w_up[1], mlp_w_down[1])

    arrays = {
        "xT": np.ascontiguousarray(x[0, ::-1].T.reshape(KT, P, S).transpose(1, 0, 2)),
        "cT": column(c[0]),
        "wt": np.concatenate(stream),
        "modw": np.concatenate([tiles_of(m, 8) for m in (mod_w[0], kv_mod_w, mod_w[1])]).reshape(MODS, P, 8, P),
        "modb": column(np.concatenate([mod_b[0], kv_mod_b, mod_b[1]])),
        "ng": column(np.concatenate([norm_g[0, 0], norm_g[0, 1], kv_norm_g, norm_g[1, 0], norm_g[1, 1]])),
        "vg": np.ascontiguousarray(np.broadcast_to(a_v_norm_g[0], (P, W))),
        "qkg": np.ascontiguousarray(np.stack([np.concatenate([k_norm_g] * 2), np.concatenate([q_norm_g[0]] * 2)], 1)),
        "spw": np.ascontiguousarray(a_w_spatial[0][:, ::-1, ::-1].transpose(2, 0, 1)),
        "spb": np.ascontiguousarray(a_b_spatial[0][:, ::-1].T),
    }
    nc = bacc.Bacc("TRN2", target_bir_lowering=False, num_devices=1)
    aps = [nc.dram_tensor(f"in_{n}", a.shape, mybir.dt.from_np(a.dtype), kind="ExternalInput").ap()
           for n, a in arrays.items()]
    out = nc.dram_tensor("out_x", (P, KT, S), F32, kind="ExternalOutput").ap()
    build(nc, *aps, out)
    r = run_bass_kernel_spmd(nc, [{f"in_{n}": a for n, a in arrays.items()}], core_ids=[0])
    y = r.results[0]["out_x"]
    return np.ascontiguousarray(y.transpose(1, 0, 2).reshape(D, S).T[::-1])[None]
```

```python
import numpy as np
from contextlib import ExitStack

import concourse.bass as bass
from concourse import mybir

F32 = mybir.dt.float32
F32R = mybir.dt.float32r
ACT = mybir.ActivationFunctionType
ALU = mybir.AluOpType
AX = mybir.AxisListType

P = 128
D = 1024
S = 1024
KT = D // P
HALF = S // 2
W = 2 * D
GROUPS = 8
CHUNK = 128
NCHUNK = S // CHUNK
FF = 4 * D
HEADS = 16
HD = D // HEADS
EPS = 1e-6
RING = 4
AHEAD = 3

T_V = 0
T_U = T_V + W // P
T_G = T_U + W // P
T_M0 = T_G + W // P
T_KV_V = T_M0 + 2 * (FF // P)
T_K = T_KV_V + D // P
T_Q = T_K + D // P
T_O = T_Q + D // P
T_M1 = T_O + D // P
TILES = T_M1 + 2 * (FF // P)

(SH1A, SC1A, G1A, SH2A, SC2A, G2A, SHKV, SCKV, SH1B, SC1B, G1B, SH2B, SC2B, G2B) = range(0, 14 * KT, KT)
MODS = 14 * KT
MOD_FIRST = 2 * KT
MOD_PE = [m for m in range(MOD_FIRST) if m % 3 == 2]
MOD_DVE = [0, MOD_FIRST - 1]
MOD_POOL = [m for m in range(MOD_FIRST) if m not in MOD_PE + MOD_DVE]
NORMS = ((SH1A, SC1A), (SH2A, SC2A), (SHKV, SCKV), (SH1B, SC1B), (SH2B, SC2B))

U_V = 0
U_SP = U_V + W // P // 2 * NCHUNK
U_U = U_SP + 2 * NCHUNK
U_G = U_U + W // P // 2 * NCHUNK
U_M0 = U_G + 4 + 3 * 12 + 8
U_KV_V = U_M0 + 8 * 12
U_K = U_KV_V + 4 * NCHUNK
U_Q = U_K + KT
U_O = U_Q + KT
U_M1 = U_O + KT


def gate_unit(q, j):
    return U_G + 4 + 12 * q + (3 if q < 3 else 2) * j


def turn_unit(q, j):
    return U_G + j if q == 0 else gate_unit(q - 1, j) + 2


def unit_at(t):
    if t < T_U:
        return U_V + (t + 1) // 2 * NCHUNK
    if t < T_G:
        return U_U + (t - T_U + 1) // 2 * NCHUNK
    if t < T_M0:
        return gate_unit(*divmod(t - T_G, 4))
    if t >= T_M1 or t < T_KV_V:
        u0, j = (U_M1, t - T_M1) if t >= T_M1 else (U_M0, t - T_M0)
        if j < 4:
            return u0 + j
        if j >= 60:
            return u0 + 88 + 2 * (j - 60)
        b, j = divmod(j - 4, 8)
        return u0 + 4 + 12 * b + (j if j < 4 else 2 * j - 4)
    if t < T_K:
        return U_KV_V + (t - T_KV_V + 1) // 2 * NCHUNK
    return U_K + t - T_K


def freed(u):
    return u - (U_U - 3)


STRIP = [sum((KT - j) * P for j in range(b)) for b in range(KT + 1)]
STRIPS = [7, 6, 5, 4, 0, 1, 2, 3]
PIECES = [(k, part, min((KT - b) * P - part * HALF, HALF)) for k, b in enumerate(STRIPS)
          for part in range(1 if b >= 4 else 2)]
GROUP = [(g, j) for g in (1, 0) for j in range(KT - 1, 4 * g - 1, -1)]
STEPS = len(GROUP)
POOL_SHARES, DVE_SHARES = [0, 1, 2, 3, 4, 6], [5, 7]
assert len(PIECES) == STEPS


def shared(h, k):
    if k in POOL_SHARES:
        return "a_ok_pool", h * len(POOL_SHARES) + POOL_SHARES.index(k) + 1
    return "a_ok_dve", h * len(DVE_SHARES) + DVE_SHARES.index(k) + 1


class Count:

    def __init__(self, c, s=0, i=None):
        self.c, self.s, self.i = c, (s if i is not None else 0), i

    def __add__(self, n):
        return Count(self.c + n, self.s, self.i)

    def __sub__(self, n):
        return self + (-n)

    def __mul__(self, n):
        return Count(self.c * n, self.s * n, self.i)

    def __floordiv__(self, n):
        assert self.s % n == 0
        return Count(self.c // n, self.s // n, self.i)

    def __mod__(self, n):
        assert self.s % n == 0
        return self.c % n

    @property
    def v(self):
        if self.i is None or self.s == 0:
            return self.c
        return self.i * self.s + self.c


def build(nc, xT, cT, wt, modw, modb, ng, vg, qkg, spw, spb, out):
    with ExitStack() as ctx:
        sem_names = """
            small_in xa_in xb_in
            m0_in0 m0_in1 m0_in2 m0_in3 m0_in4 m0_in5 m0_in6 m0_in7 raw_in0 raw_in1 mod_in spw_in vg_in x_back
            x_spilled vs_out0 vs_out1 kq_out qk_in0 qk_in1 v_in0 v_in1 y_out consts w_hi w_lo
            m0_mul_pool m0_mul_dve mod_mul mod_red mod_mm mod_vec av_done sq_done s_added stat_full
            rs_sqrt rs_done t_mul hf_done h_hi h_lo v_gelu v_sq v_ss v_gain v_rms v_rstd ws_mask ws_hi ws_lo
            sp_hi sp_lo acc_full acc_free u_gelu uz_hi relu_done hid_hi vs_hi kq_sq kq_full
            kq_sqrt kq_rec kq_norm kq_hi kq_lo ident_ok mask_turn z_full keep_ok beta_ok masked_a masked scanned
            a_ok_pool a_ok_dve at_full at_hi at_lo o_bot o_sum o_hi o_lo x_back_hi sp_z sp_zd
        """.split()
        sem = {n: ctx.enter_context(nc.semaphore(n)) for n in sem_names}

        base = -(-nc.sbuf_base // 32) * 32

        def at(name, shape, dt, off):
            return nc.alloc_sbuf_tensor_at(name, shape, dt, offset=base + off)

        KB = 1024
        RX, RB, RH, RR, RW, RC = 0, 32 * KB, 96 * KB, 160 * KB, 192 * KB, 200 * KB
        X = at("X", [P, KT, S], F32, RX)
        H_HI = at("H_HI", [P, KT, S], F32R, RH)
        H_LO = at("H_LO", [P, KT, S], F32R, RH + 32 * KB)
        W_HI = at("W_HI", [P, 8, RING * P], F32R, RR)
        W_LO = at("W_LO", [P, 8, RING * P], F32R, RR + 16 * KB)
        RAW = at("RAW", [P, 2, 1024], F32, RW)
        MODRAW = at("MODRAW", [P, 8, P], F32, RC)
        co = [RC + 4 * KB]

        def small(name, cols):
            t = at(name, [P, cols], F32, co[0])
            co[0] += -(-cols * 4 // 32) * 32
            return t

        MODACC = small("MODACC", 2 * P)
        ONES = small("ONES", P)
        MODV = small("MODV", MODS)
        MODB = small("MODB", MODS)
        NG = small("NG", 5 * KT)
        GS = small("GS", 5 * KT)
        QKG = small("QKG", 2)
        CC = small("CC", KT)
        BS = small("BS", GROUPS)
        IDENT = small("IDENT", P)
        EPSC = small("EPSC", 1)
        ROOT = small("ROOT", 3)
        SS = small("SS", KT)
        RSTDV = small("RSTDV", KT)
        assert co[0] <= 212800, co[0]

        RS = at("RS", [P, S], F32, RB + 12 * KB)
        TT = at("TT", [P, 4, HALF], F32, RB + 4 * KB)
        HF = at("HF", [P, 4, HALF], F32, RB + 16 * KB)
        SUMSQ = at("SUMSQ", [P, S], F32, RB)
        SQ = at("SQ", [P, 2, S], F32, RB + 24 * KB)
        V = at("V", [P, NCHUNK, W], F32, RB)
        UZ_HI = [at(f"UZ_HI{e}", [P, 4, S], F32R, RH + 32 * KB * e) for e in range(2)]
        UZ_LO = [at(f"UZ_LO{e}", [P, 4, S], F32R, RH + 32 * KB * e + 16 * KB) for e in range(2)]
        HID_HI = [at(f"HID_HI{e}", [P, 4, S], F32R, RB + 32 * KB * e) for e in range(2)]
        HID_LO = [at(f"HID_LO{e}", [P, 4, S], F32R, RB + 32 * KB * e + 16 * KB) for e in range(2)]
        MOD0 = at("MOD0", [P, MOD_FIRST, 8, P], F32, RH)
        WS_HI = at("WS_HI", [P, GROUPS, CHUNK], F32R, RX)
        WS_LO = at("WS_LO", [P, GROUPS, CHUNK], F32R, RX + 4 * KB)
        VC_HI = at("VC_HI", [P, 3, W // 2], F32R, RX + 8 * KB)
        VC_LO = at("VC_LO", [P, 3, W // 2], F32R, RX + 20 * KB)
        GBC = at("GBC", [P, W], F32, RX + 24 * KB)
        VSQ = at("VSQ", [P, 2, 2 * P], F32, RX + 8 * KB)
        VSS = at("VSS", [P, NCHUNK, W // P // 2], F32, RX + 10 * KB)
        WS_RAW = at("WS_RAW", [P, GROUPS, CHUNK], F32, RX + 16 * KB)
        KSQ = at("KSQ", [P, S], F32, RB + 32 * KB)
        KRAW = at("KRAW", [P, 2, S], F32, RB + 36 * KB)
        KN = at("KN", [P, S], F32, RB + 44 * KB)
        KOUT = at("KOUT", [P, 2, S], F32R, RB + 48 * KB)
        VST = at("VST", [P, 2, 4, 2 * HD], F32R, RB + 56 * KB)
        BLK = at("BLK", [P, P], F32, RB + 60 * KB)
        QK = at("QK", [P, 4, S], F32R, RX)
        A = at("A", [P, 2, STRIP[KT]], F32, RH)
        KEEP = at("KEEP", [P, 4, S + 8], F32, RH + 36 * KB)
        VH = at("VH", [P, 2, NCHUNK, 2 * HD], F32R, RH + 36 * KB + 4 * (S + 8) * 4)
        AT_HI = at("AT_HI", [P, 3, HALF], F32R, RX + 16 * KB)
        AT_LO = at("AT_LO", [P, 3, HALF], F32R, RX + 22 * KB)
        OSUM = at("OSUM", [P, HALF], F32, RX + 28 * KB)
        SUMSQ3 = at("SUMSQ3", [P, S], F32, RH)
        SQ3 = at("SQ3", [P, 2, S], F32, RH + 4 * KB)
        OT_HI = at("OT_HI", [P, KT, S], F32R, RB)
        OT_LO = at("OT_LO", [P, KT, S], F32R, RB + 32 * KB)

        PS = ctx.enter_context(nc.psum_tensor("PS", [P, 8, HALF], F32))
        STAT = PS[:, 4:6, :]
        MODPS = PS[:, 6, 0:MODS]

        def acc(slot):
            return PS[:, 2 * slot:2 * slot + 2, :]

        def flat(ap):
            return ap.rearrange("p a b -> p (a b)")

        XD = nc.dram_tensor("x_scratch", [P, KT, S], F32).ap()
        VD = nc.dram_tensor("v_scratch", [HEADS, NCHUNK, P, 2 * HD], F32).ap()
        QKD = nc.dram_tensor("qk_scratch", [KT, P, 4, S], F32).ap()

        def raw_view(n):
            return RAW[:, n % 2, :].rearrange("p (k c) -> p k c", k=8)

        def ring_view(t, n):
            s = n % RING
            return t[:, :, s * P:(s + 1) * P]

        def read_before(n):
            a = unit_at(n.c - RING + 1)
            return Count(a, unit_at(n.c + n.s - RING + 1) - a, n.i) if n.i is not None else Count(a)

        def load_raw(sp, n):
            if n.i is not None or n.c >= 2:
                sp.wait_ge(sem["w_lo"], (n - 1).v)
            sp.dma_start(RAW[:, n % 2, :], wt[n.v]).then_inc(sem[f"raw_in{n % 2}"], 16)

        def load_mod(sp, j):
            if j.i is not None or j.c >= 1:
                sp.wait_ge(sem["mod_red"], (j + MOD_FIRST).v)
            sp.dma_start(MODRAW[:], modw[(j + MOD_FIRST).v]).then_inc(sem["mod_in"], 16)

        def cut_hi(act, n):
            act.wait_ge(sem[f"raw_in{n % 2}"], ((n // 2) * 16 + 16).v)
            if n.i is not None or n.c >= RING:
                act.wait_ge(sem["acc_full"], read_before(n).v)
            act.activation(ring_view(W_HI, n), raw_view(n), ACT.Copy).then_inc(sem["w_hi"], 1)

        def cut_lo(dve, n):
            dve.wait_ge(sem["w_hi"], (n + 1).v)
            dve.tensor_tensor(ring_view(W_LO, n), raw_view(n), ring_view(W_HI, n).bitcast(F32),
                              ALU.subtract).then_inc(sem["w_lo"], 1)

        def mod_reduce(dve, j):
            dve.wait_ge(sem["mod_mul"], (j + 1).v)
            dve.wait_ge(sem["mod_mm"], (j + MOD_FIRST - 1).v)
            dve.tensor_reduce(MODACC[:, (j % 2) * P:(j % 2 + 1) * P], MODRAW[:].rearrange("p k c -> p c k"),
                              AX.X, ALU.add).then_inc(sem["mod_red"], 1)

        def mod_mm(pe, j):
            m = j + MOD_FIRST
            pe.wait_ge(sem["mod_red"], (m + 1).v)
            pe.matmul(PS[:, 6, bass.ds(m.v, 1)], MODACC[:, (j % 2) * P:(j % 2 + 1) * P], ONES[:, 0:1],
                      start=True, stop=True).then_inc(sem["mod_mm"], 1)

        block = ctx.enter_context(nc.Block())

        @block.sync
        def _(sp):
            for dst, src in ((CC, cT), (MODB, modb), (NG, ng), (BS, spb), (QKG, qkg)):
                sp.dma_start(dst[:], src).then_inc(sem["small_in"], 16)
            def load_m0(a):
                sp.dma_start(MOD0[:, 2 * a:2 * a + 2, :, :],
                             modw[2 * a:2 * a + 2].rearrange("m p k c -> p m k c")).then_inc(sem[f"m0_in{a}"], 16)
            load_m0(0)
            sp.dma_start(X[:, 0:4, :], xT[:, 0:4, :]).then_inc(sem["xa_in"], 16)
            load_m0(1)
            sp.dma_start(X[:, 4:8, :], xT[:, 4:8, :]).then_inc(sem["xb_in"], 16)
            for a in range(2, 5):
                load_m0(a)
            load_raw(sp, Count(0))
            load_raw(sp, Count(1))
            for a in range(5, 8):
                load_m0(a)
            load_mod(sp, Count(0))
            for n in range(2, 5):
                load_raw(sp, Count(n))
            sp.wait_ge(sem["h_lo"], 16)
            sp.dma_start(WS_RAW[:], spw).then_inc(sem["spw_in"], 16)
            sp.dma_start(GBC[:], vg).then_inc(sem["vg_in"], 16)

            def v_tiles(i, js):
                for j in js:
                    n = Count(T_V + j, 4, i)
                    load_raw(sp, n + 5)
                    load_mod(sp, n - T_V + 1)
            with sp.Fori(0, 4) as i:
                v_tiles(i, range(4))

            sp.wait_ge(sem["sp_z"], 2 * NCHUNK)
            sp.wait_ge(sem["sp_zd"], 2 * NCHUNK)
            sp.dma_start(X[:], xT).then_inc(sem["x_back"], 16)

            with sp.Fori(0, 4) as i:
                v_tiles(i, range(T_U, T_U + 4))

            def m_tiles(first, stop, ld_mod, i=None, step=0, t_end=TILES):
                for t in range(first, stop):
                    n = Count(t, step, i)
                    if i is not None or t + 5 < t_end:
                        load_raw(sp, n + 5)
                    if ld_mod is not None:
                        j = n - ld_mod + 1
                        load_mod(sp, j)

            m_tiles(T_G, T_M0, T_V)
            m_tiles(T_M0, T_M0 + 4, None)
            with sp.Fori(0, 2) as i:
                m_tiles(T_M0 + 4, T_M0 + 20, T_V + 4, i, 16)
            m_tiles(T_M0 + 36, T_M0 + 51, T_V + 4)
            m_tiles(T_M0 + 51, T_M0 + 64, None)

            sp.wait_ge(sem["acc_free"], freed(U_M0 + 95))
            sp.dma_start(XD[:], X[:]).then_inc(sem["x_spilled"], 16)

            for u in range(4 * NCHUNK):
                pair, chunk = divmod(u, NCHUNK)
                if chunk in (1, 7):
                    load_raw(sp, Count(T_KV_V + 2 * pair + (chunk == 7) + 5))
                sp.wait_ge(sem["acc_free"], freed(U_KV_V + u))
                sp.dma_start(VD[4 * pair:4 * pair + 4, chunk].rearrange("h p d -> p h d"),
                             VST[:, chunk % 2, :, :].bitcast(F32)).then_inc(sem[f"vs_out{chunk % 2}"], 16)

            def load_v(h, par):
                sp.dma_start(VH[:, par, :, :].bitcast(F32), VD[h.v].rearrange("c p d -> p c d")
                             ).then_inc(sem[f"v_in{par}"], 16)

            for kind, t0, c0 in ((1, T_K, 0), (0, T_Q, KT)):
                for j in range(KT):
                    load_raw(sp, Count(t0 + j + 5))
                    if c0 + j == 2 * KT - 1:
                        for b in range(2):
                            sp.wait_ge(sem[f"vs_out{b}"], 16 * 2 * NCHUNK)
                        sp.wait_ge(sem["acc_full"], U_O)
                        for par in range(2):
                            load_v(Count(par), par)
                    sp.wait_ge(sem["kq_lo"], c0 + j + 1)
                    sp.dma_start(QKD[j, :, 2 * kind:2 * kind + 2, :], KOUT[:].bitcast(F32)).then_inc(sem["kq_out"], 16)
                    if kind == 0 and j == 1:
                        sp.wait_ge(sem["kq_out"], 16 * (KT + 1))
                        sp.wait_ge(sem["x_spilled"], 16)
                        sp.wait_ge(sem["t_mul"], 16 * 4)
                        for par in range(2):
                            sp.dma_start(QK[64 * par:64 * par + 64, :, :].bitcast(F32),
                                         QKD[0, 64 * par:64 * par + 64]).then_inc(sem[f"qk_in{par}"], 16)

            sp.wait_ge(sem["kq_out"], 16 * 2 * KT)
            with sp.Fori(0, 7) as i:
                for par in range(2):
                    h = Count(par, 2, i)
                    sp.wait_ge(sem["z_full"], ((h + 1) * STEPS).v)
                    sp.dma_start(QK[64 * par:64 * par + 64, :, :].bitcast(F32),
                                 QKD[Count(1, 1, i).v, 64 * par:64 * par + 64]
                                 ).then_inc(sem[f"qk_in{par}"], 16)
                    sp.wait_ge(sem["av_done"], ((h + 1) * STEPS).v)
                    load_v(h + 2, par)
            sp.wait_ge(sem["z_full"], HEADS * STEPS)
            sp.dma_start(X[:, 0:4, :], XD[:, 0:4, :]).then_inc(sem["x_back"], 16)
            sp.wait_ge(sem["av_done"], HEADS * STEPS)
            sp.wait_ge(sem["o_lo"], 2 * HEADS)
            sp.dma_start(X[:, 4:8, :], XD[:, 4:8, :]).then_inc(sem["x_back_hi"], 16)

            for t in range(T_O, T_O + 8):
                load_raw(sp, Count(t + 5))
            m_tiles(T_M1, T_M1 + 4, None)
            with sp.Fori(0, 3) as i:
                m_tiles(T_M1 + 4, T_M1 + 20, None, i, 16)
            m_tiles(T_M1 + 52, T_M1 + 64, None)
            for k in range(KT):
                sp.wait_ge(sem["acc_free"], freed(U_M1 + 88 + k))
                sp.dma_start(out[:, k, :], X[:, k, :]).then_inc(sem["y_out"], 16)
            sp.wait_ge(sem["y_out"], 16 * KT)

        @block.gpsimd
        def _(pool):
            pool.memset(ONES[:], 1.0).then_inc(sem["consts"], 1)
            pool.memset(EPSC[:], EPS).then_inc(sem["consts"], 1)
            pool.memset(IDENT[:], 0.0).then_inc(sem["ident_ok"], 1)
            pool.wait_ge(sem["ident_ok"], 1)
            pool.affine_select(out=IDENT[:], in_=IDENT[:], compare_op=ALU.not_equal, fill=1.0, base=0,
                               pattern=[[-1, P]], channel_multiplier=1).then_inc(sem["ident_ok"], 1)
            cb = CC[:].unsqueeze(2).to_broadcast([P, 8, P])
            pool.wait_ge(sem["small_in"], 80)
            for m in MOD_POOL:
                pool.wait_ge(sem[f"m0_in{m // 2}"], 16)
                pool.tensor_tensor(MOD0[:, m], MOD0[:, m], cb, ALU.mult).then_inc(sem["m0_mul_pool"], 1)
            def mod_products(first, stop):
                with pool.Fori(first, stop) as i:
                    j = Count(0, 1, i)
                    pool.wait_ge(sem["mod_in"], ((j + 1) * 16).v)
                    pool.tensor_tensor(MODRAW[:], MODRAW[:], cb, ALU.mult).then_inc(sem["mod_mul"], 1)

            def scale_x(r, s):
                for i in range(16):
                    n, k, b = i // 8, i % 8, 16 * r + i
                    if k == 0:
                        pool.wait_ge(sem["rs_done"], 4 * s + 2 * n + 2)
                    if b >= 4:
                        pool.wait_ge(sem["h_hi"], b - 3)
                        pool.wait_ge(sem["hf_done"], b - 3)
                    sl = slice(n * HALF, (n + 1) * HALF)
                    pool.tensor_tensor(TT[:, i % 4, :], X[:, k, sl], RS[:, sl], ALU.mult).then_inc(sem["t_mul"], 1)

            scale_x(0, 0)
            pool.wait_ge(sem["spw_in"], 16)
            pool.affine_select(out=WS_RAW[:], in_=WS_RAW[:], compare_op=ALU.is_ge, fill=0.0, base=0,
                               pattern=[[0, GROUPS], [-1, CHUNK]], channel_multiplier=1).then_inc(sem["ws_mask"], 1)
            mod_products(0, T_M0)
            scale_x(1, 1)
            mod_products(T_M0, MODS - MOD_FIRST)
            pool.wait_ge(sem["acc_free"], freed(U_M0 + 95))
            pool.memset(BLK[:], 0.0).then_inc(sem["consts"], 1)
            pool.wait_ge(sem["consts"], 3)
            pool.memset(BLK[0:HD, 0:HD], 1.0).then_inc(sem["consts"], 1)
            pool.memset(BLK[HD:P, HD:P], 1.0).then_inc(sem["consts"], 1)
            pool.wait_ge(sem["consts"], 5)
            scale_x(2, 2)
            scale_x(3, 2)
            pool.wait_ge(sem["acc_full"], U_O)
            pool.memset(KEEP[:, :, 0:1], 1.0).then_inc(sem["ident_ok"], 1)

            def mask(h, par, k):
                n, b = h * KT + k, STRIPS[k]
                last = next(i for i, piece in enumerate(PIECES) if piece[0] == k)
                pool.wait_ge(sem["keep_ok"], (h * STEPS + last + 1).v)
                pool.sem_inc(sem["mask_turn"], 1)
                a = A[:, par, STRIP[b]:STRIP[b] + P]
                pool.affine_select(out=a, in_=a, compare_op=ALU.is_gt, fill=0.0, base=0,
                                   pattern=[[1, P]], channel_multiplier=-1).then_inc(sem["masked_a"], 1)
                keep = KEEP[:, k % 4, 1:1 + P]
                pool.affine_select(out=keep, in_=keep, compare_op=ALU.is_gt, fill=1.0, base=0,
                                   pattern=[[1, P]], channel_multiplier=-1).then_inc(sem["masked"], 1)

            def share(h, par, k):
                n, b = h * KT + k, STRIPS[k]
                w = (KT - b) * P
                pool.wait_ge(sem["scanned"], (n + 1).v)
                pool.wait_ge(sem["masked_a"], (n + 1).v)
                a = A[:, par, STRIP[b]:STRIP[b] + w]
                pool.tensor_tensor(a, a, KEEP[:, k % 4, 0:w], ALU.mult).then_inc(sem["a_ok_pool"], 1)

            def head(h, par):
                for k in range(KT):
                    mask(h, par, k)
                    if k - 1 in POOL_SHARES:
                        share(h, par, k - 1)

            for par in range(2):
                head(Count(par), par)
            with pool.Fori(0, HEADS // 2 - 1) as i:
                for par in range(2):
                    head(Count(2 + par, 2, i), par)
            scale_x(4, 3)

        @block.scalar
        def _(act):
            act.sem_inc(sem["v_gelu"], 2)
            act.wait_ge(sem["consts"], 2)

            def square_x(s, k, u, sq=SQ):
                act.wait_ge(sem["acc_free"], freed(u))
                if k >= 2:
                    act.wait_ge(sem["s_added"], 8 * s + k - 2)
                act.activation(sq[:, k % 2, :], X[:, k, :], ACT.Square).then_inc(sem["sq_done"], 1)

            def load_root(i):
                act.activation(ROOT[:, i:i + 1], EPSC[:, 0:1], ACT.Sqrt)

            def rms_root(s):
                for n in range(2):
                    act.wait_ge(sem["stat_full"], 2 * s + n + 1)
                    act.activation(STAT[:, n, :], STAT[:, n, :], ACT.Sqrt, bias=EPSC[:, 0:1], scale=1.0 / D
                                   ).then_inc(sem["rs_sqrt"], 1)

            def modulate(r):
                sh, _ = NORMS[r]
                for i in range(16):
                    n, k, b = i // 8, i % 8, 16 * r + i
                    g, s0 = GS[:, KT * r + k:KT * r + k + 1], MODV[:, sh + k:sh + k + 1]
                    act.wait_ge(sem["t_mul"], b + 1)
                    act.activation(H_HI[:, k, n * HALF:(n + 1) * HALF], TT[:, i % 4, :], ACT.Identity,
                                   bias=s0, scale=g).then_inc(sem["h_hi"], 1)

            for k in range(KT):
                act.wait_ge(sem["xa_in" if k < 4 else "xb_in"], 16)
                if k >= 2:
                    act.wait_ge(sem["s_added"], k - 1)
                act.activation(SQ[:, k % 2, :], X[:, k, :], ACT.Square).then_inc(sem["sq_done"], 1)
            rms_root(0)
            for n in range(AHEAD):
                cut_hi(act, Count(n))
            act.wait_ge(sem["mod_vec"], 2)
            modulate(0)

            def v_pair(i, j):
                n = Count(T_V + 2 * j, 4, i)
                cut_hi(act, n + AHEAD)
                for chunk in range(NCHUNK):
                    u = Count(8 * j + chunk, 16, i)
                    act.wait_ge(sem["acc_full"], (u + U_V + 1).v)
                    if chunk == 4:
                        act.wait_ge(sem["h_lo"], 16)
                    act.activation(V[:, (chunk + 4) % 8, bass.ds((n * P).v, 2 * P)], acc(u % 2)[:, 0, 0:2 * P],
                                   ACT.Gelu).then_inc(sem["v_gelu"], 1)
                cut_hi(act, n + AHEAD + 1)
            with act.Fori(0, 4) as i:
                for j in range(2):
                    v_pair(i, j)

            act.wait_ge(sem["ws_mask"], 1)
            act.activation(WS_HI[:], WS_RAW[:], ACT.Copy).then_inc(sem["ws_hi"], 1)

            act.wait_ge(sem["v_ss"], 8 * NCHUNK + 1)
            act.activation(RSTDV[:], SS[:], ACT.Sqrt, bias=EPSC[:, 0:1], scale=1.0 / W).then_inc(sem["v_rms"], 1)

            act.wait_ge(sem["v_rstd"], 1)
            act.wait_ge(sem["v_gain"], 8 * NCHUNK)
            act.wait_ge(sem["ws_lo"], 1)
            def sp_cut(u):
                place, half = u // 2, u % 2
                r = (place + 4) % 8
                if u >= 3:
                    act.wait_ge(sem["acc_full"], U_SP + u - 2)
                act.activation(VC_HI[:, u % 3, :], V[:, place, half * 1024:(half + 1) * 1024], ACT.Identity,
                               scale=RSTDV[:, r:r + 1]).then_inc(sem["sp_hi"], 1)

            sp_cut(0)
            sp_cut(1)
            for u in range(2 * NCHUNK):
                place, half = u // 2, u % 2
                if u + 2 < 2 * NCHUNK:
                    sp_cut(u + 2)
                act.wait_ge(sem["acc_full"], U_SP + u + 1)
                act.wait_ge(sem["sp_lo"], u + 1)
                for g in range(2):
                    c0 = half * 1024 + g * 2 * P
                    z = act.activation(V[:, place, c0:c0 + 2 * P],
                                       acc(u % 2)[:, 0, g * 2 * P:(g + 1) * 2 * P],
                                       ACT.Identity, bias=BS[:, 4 * half + g:4 * half + g + 1])
                z.then_inc(sem["sp_z"], 1)

            with act.Fori(0, 4) as i:
                for j in range(2):
                    n = Count(T_U + 2 * j, 4, i)
                    cut_hi(act, n + AHEAD)
                    for chunk in range(NCHUNK):
                        u = Count(U_U + 8 * j + chunk, 16, i)
                        act.wait_ge(sem["acc_full"], (u + 1).v)
                        p = acc(u % 2)[:, 0, 0:2 * P]
                        act.activation(p, p, ACT.Gelu).then_inc(sem["u_gelu"], 1)
                    cut_hi(act, n + AHEAD + 1)

            def uz_cut(q, j):
                u = turn_unit(q, j)
                act.wait_ge(sem["acc_full"], u + 1)
                act.activation(UZ_HI[q % 2][:, j, :], flat(acc(u % 2)), ACT.Copy).then_inc(sem["uz_hi"], 1)

            for j in range(4):
                uz_cut(0, j)
            for q in range(4):
                for j in range(4):
                    cut_hi(act, Count(T_G + 4 * q + j + AHEAD))
                    if q < 3:
                        uz_cut(q + 1, j)
                    elif j:
                        for k in (2 * j - 2, 2 * j - 1):
                            square_x(1, k, gate_unit(3, 0) + k)
            load_root(0)
            for k in (KT - 2, KT - 1):
                square_x(1, k, gate_unit(3, 0) + k)
            rms_root(1)
            act.wait_ge(sem["mod_vec"], 6)
            modulate(1)

            def up(n, hx, u, e, cut):
                for j in range(4):
                    if cut:
                        cut_hi(act, n + j + AHEAD)
                    act.wait_ge(sem["relu_done"], (hx + j + 1).v)
                    p = acc((u + j) % 2)
                    act.activation(HID_HI[e][:, j, :], flat(p), ACT.Square).then_inc(sem["hid_hi"], 1)
                    act.activation(p, p, ACT.Square).then_inc(sem["hid_hi"], 1)

            def down(n, stat=None, u=0):
                for j in range(4):
                    if n.i is not None or n.c + j + AHEAD < TILES:
                        cut_hi(act, n + j + AHEAD)
                    if stat is not None and j:
                        square_x(stat, 2 * j - 2, u + 2 * j - 2)
                        square_x(stat, 2 * j - 1, u + 2 * j - 1)

            def mlp(t0, h0, u0, stat):
                up(Count(t0), Count(h0), Count(u0), 0, True)
                with act.Fori(0, 3) as i:
                    for a in range(2):
                        up(Count(t0 + 4 + 8 * a, 16, i), Count(h0 + 4 + 4 * a, 8, i),
                           Count(u0 + 4 + 12 * a, 24, i), (a + 1) % 2, True)
                        down(Count(t0 + 8 + 8 * a, 16, i))
                up(Count(t0 + 52), Count(h0 + 28), Count(u0 + 76), 1, True)
                down(Count(t0 + 56))
                down(Count(t0 + 60), stat, u0 + 88)

            mlp(T_M0, 0, U_M0, 2)
            load_root(1)
            for k in (KT - 2, KT - 1):
                square_x(2, k, U_M0 + 88 + k)
            rms_root(2)
            act.wait_ge(sem["mod_vec"], 6)
            modulate(2)

            for u in range(4 * NCHUNK):
                pair, chunk = divmod(u, NCHUNK)
                if chunk == 0:
                    cut_hi(act, Count(T_KV_V + 2 * pair + AHEAD))
                act.wait_ge(sem["acc_full"], U_KV_V + u + 1)
                if u >= 2:
                    act.wait_ge(sem[f"vs_out{u % 2}"], 16 * (u // 2))
                src = acc(u % 2)[:, 0, 0:2 * P].rearrange("p (h d) -> p h d", h=4)
                act.activation(VST[:, u % 2, :, 0:HD], src, ACT.Copy).then_inc(sem["vs_hi"], 1)
                if chunk == NCHUNK - 1:
                    cut_hi(act, Count(T_KV_V + 2 * pair + AHEAD + 1))

            def kq_square(c, u):
                act.wait_ge(sem["acc_full"], u + 1)
                if c:
                    act.wait_ge(sem["kq_full"], 2 * c)
                act.activation(KSQ[:], flat(acc(u % 2)), ACT.Square).then_inc(sem["kq_sq"], 1)

            def kq_root(c):
                act.wait_ge(sem["kq_full"], 2 * c + 2)
                act.activation(STAT, STAT, ACT.Sqrt, bias=EPSC[:, 0:1], scale=1.0 / HD).then_inc(sem["kq_sqrt"], 1)

            def kq_hi(c):
                act.wait_ge(sem["kq_norm"], c + 1)
                if c:
                    act.wait_ge(sem["kq_out"], 16 * c)
                act.activation(KOUT[:, 0, :], KN[:], ACT.Copy).then_inc(sem["kq_hi"], 1)

            def kq(c0, t0, u0):
                for j in range(KT):
                    if j:
                        kq_square(c0 + j - 1, u0 + j - 1)
                    cut_hi(act, Count(t0 + j + AHEAD))
                    if c0 + j:
                        kq_root(c0 + j - 1)
                        kq_hi(c0 + j - 1)
                kq_square(c0 + KT - 1, u0 + KT - 1)

            kq(0, T_K, U_K)
            act.wait_ge(sem["mod_vec"], 9)
            act.wait_ge(sem["acc_full"], U_K + KT)
            modulate(3)
            kq(KT, T_Q, U_Q)
            kq_root(2 * KT - 1)

            def sig(h, par, s, first):
                k, part, w = PIECES[s]
                n, b = h * STEPS + s, STRIPS[k]
                z = PS[:, s % 3, 0:w]
                act.wait_ge(sem["z_full"], (n + 1).v)
                if not first:
                    act.wait_ge(sem["at_full"], ((h - 1) * STEPS).v)
                c = STRIP[b] + part * HALF
                act.activation(A[:, par, c:c + w], z, ACT.Sigmoid, scale=HD ** -0.5).then_inc(sem["beta_ok"], 1)
                if not (first and par == 0 and k < 4):
                    made, n = shared(h, k - 4) if k >= 4 else shared(h - 1, k + 4)
                    act.wait_ge(sem[made], n.v)
                c = 1 + part * HALF
                act.activation(KEEP[:, k % 4, c:c + w], z, ACT.Sigmoid, scale=-HD ** -0.5
                               ).then_inc(sem["keep_ok"], 1)

            def at_cut(h, s, first):
                g, j = GROUP[s]
                n = h * STEPS + s
                w = min(j - 4 * g + 1, 4) * P
                act.wait_ge(sem["at_full"], (n + 1).v)
                if not (first and s < 3):
                    act.wait_ge(sem["av_done"], (n - 2).v)
                act.activation(AT_HI[:, s % 3, 0:w], PS[:, 3 + s % 3, 0:w], ACT.Copy).then_inc(sem["at_hi"], 1)

            def o_copy(h, par, g, first):
                n = h * 2 + (1 - g)
                act.wait_ge(sem["av_done"], (h * STEPS + (STEPS, 4)[g]).v)
                if not (first and g == 1):
                    act.wait_ge(sem["o_lo"], n.v)
                act.activation(OSUM[0:HD, :], PS[HD:P, 6 + g, :], ACT.Copy).then_inc(sem["o_bot"], 1)

            def o_cut(h, par, g, pair):
                n = h * 2 + (1 - g)
                r = slice(HD * par, HD * par + HD)
                act.wait_ge(sem["o_sum"], (n + 1).v)
                act.activation(OT_HI[r, bass.ds(pair.v, 1), g * HALF:(g + 1) * HALF],
                               OSUM[r, :].unsqueeze(1), ACT.Copy).then_inc(sem["o_hi"], 1)

            def both(h1, p1, h2, p2, pair2, pair0, first1, first2):
                for s in range(STEPS):
                    if s < STEPS - 2 and h2 is not None:
                        at_cut(h2, s + 2, first2)
                    elif s >= STEPS - 2 and h1 is not None:
                        at_cut(h1, s + 2 - STEPS, h2 is None)
                    if pair0 is not None and s == 1:
                        o_copy(h2 - 1, 1 - p2, 0, False)
                    if pair0 is not None and s == 2:
                        o_cut(h2 - 1, 1 - p2, 0, pair0)
                    if h2 is not None and s == 5:
                        o_copy(h2, p2, 1, first2)
                    if h2 is not None and s == 6:
                        o_cut(h2, p2, 1, pair2)
                    if h1 is not None:
                        sig(h1, p1, s, first1)
                    if h2 is None and s == 9:
                        kq_hi(2 * KT - 1)

            act.wait_ge(sem["acc_full"], U_O)
            both(Count(0), 0, None, 0, None, None, True, False)
            both(Count(1), 1, Count(0), 0, Count(0), None, True, True)
            with act.Fori(0, 7) as i:
                both(Count(2, 2, i), 0, Count(1, 2, i), 1, Count(0, 1, i), Count(0, 1, i), False, False)
                both(Count(3, 2, i), 1, Count(2, 2, i), 0, Count(1, 1, i), Count(0, 1, i), False, False)
            both(None, 0, Count(HEADS - 1), 1, Count(KT - 1), Count(KT - 1), False, False)
            o_copy(Count(HEADS - 1), 1, 0, False)
            o_cut(Count(HEADS - 1), 1, 0, Count(KT - 1))

            for j in range(KT):
                cut_hi(act, Count(T_O + j + AHEAD))
                if j:
                    square_x(3, j - 1, U_O + j - 1, SQ3)
            load_root(2)
            square_x(3, KT - 1, U_O + KT - 1, SQ3)
            rms_root(3)
            modulate(4)
            mlp(T_M1, 32, U_M1, None)

        @block.vector
        def _(dve):
            cb = CC[:].unsqueeze(2).to_broadcast([P, 8, P])
            dve.sem_inc(sem["acc_free"], 2)
            def reciprocal(s, q):
                dve.wait_ge(sem["rs_sqrt"], 2 * s + q // 2 + 1)
                c = (q % 2) * (HALF // 2)
                dve.reciprocal(RS[:, q * (HALF // 2):(q + 1) * (HALF // 2)], STAT[:, q // 2, c:c + HALF // 2]
                               ).then_inc(sem["rs_done"], 1)

            dve.wait_ge(sem["small_in"], 80)
            for m in range(MOD_FIRST):
                if m in (8, 9, 10, 11):
                    reciprocal(0, m - 8)
                if m in (12, 13):
                    cut_lo(dve, Count(m - 12))
                if m in MOD_PE:
                    continue
                if m in MOD_DVE:
                    dve.wait_ge(sem[f"m0_in{m // 2}"], 16)
                    dve.tensor_tensor(MOD0[:, m], MOD0[:, m], cb, ALU.mult).then_inc(sem["m0_mul_dve"], 1)
                    dve.wait_ge(sem["m0_mul_dve"], MOD_DVE.index(m) + 1)
                else:
                    dve.wait_ge(sem["m0_mul_pool"], MOD_POOL.index(m) + 1)
                if m >= 2:
                    dve.wait_ge(sem["mod_mm"], m - 1)
                dve.tensor_reduce(MODACC[:, (m % 2) * P:(m % 2 + 1) * P], MOD0[:, m].rearrange("p k c -> p c k"),
                                  AX.X, ALU.add).then_inc(sem["mod_red"], 2 if m + 1 in MOD_PE else 1)

            vec = [0]

            def mod_vectors(a, b, norms, made):
                dve.wait_ge(sem["mod_mm"], made)
                dve.tensor_tensor(MODV[:, a:b], MODPS[:, a:b], MODB[:, a:b], ALU.add).then_inc(sem["mod_vec"], 1)
                vec[0] += 1
                dve.wait_ge(sem["mod_vec"], vec[0])
                for r in norms:
                    sc = NORMS[r][1]
                    dve.scalar_tensor_tensor(GS[:, KT * r:KT * r + KT], MODV[:, sc:sc + KT], 1.0,
                                             NG[:, KT * r:KT * r + KT], ALU.add, ALU.mult
                                             ).then_inc(sem["mod_vec"], 1)
                    vec[0] += 1

            def sum_squares(s, k):
                dve.wait_ge(sem["sq_done"], 8 * s + k + 1)
                total, sq = (SUMSQ3, SQ3) if s == 3 else (SUMSQ, SQ)
                if k == 0:
                    dve.tensor_copy(total[:], sq[:, 0, :]).then_inc(sem["s_added"], 1)
                else:
                    dve.wait_ge(sem["s_added"], 8 * s + k - 1)
                    dve.tensor_tensor(total[:], total[:], sq[:, k % 2, :], ALU.add).then_inc(sem["s_added"], 1)

            def normalise(r, s, quarters):
                sh, _ = NORMS[r]
                for q in quarters[:2]:
                    reciprocal(s, q)
                dve.wait_ge(sem["mod_vec"], vec[0])

                def full(i):
                    k, b = i % 8, 16 * r + i
                    dve.wait_ge(sem["t_mul"], b + 1)
                    if b >= 4:
                        dve.wait_ge(sem["h_lo"], b - 3)
                    dve.tensor_scalar(HF[:, i % 4, :], TT[:, i % 4, :], GS[:, KT * r + k:KT * r + k + 1],
                                      MODV[:, sh + k:sh + k + 1], ALU.mult, ALU.add).then_inc(sem["hf_done"], 1)

                full(0)
                for i in range(16):
                    n, k, b = i // 8, i % 8, 16 * r + i
                    if i in (2, 4) and quarters:
                        reciprocal(s, quarters[1 + i // 2])
                    if i + 1 < 16:
                        full(i + 1)
                    dve.wait_ge(sem["h_hi"], b + 1)
                    dve.wait_ge(sem["hf_done"], b + 1)
                    sl = slice(n * HALF, (n + 1) * HALF)
                    dve.tensor_tensor(H_LO[:, k, sl], HF[:, i % 4, :], H_HI[:, k, sl].bitcast(F32),
                                      ALU.subtract).then_inc(sem["h_lo"], 1)

            mod_vectors(0, MOD_FIRST, (0,), MOD_FIRST)
            cut_lo(dve, Count(2))
            normalise(0, 0, ())

            dve.wait_ge(sem["vg_in"], 16)
            with dve.Fori(0, 4) as i:
                for j in range(2):
                    n = Count(T_V + 2 * j, 4, i)
                    cut_lo(dve, n + AHEAD)
                    for chunk in range(NCHUNK):
                        u = Count(8 * j + chunk, 16, i)
                        cols = bass.ds((n * P).v, 2 * P)
                        v, sq = V[:, (chunk + 4) % 8, cols], VSQ[:, chunk % 2, :]
                        dve.wait_ge(sem["v_gelu"], (u + 3).v)
                        dve.tensor_tensor(sq, v, v, ALU.mult).then_inc(sem["v_sq"], 1)
                        dve.wait_ge(sem["v_sq"], (u + 1).v)
                        dve.tensor_tensor(v, v, GBC[:, cols], ALU.mult).then_inc(sem["v_gain"], 1)
                        dve.tensor_reduce(VSS[:, chunk, bass.ds(Count(j, 2, i).v, 1)], sq, AX.X, ALU.add
                                          ).then_inc(sem["v_ss"], 1)
                        if chunk in (2, 5):
                            mod_reduce(dve, n - T_V + (chunk == 5))
                    cut_lo(dve, n + AHEAD + 1)
            dve.wait_ge(sem["v_gain"], 8 * NCHUNK)
            dve.wait_ge(sem["v_ss"], 8 * NCHUNK)
            dve.tensor_reduce(SS[:], VSS[:], AX.X, ALU.add).then_inc(sem["v_ss"], 1)
            dve.wait_ge(sem["ws_hi"], 1)
            dve.tensor_tensor(WS_LO[:], WS_RAW[:], WS_HI[:].bitcast(F32), ALU.subtract).then_inc(sem["ws_lo"], 1)
            mod_vectors(MOD_FIRST, MOD_FIRST + 8, (), MOD_FIRST + T_U)
            dve.wait_ge(sem["v_rms"], 1)
            dve.reciprocal(RSTDV[:], RSTDV[:]).then_inc(sem["v_rstd"], 1)
            dve.wait_ge(sem["v_rstd"], 1)

            def sp_cut(u):
                place, half = u // 2, u % 2
                v, r = V[:, place, half * 1024:(half + 1) * 1024], (place + 4) % 8
                dve.wait_ge(sem["sp_hi"], u + 1)
                dve.scalar_tensor_tensor(VC_LO[:, u % 3, :], v, RSTDV[:, r:r + 1], VC_HI[:, u % 3, :].bitcast(F32),
                                         ALU.mult, ALU.subtract).then_inc(sem["sp_lo"], 1)

            sp_cut(0)
            sp_cut(1)
            for u in range(2 * NCHUNK):
                if u + 2 < 2 * NCHUNK:
                    sp_cut(u + 2)
                dve.wait_ge(sem["acc_full"], U_SP + u + 1)
                dve.wait_ge(sem["sp_lo"], u + 1)
                for g in range(2, 4):
                    place, half = u // 2, u % 2
                    c0 = half * 1024 + g * 2 * P
                    z = dve.tensor_scalar(V[:, place, c0:c0 + 2 * P],
                                          acc(u % 2)[:, 1, (g % 2) * 2 * P:(g % 2 + 1) * 2 * P],
                                          BS[:, 4 * half + g:4 * half + g + 1], None, ALU.add)
                z.then_inc(sem["sp_zd"], 1)

            dve.wait_ge(sem["sp_z"], 2 * NCHUNK)
            dve.wait_ge(sem["sp_zd"], 2 * NCHUNK)
            with dve.Fori(0, 4) as i:
                for j in range(2):
                    n = Count(T_U + 2 * j, 4, i)
                    cut_lo(dve, n + AHEAD)
                    for chunk in range(NCHUNK):
                        u = Count(8 * j + chunk, 16, i)
                        z = V[:, (chunk + 4) % 8, bass.ds(((n - T_U) * P).v, 2 * P)]
                        dve.wait_ge(sem["u_gelu"], (u + 1).v)
                        dve.tensor_tensor(z, acc(u % 2)[:, 0, 0:2 * P], z, ALU.mult).then_inc(sem["acc_free"], 1)
                        if chunk in (2, 5):
                            mod_reduce(dve, n - T_V + (chunk == 5))
                    cut_lo(dve, n + AHEAD + 1)

            def add_x(u, k, gate):
                dve.wait_ge(sem["acc_full"], (u + 1).v)
                dve.wait_ge(sem["acc_free"], freed(u - 1).v)
                dve.scalar_tensor_tensor(X[:, k, :], flat(acc(u % 2)), MODV[:, gate + k:gate + k + 1], X[:, k, :],
                                         ALU.mult, ALU.add).then_inc(sem["acc_free"], 1)

            pending = []

            def sum_squares_late(s, k):
                pending.append((s, k))
                if len(pending) > 1:
                    sum_squares(*pending.pop(0))

            def uz_cut(q, j):
                u = turn_unit(q, j)
                dve.wait_ge(sem["uz_hi"], 4 * q + j + 1)
                dve.tensor_tensor(UZ_LO[q % 2][:, j, :], flat(acc(u % 2)), UZ_HI[q % 2][:, j, :].bitcast(F32),
                                  ALU.subtract).then_inc(sem["acc_free"], 1)

            for j in range(4):
                uz_cut(0, j)
            dve.wait_ge(sem["x_back"], 16)
            for q in range(4):
                for j in range(4):
                    n = Count(T_G + 4 * q + j)
                    cut_lo(dve, n + AHEAD)
                    mod_reduce(dve, n - T_V)
                    for m in range(2):
                        add_x(Count(gate_unit(q, j) + m), 2 * j + m, G1A)
                        if q == 3:
                            sum_squares_late(1, 2 * j + m)
                    if q < 3:
                        uz_cut(q + 1, j)
            sum_squares(*pending.pop(0))
            mod_vectors(MOD_FIRST + 8, MOD_FIRST + 48, (1, 2), MOD_FIRST + T_M0)
            normalise(1, 1, range(4))

            def up(n, hx, u, e, jm):
                for j in range(4):
                    p = acc((u + j) % 2)
                    cut_lo(dve, n + j + AHEAD)
                    if jm is not None:
                        mod_reduce(dve, jm + j)
                    dve.wait_ge(sem["acc_full"], (u + j + 1).v)
                    dve.tensor_scalar(p, p, 0.0, None, ALU.max).then_inc(sem["relu_done"], 1)
                    dve.wait_ge(sem["hid_hi"], ((hx + j) * 2 + 2).v)
                    dve.tensor_tensor(HID_LO[e][:, j, :], flat(p), HID_HI[e][:, j, :].bitcast(F32), ALU.subtract
                                      ).then_inc(sem["acc_free"], 1)

            def down(n, u, gate, jm, stat):
                for j in range(4):
                    if n.i is not None or n.c + j + AHEAD < TILES:
                        cut_lo(dve, n + j + AHEAD)
                    if jm is not None:
                        mod_reduce(dve, jm + j)
                    for m in range(2):
                        k = 2 * j + m
                        add_x(u + k, k, gate)
                        if stat is not None:
                            sum_squares_late(stat, k)

            def mlp(t0, h0, u0, gate, mods, stat):
                up(Count(t0), Count(h0), Count(u0), 0, None)
                with dve.Fori(0, 3) as i:
                    for a in range(2):
                        jm = Count(mods + 8 * a, 16, i) if mods is not None else None
                        up(Count(t0 + 4 + 8 * a, 16, i), Count(h0 + 4 + 4 * a, 8, i),
                           Count(u0 + 4 + 12 * a, 24, i), (a + 1) % 2, jm)
                        down(Count(t0 + 8 + 8 * a, 16, i), Count(u0 + 8 + 12 * a, 24, i),
                             gate, jm + 4 if jm is not None else None, None)
                up(Count(t0 + 52), Count(h0 + 28), Count(u0 + 76), 1, None)
                down(Count(t0 + 56), Count(u0 + 80), gate, None, None)
                down(Count(t0 + 60), Count(u0 + 88), gate, None, stat)
                if stat is not None:
                    sum_squares(*pending.pop(0))

            mlp(T_M0, 0, U_M0, G2A, 48, 2)
            mod_vectors(MOD_FIRST + 48, MODS, (3, 4), MODS)
            normalise(2, 2, range(4))

            for u in range(4 * NCHUNK):
                pair, chunk = divmod(u, NCHUNK)
                if chunk == 0:
                    cut_lo(dve, Count(T_KV_V + 2 * pair + AHEAD))
                src = acc(u % 2)[:, 0, 0:2 * P].rearrange("p (h d) -> p h d", h=4)
                dve.wait_ge(sem["vs_hi"], u + 1)
                dve.tensor_tensor(VST[:, u % 2, :, HD:2 * HD], src, VST[:, u % 2, :, 0:HD].bitcast(F32),
                                  ALU.subtract).then_inc(sem["acc_free"], 1)
                if chunk == NCHUNK - 1:
                    cut_lo(dve, Count(T_KV_V + 2 * pair + AHEAD + 1))

            def kq_copy(c, u):
                dve.wait_ge(sem["acc_full"], u + 1)
                dve.wait_ge(sem["kq_sq"], c + 1)
                dve.tensor_copy(KRAW[:, c % 2, :], flat(acc(u % 2))).then_inc(sem["acc_free"], 1)

            def kq_reciprocal(c, q, parts):
                dve.wait_ge(sem["kq_sqrt"], c + 1)
                if c and q == 0:
                    dve.wait_ge(sem["kq_lo"], c)
                sl = slice(q * S // parts, (q + 1) * S // parts)
                r = dve.reciprocal(KN[:, sl], flat(STAT)[:, sl])
                if q == parts - 1:
                    r.then_inc(sem["kq_rec"], 1)

            def kq_rest(c, u):
                dve.wait_ge(sem["kq_rec"], c + 1)
                dve.wait_ge(sem["acc_free"], freed(u))
                g = QKG[:, 0:1] if c < KT else QKG[:, 1:2]
                dve.scalar_tensor_tensor(KN[:], KRAW[:, c % 2, :], g, KN[:], ALU.mult, ALU.mult
                                         ).then_inc(sem["kq_norm"], 1)
                dve.wait_ge(sem["kq_hi"], c + 1)
                dve.tensor_tensor(KOUT[:, 1, :], KN[:], KOUT[:, 0, :].bitcast(F32), ALU.subtract
                                  ).then_inc(sem["kq_lo"], 1)

            def kq(c0, t0, u0):
                for j in range(KT):
                    if j:
                        kq_copy(c0 + j - 1, u0 + j - 1)
                    cut_lo(dve, Count(t0 + j + AHEAD))
                    if c0 + j:
                        kq_reciprocal(c0 + j - 1, 0, 1)
                        kq_rest(c0 + j - 1, u0 + j - 1)
                kq_copy(c0 + KT - 1, u0 + KT - 1)

            kq(0, T_K, U_K)
            normalise(3, 2, ())
            kq(KT, T_Q, U_Q)

            def stick(h, par, k):
                n, b = h * KT + k, STRIPS[k]
                w = (KT - b) * P
                last = max(i for i, piece in enumerate(PIECES) if piece[0] == k)
                dve.wait_ge(sem["masked"], (n + 1).v)
                if b < 4:
                    dve.wait_ge(sem["keep_ok"], (h * STEPS + last + 1).v)
                keep = KEEP[:, k % 4, 1:1 + w]
                dve.tensor_tensor_scan(keep, keep, keep, 1.0, ALU.mult, ALU.min).then_inc(sem["scanned"], 1)
                if k in DVE_SHARES:
                    dve.wait_ge(sem["scanned"], (n + 1).v)
                    dve.wait_ge(sem["masked_a"], (n + 1).v)
                    a = A[:, par, STRIP[b]:STRIP[b] + w]
                    dve.tensor_tensor(a, a, KEEP[:, k % 4, 0:w], ALU.mult).then_inc(sem["a_ok_dve"], 1)

            def at_cut(h, s):
                g, j = GROUP[s]
                n = h * STEPS + s
                w = min(j - 4 * g + 1, 4) * P
                dve.wait_ge(sem["at_hi"], (n + 1).v)
                dve.tensor_tensor(AT_LO[:, s % 3, 0:w], PS[:, 3 + s % 3, 0:w], AT_HI[:, s % 3, 0:w].bitcast(F32),
                                  ALU.subtract).then_inc(sem["at_lo"], 1)

            def o_add(h, par, g):
                n = h * 2 + (1 - g)
                r = slice(HD * par, HD * par + HD)
                dve.wait_ge(sem["o_bot"], (n + 1).v)
                dve.tensor_tensor(OSUM[r, :], PS[0:HD, 6 + g, :], OSUM[0:HD, :], ALU.add).then_inc(sem["o_sum"], 1)

            def o_cut(h, par, g, pair):
                n = h * 2 + (1 - g)
                r = slice(HD * par, HD * par + HD)
                dve.wait_ge(sem["o_hi"], (n + 1).v)
                o = (r, bass.ds(pair.v, 1), slice(g * HALF, (g + 1) * HALF))
                dve.tensor_tensor(OT_LO[o], OSUM[r, :].unsqueeze(1), OT_HI[o].bitcast(F32), ALU.subtract
                                  ).then_inc(sem["o_lo"], 1)

            def both(h1, p1, h2, p2, pair2, pair0):
                for s in range(STEPS):
                    if s < STEPS - 2 and h2 is not None:
                        at_cut(h2, s + 2)
                    elif s >= STEPS - 2 and h1 is not None:
                        at_cut(h1, s + 2 - STEPS)
                    if pair0 is not None and s == 1:
                        o_add(h2 - 1, 1 - p2, 0)
                    if pair0 is not None and s == 2:
                        o_cut(h2 - 1, 1 - p2, 0, pair0)
                    if h2 is not None and s == 5:
                        o_add(h2, p2, 1)
                    if h2 is not None and s == 6:
                        o_cut(h2, p2, 1, pair2)
                    if s == 0 and h2 is not None:
                        stick(h2, p2, KT - 1)
                    if s and h1 is not None and PIECES[s][1] == 0:
                        stick(h1, p1, PIECES[s][0] - 1)
                    if h2 is None and s in (2, 4, 6, 7):
                        kq_reciprocal(2 * KT - 1, (2, 4, 6, 7).index(s), 4)
                    if h2 is None and s == 9:
                        kq_rest(2 * KT - 1, U_Q + KT - 1)

            both(Count(0), 0, None, 0, None, None)
            both(Count(1), 1, Count(0), 0, Count(0), None)
            with dve.Fori(0, 7) as i:
                both(Count(2, 2, i), 0, Count(1, 2, i), 1, Count(0, 1, i), Count(0, 1, i))
                both(Count(3, 2, i), 1, Count(2, 2, i), 0, Count(1, 1, i), Count(0, 1, i))
            both(None, 0, Count(HEADS - 1), 1, Count(KT - 1), Count(KT - 1))
            o_add(Count(HEADS - 1), 1, 0)
            o_cut(Count(HEADS - 1), 1, 0, Count(KT - 1))

            dve.wait_ge(sem["x_back"], 32)
            for j in range(8):
                cut_lo(dve, Count(T_O + j + AHEAD))
                if j == 4:
                    dve.wait_ge(sem["x_back_hi"], 16)
                add_x(Count(U_O + j), j, G1B)
                sum_squares_late(3, j)
            sum_squares(*pending.pop(0))
            normalise(4, 3, range(4))
            mlp(T_M1, 32, U_M1, G2B, None, None)

        @block.tensor
        def _(pe):
            def three(dst, w_hi, w_lo, m_hi, m_lo, first, last):
                pe.matmul(dst, w_hi, m_hi, start=first, stop=False)
                pe.matmul(dst, w_hi, m_lo, start=False, stop=False)
                return pe.matmul(dst, w_lo, m_hi, start=False, stop=last)

            def ones_sum(s):
                pe.wait_ge(sem["s_added"], 8 * s + 7)
                total = SUMSQ3 if s == 3 else SUMSQ
                for n in range(2):
                    pe.matmul(STAT[:, n, :], ONES[:], total[:, n * HALF:(n + 1) * HALF], start=True, stop=True
                              ).then_inc(sem["stat_full"], 1)

            def wide_unit(n, u, m_hi, m_lo, piece=None, between=None):
                s, slot = n % RING, u % 2
                pe.wait_ge(sem["w_lo"], (n + 1).v)
                pe.wait_ge(sem["acc_free"], freed(u - 2).v)
                for half in range(2):
                    sl = slice(half * HALF, (half + 1) * HALF)
                    for k in range(8):
                        if piece is not None:
                            pe.wait_ge(sem["h_lo"], piece + 8 * half + k + 1)
                        mm = three(PS[:, 2 * slot + half, :], W_HI[:, k, s * P:(s + 1) * P],
                                   W_LO[:, k, s * P:(s + 1) * P], m_hi[:, k, sl], m_lo[:, k, sl], k == 0, k == 7)
                    if half == 0 and between is not None:
                        between()
                mm.then_inc(sem["acc_full"], 1)

            def first_units(n, u, piece):
                for half in range(2):
                    sl = slice(half * HALF, (half + 1) * HALF)
                    for t in range(2):
                        s, slot = (n + t) % RING, (u + t) % 2
                        if half == 0:
                            pe.wait_ge(sem["w_lo"], (n + t + 1).v)
                            pe.wait_ge(sem["acc_free"], freed(u + t - 2).v)
                        for k in range(8):
                            if t == 0:
                                pe.wait_ge(sem["h_lo"], piece + 8 * half + k + 1)
                            mm = three(PS[:, 2 * slot + half, :], W_HI[:, k, s * P:(s + 1) * P],
                                       W_LO[:, k, s * P:(s + 1) * P], H_HI[:, k, sl], H_LO[:, k, sl], k == 0, k == 7)
                        if half == 1:
                            mm.then_inc(sem["acc_full"], 1)

            def narrow_units(n, u, m_hi, m_lo, ready=None):
                s = n % RING
                pe.wait_ge(sem["w_lo"], (n + 1).v)
                for m in range(2):
                    slot = (u + m) % 2
                    pe.wait_ge(sem["acc_free"], freed(u + m - 2).v)
                    for half in range(2):
                        sl = slice(half * HALF, (half + 1) * HALF)
                        for k in range(4):
                            if ready is not None and m == 0 and half == 0:
                                ready(k)
                            mm = three(PS[:, 2 * slot + half, :], W_HI[:, 2 * k + m, s * P:(s + 1) * P],
                                       W_LO[:, 2 * k + m, s * P:(s + 1) * P], m_hi[:, k, sl], m_lo[:, k, sl],
                                       k == 0, k == 3)
                    mm.then_inc(sem["acc_full"], 1)

            def token_unit(n, chunk, slot, piece=None):
                s, sl, dst = n % RING, slice(chunk * CHUNK, (chunk + 1) * CHUNK), PS[:, 2 * slot, 0:2 * P]
                for k in range(8):
                    if piece is not None:
                        pe.wait_ge(sem["h_lo"], piece + 8 * (chunk // 4) + k + 1)
                    hi, lo = W_HI[:, k, s * P:(s + 2) * P], W_LO[:, k, s * P:(s + 2) * P]
                    pe.matmul(dst, H_HI[:, k, sl], hi, start=(k == 0), stop=False)
                    pe.matmul(dst, H_LO[:, k, sl], hi, start=False, stop=False)
                    mm = pe.matmul(dst, H_HI[:, k, sl], lo, start=False, stop=(k == 7))
                mm.then_inc(sem["acc_full"], 1)

            pe.wait_ge(sem["consts"], 1)
            def sum_tile(k):
                pe.wait_ge(sem["sq_done"], k + 1)
                for n in range(2):
                    mm = pe.matmul(STAT[:, n, :], ONES[:], SQ[:, k % 2, n * HALF:(n + 1) * HALF],
                                   start=(k == 0), stop=(k == KT - 1))
                    if k == KT - 1:
                        mm.then_inc(sem["stat_full"], 1)
                if k < KT - 1:
                    mm.then_inc(sem["s_added"], 1)

            for m in range(MOD_FIRST):
                if m in MOD_PE:
                    pe.wait_ge(sem["small_in"], 80)
                    pe.wait_ge(sem[f"m0_in{m // 2}"], 16)
                    for k in range(KT):
                        mm = pe.matmul(PS[:, 6, m:m + 1], MOD0[:, m, k, :], CC[:, k:k + 1], start=(k == 0),
                                       stop=(k == KT - 1))
                    mm.then_inc(sem["mod_mm"], 1)
                else:
                    mod_mm(pe, Count(m - MOD_FIRST))
                for k in {1: (0, 1), 2: (2,), 3: (3, 4, 5), 4: (6,), 5: (7,)}.get(m, ()):
                    sum_tile(k)

            with pe.Fori(0, 4) as i:
                for j in range(2):
                    n = Count(T_V + 2 * j, 4, i)
                    pe.wait_ge(sem["w_lo"], (n + 2).v)
                    for chunk in range(NCHUNK):
                        u = Count(8 * j + chunk, 16, i)
                        pe.wait_ge(sem["v_gelu"], (u + 1).v)
                        token_unit(n, chunk, u % 2, 0 if j == 0 and chunk in (0, 4) else None)
                    mod_mm(pe, n - T_V)
                    mod_mm(pe, n - T_V + 1)

            for u in range(2 * NCHUNK):
                half = u % 2
                pe.wait_ge(sem["sp_lo"], u + 1)
                if u < 2:
                    pe.wait_ge(sem["v_gelu"], U_SP + 2)
                    pe.wait_ge(sem["ws_lo"], 1)
                else:
                    pe.wait_ge(sem["sp_z"], u - 1)
                    pe.wait_ge(sem["sp_zd"], u - 1)
                for g in range(4):
                    sl = slice(g * 2 * P, (g + 1) * 2 * P)
                    dst = PS[:, 2 * (u % 2) + g // 2, (g % 2) * 2 * P:(g % 2 + 1) * 2 * P]
                    mm = three(dst, WS_HI[:, 4 * half + g, :], WS_LO[:, 4 * half + g, :], VC_HI[:, u % 3, sl],
                               VC_LO[:, u % 3, sl], True, True)
                mm.then_inc(sem["acc_full"], 1)

            pe.wait_ge(sem["sp_z"], 2 * NCHUNK)
            pe.wait_ge(sem["sp_zd"], 2 * NCHUNK)
            with pe.Fori(0, 4) as i:
                for j in range(2):
                    n = Count(T_U + 2 * j, 4, i)
                    pe.wait_ge(sem["w_lo"], (n + 2).v)
                    for chunk in range(NCHUNK):
                        u = Count(U_U + 8 * j + chunk, 16, i)
                        pe.wait_ge(sem["acc_free"], freed(u - 2).v)
                        token_unit(n, chunk, u % 2)
                    mod_mm(pe, n - T_V)
                    mod_mm(pe, n - T_V + 1)

            def uz_turn(q, j):
                u = turn_unit(q, j)
                pe.wait_ge(sem["acc_free"], freed(u - 2))
                for chunk in range(NCHUNK):
                    c = (4 * q + j) * P
                    mm = pe.transpose(PS[:, 2 * (u % 2) + chunk // 4, (chunk % 4) * P:(chunk % 4 + 1) * P],
                                      V[:, (chunk + 4) % 8, c:c + P], IDENT[:])
                mm.then_inc(sem["acc_full"], 1)

            pe.wait_ge(sem["acc_free"], freed(U_G - 1))
            pe.wait_ge(sem["ident_ok"], 2)
            for j in range(4):
                uz_turn(0, j)
            for q in range(4):
                for j in range(4):
                    n = Count(T_G + 4 * q + j)
                    narrow_units(n, Count(gate_unit(q, j)), UZ_HI[q % 2], UZ_LO[q % 2],
                                 (lambda k: pe.wait_ge(sem["acc_free"], freed(turn_unit(q, k)))) if j == 0 else None)
                    if q < 3:
                        uz_turn(q + 1, j)
                    mod_mm(pe, n - T_V)
            ones_sum(1)

            def up(n, u, jm, piece=None):
                if piece is not None:
                    first_units(n, u, piece)
                for j in range(2 if piece is not None else 0, 4):
                    wide_unit(n + j, u + j, H_HI, H_LO)
                    if jm is not None:
                        mod_mm(pe, jm + j)

            def down(n, u, e, hid_unit, jm):
                for j in range(4):
                    if j == 0:
                        ready = lambda k: pe.wait_ge(sem["acc_free"], freed(hid_unit + k).v)
                    narrow_units(n + j, u + 2 * j, HID_HI[e], HID_LO[e], ready if j == 0 else None)
                    if jm is not None:
                        mod_mm(pe, jm + j)

            def mlp(t0, u0, mods, piece):
                up(Count(t0), Count(u0), None, piece)
                with pe.Fori(0, 3) as i:
                    for a in range(2):
                        jm = Count(mods + 8 * a, 16, i) if mods is not None else None
                        up(Count(t0 + 4 + 8 * a, 16, i), Count(u0 + 4 + 12 * a, 24, i), jm)
                        before = Count(u0, 24, i) if a == 0 else Count(u0 + 4, 24, i)
                        down(Count(t0 + 8 + 8 * a, 16, i), Count(u0 + 8 + 12 * a, 24, i), a,
                             before, jm + 4 if jm is not None else None)
                up(Count(t0 + 52), Count(u0 + 76), None)
                down(Count(t0 + 56), Count(u0 + 80), 0, Count(u0 + 64), None)
                down(Count(t0 + 60), Count(u0 + 88), 1, Count(u0 + 76), None)

            mlp(T_M0, U_M0, 48, 16)
            ones_sum(2)

            with pe.Fori(0, 2) as i:
                for j in range(2):
                    n = Count(T_KV_V + 2 * j, 4, i)
                    pe.wait_ge(sem["w_lo"], (n + 2).v)
                    for chunk in range(NCHUNK):
                        u = Count(U_KV_V + 8 * j + chunk, 16, i)
                        pe.wait_ge(sem["acc_free"], freed(u - 2).v)
                        token_unit(n, chunk, u % 2, 32 if j == 0 and chunk in (0, 4) else None)

            def head_sums(c):
                pe.wait_ge(sem["kq_sq"], c + 1)
                pe.wait_ge(sem["consts"], 5)
                if c:
                    pe.wait_ge(sem["kq_rec"], c)
                for n in range(2):
                    pe.matmul(STAT[:, n, :], BLK[:], KSQ[:, n * HALF:(n + 1) * HALF], start=True, stop=True
                              ).then_inc(sem["kq_full"], 1)

            def kq(c0, t0, u0, piece):
                for j in range(KT):
                    wide_unit(Count(t0 + j), Count(u0 + j), H_HI, H_LO, piece if j == 0 else None,
                              (lambda: head_sums(c0 + j - 1)) if j else None)
                head_sums(c0 + KT - 1)

            kq(0, T_K, U_K, None)
            kq(KT, T_Q, U_Q, 48)

            def scores(h, par, s, first):
                k, part, w = PIECES[s]
                n, b = h * STEPS + s, STRIPS[k]
                r = slice(HD * par, HD * par + HD)
                if s == 0:
                    pe.wait_ge(sem[f"qk_in{par}"], ((h // 2) * 16 + 16).v)
                if not (first and par == 0 and s < 3):
                    pe.wait_ge(sem["keep_ok"], (n - 2).v)
                q = QK[r, 0:2, b * P:(b + 1) * P]
                c = b * P + part * HALF
                keys = QK[r, 2:4, c:c + w]
                three(PS[:, s % 3, 0:w], q[:, 0, :], q[:, 1, :], keys[:, 0, :], keys[:, 1, :], True, True
                      ).then_inc(sem["z_full"], 1)

            def turn(h, par, s, first):
                g, j = GROUP[s]
                n = h * STEPS + s
                if j == KT - 1:
                    made = [shared(h, 3)] if g else [shared(h, 6), shared(h, 7)]
                    for name, count in made:
                        pe.wait_ge(sem[name], count.v)
                if not (first and s < 3):
                    pe.wait_ge(sem["at_lo"], (n - 2).v)
                elif s == 1:
                    pe.wait_ge(sem["kq_rec"], 2 * KT)
                for b in range(min(j - 4 * g + 1, 4)):
                    t = 4 * g + b
                    c = STRIP[t] + (j - t) * P
                    mm = pe.transpose(PS[:, 3 + s % 3, b * P:(b + 1) * P], A[:, par, c:c + P], IDENT[:])
                mm.then_inc(sem["at_full"], 1)

            def weigh(h, par, s, first):
                g, j = GROUP[s]
                n = h * STEPS + s
                w = min(j - 4 * g + 1, 4) * P
                if s == 0:
                    pe.wait_ge(sem[f"v_in{par}"], ((h // 2) * 16 + 16).v)
                if j == KT - 1 and not first:
                    pe.wait_ge(sem["o_sum"], (h * 2 - g).v)
                pe.wait_ge(sem["at_lo"], (n + 1).v)
                dst = PS[:, 6 + g, 0:w]
                pe.matmul(dst, VH[:, par, j, :], AT_HI[:, s % 3, 0:w], start=(j == KT - 1), stop=False)
                pe.matmul(dst, VH[:, par, j, :], AT_LO[:, s % 3, 0:w], start=False, stop=(j == 4 * g)
                          ).then_inc(sem["av_done"], 1)

            def both(h1, p1, h2, p2, first1, first2):
                for s in range(STEPS):
                    if s < STEPS - 2 and h2 is not None:
                        turn(h2, p2, s + 2, first2)
                    elif s >= STEPS - 2 and h1 is not None:
                        turn(h1, p1, s + 2 - STEPS, h2 is None)
                    if h1 is not None:
                        scores(h1, p1, s, first1)
                    if h2 is not None:
                        weigh(h2, p2, s, first2)

            pe.wait_ge(sem["acc_free"], freed(U_O - 1))
            pe.wait_ge(sem["ident_ok"], 3)
            both(Count(0), 0, None, 0, True, False)
            both(Count(1), 1, Count(0), 0, False, True)
            with pe.Fori(0, 7) as i:
                both(Count(2, 2, i), 0, Count(1, 2, i), 1, False, False)
                both(Count(3, 2, i), 1, Count(2, 2, i), 0, False, False)
            both(None, 0, Count(HEADS - 1), 1, False, False)

            pe.wait_ge(sem["o_lo"], 2 * HEADS)
            for j in range(KT):
                wide_unit(Count(T_O + j), Count(U_O + j), OT_HI, OT_LO)
            ones_sum(3)
            mlp(T_M1, U_M1, None, 64)


def tiles_of(w, rows):
    cols = 1024 // rows
    k, n = w.shape
    a = w.reshape(k // (rows * P), rows, P, n // cols, cols)
    return a.transpose(0, 3, 2, 1, 4).reshape(-1, P, 1024)


def column(v):
    return np.ascontiguousarray(v.reshape(-1, P).T)


def mlp_tiles(up, down):
    u = tiles_of(up, 8).reshape(8, 4, P, 1024)
    d = tiles_of(down, 4).reshape(8, 4, P, 1024)
    parts = [u[0]]
    for e in range(7):
        parts += [u[e + 1], d[e]]
    return parts + [d[7]]


def kernel(x, c, mod_w, mod_b, norm_g, mlp_w_up, mlp_w_down, a_w_in, a_v_norm_g, a_w_spatial, a_b_spatial,
           a_w_out, kv_mod_w, kv_mod_b, kv_norm_g, kv_w, k_norm_g, b_w_q, q_norm_g, b_w_out):
    import concourse.bacc as bacc
    from concourse.bass_utils import run_bass_kernel_spmd

    args = [np.asarray(a) for a in (x, c, mod_w, mod_b, norm_g, mlp_w_up, mlp_w_down, a_w_in, a_v_norm_g,
                                    a_w_spatial, a_b_spatial, a_w_out, kv_mod_w, kv_mod_b, kv_norm_g, kv_w,
                                    k_norm_g, b_w_q, q_norm_g, b_w_out)]
    (x, c, mod_w, mod_b, norm_g, mlp_w_up, mlp_w_down, a_w_in, a_v_norm_g, a_w_spatial, a_b_spatial,
     a_w_out, kv_mod_w, kv_mod_b, kv_norm_g, kv_w, k_norm_g, b_w_q, q_norm_g, b_w_out) = args

    stream = [tiles_of(a_w_in[0][:, W:2 * W], 8), tiles_of(a_w_in[0][:, 0:W], 8), tiles_of(a_w_out[0], 4)]
    stream += mlp_tiles(mlp_w_up[0], mlp_w_down[0])
    stream += [tiles_of(kv_w[:, D:2 * D], 8), tiles_of(kv_w[:, 0:D], 8), tiles_of(b_w_q[0], 8),
               tiles_of(b_w_out[0], 8)]
    stream += mlp_tiles(mlp_w_up[1], mlp_w_down[1])

    arrays = {
        "xT": np.ascontiguousarray(x[0, ::-1].T.reshape(KT, P, S).transpose(1, 0, 2)),
        "cT": column(c[0]),
        "wt": np.concatenate(stream),
        "modw": np.concatenate([tiles_of(m, 8) for m in (mod_w[0], kv_mod_w, mod_w[1])]).reshape(MODS, P, 8, P),
        "modb": column(np.concatenate([mod_b[0], kv_mod_b, mod_b[1]])),
        "ng": column(np.concatenate([norm_g[0, 0], norm_g[0, 1], kv_norm_g, norm_g[1, 0], norm_g[1, 1]])),
        "vg": np.ascontiguousarray(np.broadcast_to(a_v_norm_g[0], (P, W))),
        "qkg": np.ascontiguousarray(np.stack([np.concatenate([k_norm_g] * 2), np.concatenate([q_norm_g[0]] * 2)], 1)),
        "spw": np.ascontiguousarray(a_w_spatial[0][:, ::-1, ::-1].transpose(2, 0, 1)),
        "spb": np.ascontiguousarray(a_b_spatial[0][:, ::-1].T),
    }
    nc = bacc.Bacc("TRN2", target_bir_lowering=False, num_devices=1)
    aps = [nc.dram_tensor(f"in_{n}", a.shape, mybir.dt.from_np(a.dtype), kind="ExternalInput").ap()
           for n, a in arrays.items()]
    out = nc.dram_tensor("out_x", (P, KT, S), F32, kind="ExternalOutput").ap()
    build(nc, *aps, out)
    r = run_bass_kernel_spmd(nc, [{f"in_{n}": a for n, a in arrays.items()}], core_ids=[0])
    y = r.results[0]["out_x"]
    return np.ascontiguousarray(y.transpose(1, 0, 2).reshape(D, S).T[::-1])[None]
```
